# Optimizing a Trainium2 kernel written in Bass

```python
import math
import jax
import jax.numpy as jnp
from jax import lax
import numpy as np

D_MODEL = 1024
BATCH = 1
SEQ = 256
DEPTH = 2

HEAD_DIM = 64
A_HEADS = 6
A_KV_HEADS = 2
A_GROUP = A_HEADS // A_KV_HEADS
A_WIDTH = A_HEADS * HEAD_DIM
CMP_BLOCK = 32
CMP_STRIDE = 16
SEL_BLOCK = 64
N_SELECT = 16
WINDOW = 512
NSA_Q_BLOCK = 64
FORCE = 1e4
B_HEADS = 4
B_WIDTH = B_HEADS * HEAD_DIM
CONV_K = 4
MLSTM_CHUNK = 64
C_HEADS = 6
C_NOPE = 64
C_ROPE = 32
C_V = 64
C_WIDTH = C_HEADS * C_V
Q_RANK = 192
KV_RANK = 128
ROPE_THETA = 10000.0
ATTN_Q_BLOCK = 128
D_MIX = A_WIDTH + B_WIDTH + C_WIDTH
REL_BUCKETS = 32
REL_MAX_DIST = 128
N_GROUPS = 4
EXPERTS_PER_GROUP = 8
N_EXPERTS = N_GROUPS * EXPERTS_PER_GROUP
TOP_K_INNER = 2
D_EXPERT = 256
EPS = 1e-6
NEG = -1e30
IN_SPLITS = (A_WIDTH, 3 * 2 * A_KV_HEADS * HEAD_DIM, 3 * A_HEADS,
             2 * B_WIDTH, B_WIDTH, 2 * B_HEADS, B_WIDTH,
             Q_RANK, KV_RANK, C_ROPE)
D_IN = 384 + 768 + 18 + 512 + 256 + 8 + 256 + 192 + 128 + 32

kernel_name = 'hybrid_nsa_mlstm_mla_hmoe'

def split_points():
    pts, acc = [], 0
    for w in IN_SPLITS[:-1]:
        acc += w
        pts.append(acc)
    return pts

def rms_norm(x, g):
    xf = x.astype(jnp.float32)
    y = xf * lax.rsqrt(jnp.mean(xf * xf, axis=-1, keepdims=True) + EPS)
    return (y * g.astype(jnp.float32)).astype(x.dtype)

def masked_softmax(logits, mask):
    p = jax.nn.softmax(jnp.where(mask, logits, NEG), axis=-1)
    return jnp.where(mask, p, 0.0)

def t5_bucket(dist):
    n = jnp.maximum(dist, 0)
    exact = REL_BUCKETS // 2
    nf = jnp.maximum(n, 1).astype(jnp.float32)
    large = exact + (jnp.log(nf / exact) / math.log(REL_MAX_DIST / exact)
                     * (REL_BUCKETS - exact)).astype(jnp.int32)
    large = jnp.minimum(large, REL_BUCKETS - 1)
    return jnp.where(n < exact, n, large)

def rope(x, positions):
    half = x.shape[-1] // 2
    inv = 1.0 / (ROPE_THETA ** (jnp.arange(half, dtype=jnp.float32) * 2.0 / x.shape[-1]))
    ang = positions.astype(jnp.float32)[:, :, None, None] * inv
    cos, sin = jnp.cos(ang).astype(x.dtype), jnp.sin(ang).astype(x.dtype)
    x1, x2 = x[..., :half], x[..., half:]
    return jnp.concatenate([x1 * cos - x2 * sin, x2 * cos + x1 * sin], axis=-1)

def causal_dwconv(x, w):
    T = x.shape[1]
    xp = jnp.pad(x, ((0, 0), (CONV_K - 1, 0), (0, 0)))
    y = xp[:, 0:T] * w[0]
    for j in range(1, CONV_K):
        y = y + xp[:, j:j + T] * w[j]
    return y

def nsa_mixer(q, kv, gates, rel_bias, cmp_pe, cmp_w1, cmp_w2, q_norm_g, k_norm_g):
    bsz, T, _ = q.shape
    dt = q.dtype
    f32 = jnp.float32
    scale = HEAD_DIM ** -0.5
    n_cmp = (T - CMP_BLOCK) // CMP_STRIDE + 1
    n_sel = T // SEL_BLOCK
    k_top = min(N_SELECT, n_sel)
    qh = rms_norm(q.reshape(bsz, T, A_HEADS, HEAD_DIM), q_norm_g)
    qh = qh.reshape(bsz, T, A_KV_HEADS, A_GROUP, HEAD_DIM).transpose(0, 2, 3, 1, 4)
    kv = kv.reshape(bsz, T, 3, 2, A_KV_HEADS, HEAD_DIM)

    def to_heads(t):
        return t.transpose(0, 2, 1, 3)

    starts = jnp.arange(n_cmp) * CMP_STRIDE
    cmp_end = starts + (CMP_BLOCK - 1)
    tok = starts[:, None] + jnp.arange(CMP_BLOCK)[None, :]
    blk = kv[:, :, 0][:, tok]
    blk = blk + cmp_pe.transpose(1, 0, 2)[:, :, None, :]
    hid = jax.nn.silu(jnp.einsum('bnlshd,sldf->bnshf', blk, cmp_w1))
    comp = jnp.einsum('bnshf,sfd->bnshd', hid, cmp_w2)
    k_cmp = rms_norm(comp[:, :, 0], k_norm_g).transpose(0, 2, 1, 3)
    v_cmp = comp[:, :, 1].transpose(0, 2, 1, 3)
    k_slc = to_heads(rms_norm(kv[:, :, 1, 0], k_norm_g)).reshape(bsz, A_KV_HEADS, n_sel, SEL_BLOCK, HEAD_DIM)
    v_slc = to_heads(kv[:, :, 1, 1]).reshape(bsz, A_KV_HEADS, n_sel, SEL_BLOCK, HEAD_DIM)
    sel_id = jnp.arange(n_sel)
    overlap = ((starts[:, None] < (sel_id[None, :] + 1) * SEL_BLOCK)
               & (starts[:, None] + CMP_BLOCK > sel_id[None, :] * SEL_BLOCK)).astype(f32)
    pad = ((0, 0), (0, 0), (WINDOW, 0), (0, 0))
    k_win = jnp.pad(to_heads(rms_norm(kv[:, :, 2, 0], k_norm_g)), pad)
    v_win = jnp.pad(to_heads(kv[:, :, 2, 1]), pad)
    g = jax.nn.sigmoid(gates.astype(f32)).reshape(bsz, T, A_KV_HEADS, A_GROUP, 3).transpose(0, 2, 3, 1, 4)
    bias_tbl = rel_bias.astype(f32).reshape(REL_BUCKETS, A_KV_HEADS, A_GROUP)
    b_idx = jnp.arange(bsz)[:, None, None, None]
    h_idx = jnp.arange(A_KV_HEADS)[None, :, None, None]

    def head_bias(dist):
        return bias_tbl[t5_bucket(dist)].transpose(2, 3, 0, 1)

    def block(i):
        t0 = i * NSA_Q_BLOCK
        tq = t0 + jnp.arange(NSA_Q_BLOCK)
        qb = lax.dynamic_slice_in_dim(qh, t0, NSA_Q_BLOCK, axis=3)
        gb = lax.dynamic_slice_in_dim(g, t0, NSA_Q_BLOCK, axis=3).astype(dt)
        dist_c = tq[:, None] - cmp_end[None, :]
        lc = jnp.einsum('bhgqd,bhnd->bhgqn', qb, k_cmp).astype(f32) * scale + head_bias(dist_c)
        pc = masked_softmax(lc, dist_c >= 0)
        o_c = jnp.einsum('bhgqn,bhnd->bhgqd', pc.astype(dt), v_cmp)
        ps = jnp.einsum('bhgqn,ns->bhqs', pc, overlap)
        cur = tq[:, None] // SEL_BLOCK
        forced = (sel_id[None, :] == 0) | (sel_id[None, :] == cur) | (sel_id[None, :] == cur - 1)
        ps = jnp.where(forced, ps + FORCE, ps)
        ps = jnp.where(sel_id[None, :] <= cur, ps, -1.0)
        top_s, top_i = lax.top_k(ps, k_top)
        n_tok = k_top * SEL_BLOCK
        ks = k_slc[b_idx, h_idx, top_i].reshape(bsz, A_KV_HEADS, NSA_Q_BLOCK, n_tok, HEAD_DIM)
        vs = v_slc[b_idx, h_idx, top_i].reshape(bsz, A_KV_HEADS, NSA_Q_BLOCK, n_tok, HEAD_DIM)
        pos_s = (top_i[..., None] * SEL_BLOCK + jnp.arange(SEL_BLOCK)).reshape(bsz, A_KV_HEADS, NSA_Q_BLOCK, n_tok)
        dist_s = tq[:, None] - pos_s
        mask_s = (dist_s >= 0) & jnp.repeat(top_s >= 0, SEL_BLOCK, axis=-1)
        bias_s = bias_tbl[t5_bucket(dist_s), h_idx].transpose(0, 1, 4, 2, 3)
        ls = jnp.einsum('bhgqd,bhqnd->bhgqn', qb, ks).astype(f32) * scale + bias_s
        p_s = masked_softmax(ls, mask_s[:, :, None])
        o_s = jnp.einsum('bhgqn,bhqnd->bhgqd', p_s.astype(dt), vs)
        kw = lax.dynamic_slice_in_dim(k_win, t0, WINDOW + NSA_Q_BLOCK, axis=2)
        vw = lax.dynamic_slice_in_dim(v_win, t0, WINDOW + NSA_Q_BLOCK, axis=2)
        pos_w = t0 - WINDOW + jnp.arange(WINDOW + NSA_Q_BLOCK)
        dist_w = tq[:, None] - pos_w[None, :]
        mask_w = (dist_w >= 0) & (dist_w < WINDOW) & (pos_w[None, :] >= 0)
        lw = jnp.einsum('bhgqd,bhkd->bhgqk', qb, kw).astype(f32) * scale + head_bias(dist_w)
        p_w = masked_softmax(lw, mask_w)
        o_w = jnp.einsum('bhgqk,bhkd->bhgqd', p_w.astype(dt), vw)
        return gb[..., 0:1] * o_c + gb[..., 1:2] * o_s + gb[..., 2:3] * o_w

    out = lax.map(block, jnp.arange(T // NSA_Q_BLOCK))
    return out.transpose(1, 0, 4, 2, 3, 5).reshape(bsz, T, A_WIDTH)

def mlstm_chunkwise(q, k, v, i_pre, f_pre):
    bsz, H, T, dh = q.shape
    L = MLSTM_CHUNK
    nc = T // L
    log_f = jax.nn.log_sigmoid(f_pre)

    def chunks(t):
        return jnp.moveaxis(t.reshape(bsz, H, nc, L, *t.shape[3:]), 2, 0)

    tri = jnp.tril(jnp.ones((L, L), dtype=bool))

    def step(carry, inp):
        C, n, m = carry
        qc, kc, vc, ic, lfc = inp
        b = jnp.cumsum(lfc, axis=-1)
        D = jnp.where(tri, b[..., :, None] - b[..., None, :] + ic[..., None, :], -jnp.inf)
        m_inter = b + m[..., None]
        m_j = jnp.maximum(m_inter, D.max(-1))
        inter_scale = jnp.exp(m_inter - m_j)
        s = jnp.einsum('bhjd,bhsd->bhjs', qc, kc) * jnp.exp(D - m_j[..., None])
        num = jnp.einsum('bhjs,bhsd->bhjd', s, vc) + inter_scale[..., None] * jnp.einsum('bhed,bhjd->bhje', C, qc)
        den = s.sum(-1) + inter_scale * jnp.einsum('bhd,bhjd->bhj', n, qc)
        h = num / jnp.maximum(jnp.abs(den), jnp.exp(-m_j))[..., None]
        bL = b[..., -1]
        w_log = bL[..., None] - b + ic
        m_new = jnp.maximum(bL + m, w_log.max(-1))
        w = jnp.exp(w_log - m_new[..., None])
        decay = jnp.exp(bL + m - m_new)
        C_new = decay[..., None, None] * C + jnp.einsum('bhs,bhse,bhsd->bhed', w, vc, kc)
        n_new = decay[..., None] * n + jnp.einsum('bhs,bhsd->bhd', w, kc)
        return (C_new, n_new, m_new), h

    init = (jnp.zeros((bsz, H, dh, dh), jnp.float32), jnp.zeros((bsz, H, dh), jnp.float32),
            jnp.zeros((bsz, H), jnp.float32))
    _, hs = lax.scan(step, init, (chunks(q), chunks(k), chunks(v), chunks(i_pre), chunks(log_f)))
    return jnp.moveaxis(hs, 0, 2).reshape(bsz, H, T, dh)

def mlstm_mixer(qk, v, if_pre, o_pre, conv_w, i_bias, f_bias, out_norm_g):
    bsz, T, _ = qk.shape
    dt = qk.dtype
    f32 = jnp.float32
    qk = jax.nn.silu(causal_dwconv(qk, conv_w))

    def heads(t):
        return t.reshape(bsz, T, B_HEADS, HEAD_DIM).transpose(0, 2, 1, 3).astype(f32)

    q = heads(qk[..., :B_WIDTH])
    k = heads(qk[..., B_WIDTH:]) * (HEAD_DIM ** -0.5)
    vh = heads(v)
    i_pre = (if_pre[..., :B_HEADS].astype(f32) + i_bias.astype(f32)).transpose(0, 2, 1)
    f_pre = (if_pre[..., B_HEADS:].astype(f32) + f_bias.astype(f32)).transpose(0, 2, 1)
    h = mlstm_chunkwise(q, k, vh, i_pre, f_pre).transpose(0, 2, 1, 3)
    h = rms_norm(h, out_norm_g.reshape(B_HEADS, HEAD_DIM)).reshape(bsz, T, B_WIDTH)
    return (jax.nn.sigmoid(o_pre.astype(f32)) * h).astype(dt)

def mla_mixer(dq, dkv, kr, positions, q_a_norm, w_uq, kv_a_norm, w_ukv, qk_norm):
    bsz, T, _ = dq.shape
    dt = dq.dtype
    f32 = jnp.float32
    q = (rms_norm(dq, q_a_norm) @ w_uq).reshape(bsz, T, C_HEADS, C_NOPE + C_ROPE)
    kv = (rms_norm(dkv, kv_a_norm) @ w_ukv).reshape(bsz, T, C_HEADS, C_NOPE + C_V)
    q_nope = rms_norm(q[..., :C_NOPE], qk_norm[0, :C_NOPE]).transpose(0, 2, 1, 3)
    q_rope = rope(rms_norm(q[..., C_NOPE:], qk_norm[0, C_NOPE:]), positions).transpose(0, 2, 1, 3)
    k_nope = rms_norm(kv[..., :C_NOPE], qk_norm[1, :C_NOPE]).transpose(0, 2, 1, 3)
    v = kv[..., C_NOPE:].transpose(0, 2, 1, 3)
    k_rope = rope(rms_norm(kr, qk_norm[1, C_NOPE:])[:, :, None, :], positions)[:, :, 0]
    scale = (C_NOPE + C_ROPE) ** -0.5
    k_pos = jnp.arange(T)

    def block(i):
        t0 = i * ATTN_Q_BLOCK
        qn = lax.dynamic_slice_in_dim(q_nope, t0, ATTN_Q_BLOCK, axis=2)
        qr = lax.dynamic_slice_in_dim(q_rope, t0, ATTN_Q_BLOCK, axis=2)
        logits = (jnp.einsum('bhqd,bhkd->bhqk', qn, k_nope)
                  + jnp.einsum('bhqr,bkr->bhqk', qr, k_rope)).astype(f32) * scale
        mask = k_pos[None, :] <= (t0 + jnp.arange(ATTN_Q_BLOCK))[:, None]
        p = masked_softmax(logits, mask)
        return jnp.einsum('bhqk,bhkd->bhqd', p.astype(dt), v)

    out = lax.map(block, jnp.arange(T // ATTN_Q_BLOCK))
    return out.transpose(1, 0, 3, 2, 4).reshape(bsz, T, C_WIDTH)

def hier_moe(x, w_group, b_group, w_expert, b_expert, w_gate, w_up, w_down):
    bsz, T, D = x.shape
    dt = x.dtype
    f32 = jnp.float32
    xt = x.reshape(-1, D)
    gp = jax.nn.softmax((xt @ w_group).astype(f32) + b_group.astype(f32), axis=-1)
    g_top, g_idx = lax.top_k(gp, 1)
    el = ((xt @ w_expert).astype(f32) + b_expert.astype(f32)).reshape(-1, N_GROUPS, EXPERTS_PER_GROUP)
    el_sel = jnp.take_along_axis(el, g_idx[:, :, None], axis=1)[:, 0]
    e_top, e_idx = lax.top_k(jax.nn.softmax(el_sel, axis=-1), TOP_K_INNER)
    e_w = e_top / e_top.sum(-1, keepdims=True) * g_top
    expert_id = g_idx * EXPERTS_PER_GROUP + e_idx
    combine = (jax.nn.one_hot(expert_id, N_EXPERTS, dtype=f32) * e_w[..., None]).sum(1).astype(dt)
    h = jax.nn.silu(jnp.einsum('nd,edf->nef', xt, w_gate)) * jnp.einsum('nd,edf->nef', xt, w_up)
    y = jnp.einsum('nef,ne,efd->nd', h, combine, w_down)
    return y.reshape(bsz, T, D)

def setup_inputs(seed: int = 0) -> dict:
    key = jax.random.key(seed)
    ks = jax.random.split(key, 30)
    f32 = jnp.float32
    L = DEPTH

    def nrm(k, shape, scale):
        return jax.random.normal(k, shape, f32) * scale

    def gain(k, shape):
        return 1.0 + 0.1 * jax.random.normal(k, shape, f32)

    return {
        'x': nrm(ks[0], (BATCH, SEQ, D_MODEL), 1.0),
        'positions': (jax.random.randint(ks[1], (BATCH, 1), 0, 4096) + jnp.arange(SEQ)[None, :]).astype(jnp.int32),
        'rel_bias': nrm(ks[2], (REL_BUCKETS, A_HEADS), 0.5),
        'norm1_g': gain(ks[3], (L, D_MODEL)),
        'w_in': nrm(ks[4], (L, D_MODEL, D_IN), D_MODEL ** -0.5),
        'nsa_cmp_pe': nrm(ks[5], (L, 2, CMP_BLOCK, HEAD_DIM), 0.1),
        'nsa_cmp_w1': nrm(ks[6], (L, 2, CMP_BLOCK, HEAD_DIM, HEAD_DIM), (CMP_BLOCK * HEAD_DIM) ** -0.5),
        'nsa_cmp_w2': nrm(ks[7], (L, 2, HEAD_DIM, HEAD_DIM), HEAD_DIM ** -0.5),
        'nsa_q_norm': gain(ks[8], (L, HEAD_DIM)),
        'nsa_k_norm': gain(ks[9], (L, HEAD_DIM)),
        'nsa_out_norm': gain(ks[10], (L, A_WIDTH)),
        'mlstm_conv': nrm(ks[11], (L, CONV_K, 2 * B_WIDTH), 0.5),
        'mlstm_i_bias': nrm(ks[12], (L, B_HEADS), 0.1),
        'mlstm_f_bias': jnp.linspace(3.0, 6.0, B_HEADS, dtype=f32)[None, :] + nrm(ks[13], (L, B_HEADS), 0.1),
        'mlstm_out_norm': gain(ks[14], (L, B_WIDTH)),
        'mla_q_a_norm': gain(ks[15], (L, Q_RANK)),
        'mla_w_uq': nrm(ks[16], (L, Q_RANK, C_HEADS * (C_NOPE + C_ROPE)), Q_RANK ** -0.5),
        'mla_kv_a_norm': gain(ks[17], (L, KV_RANK)),
        'mla_w_ukv': nrm(ks[18], (L, KV_RANK, C_HEADS * (C_NOPE + C_V)), KV_RANK ** -0.5),
        'mla_qk_norm': gain(ks[19], (L, 2, C_NOPE + C_ROPE)),
        'mla_out_norm': gain(ks[20], (L, C_WIDTH)),
        'w_out': nrm(ks[21], (L, D_MIX, D_MODEL), D_MIX ** -0.5),
        'norm2_g': gain(ks[22], (L, D_MODEL)),
        'moe_w_group': nrm(ks[23], (L, D_MODEL, N_GROUPS), D_MODEL ** -0.5),
        'moe_b_group': nrm(ks[24], (L, N_GROUPS), 0.01),
        'moe_w_expert': nrm(ks[25], (L, D_MODEL, N_EXPERTS), D_MODEL ** -0.5),
        'moe_b_expert': nrm(ks[26], (L, N_EXPERTS), 0.01),
        'moe_w_gate': nrm(ks[27], (L, N_EXPERTS, D_MODEL, D_EXPERT), D_MODEL ** -0.5),
        'moe_w_up': nrm(ks[28], (L, N_EXPERTS, D_MODEL, D_EXPERT), D_MODEL ** -0.5),
        'moe_w_down': nrm(ks[29], (L, N_EXPERTS, D_EXPERT, D_MODEL), D_EXPERT ** -0.5),
    }

def reference(x, positions, rel_bias, norm1_g, w_in, nsa_cmp_pe, nsa_cmp_w1, nsa_cmp_w2, nsa_q_norm,
              nsa_k_norm, nsa_out_norm, mlstm_conv, mlstm_i_bias, mlstm_f_bias, mlstm_out_norm,
              mla_q_a_norm, mla_w_uq, mla_kv_a_norm, mla_w_ukv, mla_qk_norm, mla_out_norm, w_out,
              norm2_g, moe_w_group, moe_b_group, moe_w_expert, moe_b_expert, moe_w_gate, moe_w_up,
              moe_w_down):
    points = split_points()
    for l in range(DEPTH):
        h = rms_norm(x, norm1_g[l])
        proj = h @ w_in[l]
        a_q, a_kv, a_gate, b_qk, b_v, b_if, b_o, c_dq, c_dkv, c_kr = jnp.split(proj, points, axis=-1)
        y_a = nsa_mixer(a_q, a_kv, a_gate, rel_bias, nsa_cmp_pe[l], nsa_cmp_w1[l], nsa_cmp_w2[l],
                        nsa_q_norm[l], nsa_k_norm[l])
        y_b = mlstm_mixer(b_qk, b_v, b_if, b_o, mlstm_conv[l], mlstm_i_bias[l], mlstm_f_bias[l],
                          mlstm_out_norm[l])
        y_c = mla_mixer(c_dq, c_dkv, c_kr, positions, mla_q_a_norm[l], mla_w_uq[l], mla_kv_a_norm[l],
                        mla_w_ukv[l], mla_qk_norm[l])
        y = jnp.concatenate([rms_norm(y_a, nsa_out_norm[l]), y_b, rms_norm(y_c, mla_out_norm[l])], axis=-1)
        x = x + y @ w_out[l]
        x = x + hier_moe(rms_norm(x, norm2_g[l]), moe_w_group[l], moe_b_group[l], moe_w_expert[l],
                         moe_b_expert[l], moe_w_gate[l], moe_w_up[l], moe_w_down[l])
    return x


_drawn_inputs = setup_inputs


def setup_inputs(seed=0):
    import zlib

    import numpy as np

    out = dict(_drawn_inputs(seed))
    spreads = {}
    factors = {'mlstm_i_bias': 64.0, 'moe_b_group': 8.0, 'moe_b_expert': 5.959}
    for name, (base, spread) in spreads.items():
        noise = np.random.default_rng([zlib.crc32(name.encode()), seed]).standard_normal(out[name].shape)
        drawn = base * np.exp(spread * noise) if base else spread * noise
        out[name] = jnp.asarray(drawn.astype(out[name].dtype))
    for name, factor in factors.items():
        out[name] = (out[name] * factor).astype(out[name].dtype)
    return out
```

```python
from contextlib import ExitStack

import concourse.bass as bass
from concourse import mybir

ALU = mybir.AluOpType
ACT = mybir.ActivationFunctionType
AX = mybir.AxisListType
F32 = mybir.dt.float32
I32 = mybir.dt.int32
U32 = mybir.dt.uint32

P = 128
D = 1024
KM = D // P
SEQ = 256
CH = SEQ // P
DEPTH = 2
HD = 64
AH, AKV = 6, 2
AG = AH // AKV
AW = AH * HD
BH = 4
BW = BH * HD
CHD = 6
NOPE, ROPE = 64, 32
QK = NOPE + ROPE
QR, KVR = 192, 128
QRC = QR // 2
CMP_L, CMP_S = 32, 16
NCMP = (SEQ - CMP_L) // CMP_S + 1
CONV_K = 4
NG, EPG = 4, 8
NE = NG * EPG
FE = 256
NSLOT = 2 * SEQ
WIN = 64
NEX = NE - 1
NJOB = 8
EPS = 1e-6
NEG = -1e30
LOWEST = -3.0e38
BIASW = 384

C_KV, C_GATE, C_BQK, C_BV = AW, 1152, 1170, 1682
O_BV = C_BV - 512
O_IF, O_O, O_DQ = O_BV + BW, O_BV + BW + 8, O_BV + 2 * BW + 8
O_DKV, O_KR, PROJ = O_DQ + QR, O_DQ + QR + KVR, O_DQ + QR + KVR + ROPE
W_IN_ITEMS = [(0, 512), (512, 1170), (1170, 1682), (1682, 2194), (2194, 2554)]
SLOT = KM * 768
NSLOTS = 3
E0 = len(W_IN_ITEMS) + 2
ITEM_DMAS = [1, 1, 3, 1, 1, 1, 1] + [2] * NEX
JOB_SLOT = (E0 + NEX) % NSLOTS
JOB = NEX % 3

C128 = [("ident", 128), ("before", 128), ("causal", 256), ("after", 256), ("iota", 512),
        ("inv_freq", 16), ("row_ok", 1), ("head_block", 6)]
C128_AT = {}
_at = 0
for _n, _w in C128:
    C128_AT[_n] = (_at, _w)
    _at += _w
C128_W = _at

BANK_USES = (
    [(f"xT{i}", i) for i in range(4)]
    + [("T0c0", 4), ("T0c1", 5), ("T1ac0", 6), ("T1ac1", 7), ("T1b", 0), ("F01", 1), ("F23", 2),
       ("T3c0", 3), ("T3c1", 4), ("T4c0", 5), ("T4c1", 6), ("params", 7)]
    + [("qT0", 0), ("qT1", 1), ("qT2", 2), ("kT0", 3), ("kT1", 4), ("cmp0", 5), ("cmp1", 6), ("hid", 7),
       ("comp", 0), ("kcT", 1), ("clog", 2), ("cPT", 3), ("cO0", 4), ("cO1", 5)]
    + [("ifT", 6), ("umT", 7), ("mB0", 0), ("mB1", 1), ("SS0", 2), ("SS1", 3), ("SS2", 4), ("SS3", 5),
       ("num0", 6), ("num1", 7)]
    + [("dqT", 0), ("dkvT", 1), ("uq00", 2), ("uq01", 3), ("uq10", 4), ("uq11", 5), ("ukv00", 6), ("ukv01", 7),
       ("ukv10", 0), ("ukv11", 1)]
    + [("mq0", 2), ("mq1", 3), ("mq2", 4), ("mk0", 5), ("mk1", 6), ("mk2", 7)]
)
N_GROUPS_ATT = 9


def group_uses():
    uses = []
    for s in range(N_GROUPS_ATT + 2):
        if s < N_GROUPS_ATT:
            uses += [(f"LA{s}", 2 * (s % 2)), (f"LB{s}", 2 * (s % 2) + 1)]
        if 1 <= s <= N_GROUPS_ATT:
            uses += [(f"PA{s - 1}", 4), (f"PB{s - 1}", 5)]
        if s >= 2:
            uses += [(f"O{s - 2}", 6 + s % 2)]
    return uses


BANK_USES += group_uses()
BANK_USES += [(f"yT{i}", i) for i in range(4)] + [("wo00", 4), ("wo10", 5), ("wo01", 6), ("wo11", 7)]
BANK_USES += [(f"nT{i}", i) for i in range(4)] + [("rout", 4), ("rank", 5)]
BANK_USES += [(f"xs{m}", (6 + m) % 8) for m in range(8)] + [("cw0", 6), ("cw1", 7)]
BANK_USES += [(f"ys{i}", i) for i in range(8)] + [("fo00", 0), ("fo01", 1), ("fo10", 2), ("fo11", 3)]
PER_BANK = [sum(b == k for _, b in BANK_USES) for k in range(8)]
USE = {}
for _n, _b in BANK_USES:
    assert _n not in USE
    USE[_n] = (_b, 1 + sum(1 for x, b in BANK_USES[:[u[0] for u in BANK_USES].index(_n)] if b == _b))


def landed_at(item):
    s = item % NSLOTS
    return s, 16 * sum(ITEM_DMAS[j] for j in range(s, item + 1, NSLOTS))


DOWN_PER_LAYER = [16 * len(range((s - E0) % NSLOTS, NEX, NSLOTS)) for s in range(NSLOTS)]
LANDED_PER_LAYER = [16 * sum(ITEM_DMAS[s::NSLOTS]) for s in range(NSLOTS)]


def trunk(nc, t, out):
    x_in, positions, rel_bias = t["x"], t["positions"], t["rel_bias"]
    ctx = ExitStack()
    with ctx:
        def sb(name, shape, dt=F32):
            return ctx.enter_context(nc.sbuf_tensor(name, shape, dt))

        waits_passed = ctx.enter_context(nc.semaphore("waits_passed"))

        def settle(eng):
            eng.sem_inc(waits_passed, 1)

        class Signal:
            def __init__(self, name, per, credit=0):
                self.sem = ctx.enter_context(nc.semaphore(name))
                self.per, self.credit = per, credit

            def at(self, lay, k):
                return lay * self.per + (k + self.credit)

        x = sb("x", [P, CH, D])
        ring = sb("ring", [P, NSLOTS, SLOT])
        cst = sb("cst", [P, C128_W])
        ident = cst[:, 0:128]

        def const(name):
            a, w = C128_AT[name]
            return cst[:, a:a + w]

        ones = sb("ones", [P, P])
        bias_t = sb("bias_t", [P, AH, BIASW])
        sel4 = sb("sel4", [4, 4 * P])
        cosn = sb("cosn", [P, CH, 16])
        sinn = sb("sinn", [P, CH, 16])
        rot = sb("rot", [P, 2, 4, CH, 16])
        w_uq = sb("w_uq", [QRC, 2, CHD * QK])
        w_ukv = sb("w_ukv", [P, CHD * P])
        w_cmp2 = sb("w_cmp2", [HD, 2, HD])
        rows = sb("rows", [48, P])
        cols = sb("cols", [P, 48])
        g1 = sb("g1", [P, KM])
        g2 = sb("g2", [P, KM])
        gy = sb("gy", [P, KM])
        gq = sb("gq", [HD, 1])
        gqs = sb("gqs", [HD, 1])
        gk = sb("gk", [HD, 1])
        if_bias = sb("if_bias", [4, 2])
        g_qa = sb("g_qa", [QRC, 2])
        g_kva = sb("g_kva", [P, 1])
        g_mq = sb("g_mq", [QK, 1])
        g_mqs = sb("g_mqs", [QK, 1])
        g_mk = sb("g_mk", [QK, 1])
        g_rope = sb("g_rope", [P, 2, ROPE])
        w_rout = sb("w_rout", [P, KM, NG + NE])
        b_rout = sb("b_rout", [P, NG + NE])
        eps_col = sb("eps_col", [P, 1])
        st = sb("st", [P, 256])

        ARENA = 23480
        arena = sb("arena", [P, ARENA + 1032])
        at = [0]

        def carve(*shape, parts=P, start=None):
            n = 1
            for s in shape:
                n *= s
            a = at[0] if start is None else start
            if start is None:
                at[0] = a + n
            v = arena[0:parts, a:a + n]
            if len(shape) == 1:
                return v
            names = "abcde"[:len(shape)]
            kw = {names[i]: shape[i] for i in range(len(shape))}
            return v.rearrange(f"p ({' '.join(names)}) -> p {' '.join(names)}", **kw)

        xn = carve(CH, KM, P)
        y = carve(CH, D, start=0)
        xT_at = at[0]
        xT = carve(KM, SEQ)
        moe_at = at[0]
        LP = [carve(768, start=xT_at), carve(768, start=xT_at + 768)]
        proj = carve(CH, PROJ)
        qT = carve(AH, SEQ, parts=HD)
        kT = carve(2, AKV, SEQ, parts=HD)
        sq_at = at[0]
        sq = carve(1536)
        nd = carve(2 * BH, HD + 1, start=sq_at)
        hB = carve(CH, BW, start=sq_at + 2 * BH * (HD + 1) + 8)
        kc = carve(CH, CHD, QK)
        rows_at = at[0]
        qc = carve(CH, CHD, QK)
        vC = carve(CH, CHD, HD)
        conv_in = carve(4, CONV_K - 1 + SEQ)
        mq_at = at[0]
        qk = carve(4, SEQ)
        E2 = carve(BH, P)
        mk_at = at[0]
        E1 = carve(BH, SEQ)
        ebuf = carve(4, SEQ, start=mk_at)
        v_aug = carve(CH, BH, HD + 1)
        mqT = carve(CHD, SEQ, parts=QK, start=mq_at)
        mkT = carve(CHD, SEQ, parts=QK, start=mk_at)
        assert at[0] - mk_at >= CHD * SEQ
        pt_at = at[0]
        cmp_x = carve(2, 3, SEQ)
        PT = [carve(6, P, start=pt_at), carve(6, P, start=pt_at + 768)]
        eo = carve(CH, BW)
        gates = carve(CH, 3 * AH)
        hid_e = carve(2, 30, parts=HD)
        hid_b = carve(2, 30, parts=HD)
        hid_k = carve(30, parts=HD)
        hid_v = carve(90, parts=HD)
        ck = carve(HD, parts=30)
        kcT = carve(30, parts=HD)
        vblk = carve(AH, HD, parts=90)
        clog = carve(CH, AH, NCMP)
        cPT = carve(SEQ, parts=90)
        rowi, rowf, rowa, rowB, rowu, rowm, rownm = [carve(SEQ, parts=4, start=rows_at + SEQ * i) for i in range(7)]
        rowe = rownm
        tmpr = carve(4, CH * CHD * 16)
        arena_att = at[0]
        at[0] = moe_at
        xs = carve(KM, NSLOT + WIN)
        ysT = carve(KM, NSLOT + WIN)
        ys = carve(4, D, start=moe_at)
        S = carve(CH, NSLOT)
        tmpS = carve(NSLOT)
        Cw = carve(CH, NSLOT)
        tmpC = carve(NSLOT)
        cwT = carve(4, SEQ)
        xw = [carve(KM, WIN) for _ in range(3)]
        sg = carve(FE // 2)
        h = carve(FE // 2)
        hT = carve(2, WIN)
        rl = carve(CH, NG + NE)
        pg = carve(CH, 8)
        m8 = carve(CH, 8)
        m8e = carve(CH, 8)
        elp = carve(CH, NE)
        els = carve(CH, 8)
        oh = carve(2, CH, NE)
        ind = carve(CH, NE)
        base = carve(CH, NE)
        cnt = carve(NE)
        offs = carve(NE)
        junk = carve(NE)
        jx = carve(NE)
        jlast = carve(NE)
        jfirst = carve(NE)
        jM = carve(NJOB, NE)
        jt = carve(NJOB, NE)
        jobs = carve(2 * NJOB + 2)
        assert max(at[0], arena_att) <= ARENA, (at[0], arena_att)
        table_in = arena[0:33, ARENA:ARENA + AH]
        buckets = arena[0:33, ARENA + 8:ARENA + 520]
        bias_out = arena[0:AH, ARENA + 520:ARENA + 1032]
        i8g = sb("i8g", [P, CH, 8], U32)
        i8e = sb("i8e", [P, CH, 8], U32)
        offs_i = sb("offs_i", [1, NE], I32)
        jobs_i = sb("jobs_i", [1, 2 * NJOB + 2], I32)
        jobs_before = sb("jobs_before", [1, 1])
        pos_i = sb("pos_i", [P, CH], I32)

        PS = ctx.enter_context(nc.psum_tensor("PS", [P, 8, 512], F32))
        bias_rows = nc.dram_tensor("bias_rows", [AH, P, 513], F32, kind="Internal").ap()

        filled = [Signal(f"bank{b}_filled", PER_BANK[b]) for b in range(8)]
        evacuated = [Signal(f"bank{b}_evacuated", PER_BANK[b], credit=1) for b in range(8)]
        landed = [ctx.enter_context(nc.semaphore(f"slot{s}_landed")) for s in range(NSLOTS)]
        down_landed = [ctx.enter_context(nc.semaphore(f"slot{s}_down_landed")) for s in range(NSLOTS)]
        n_att_dmas, n_moe_dmas = 19, 5
        att_params = ctx.enter_context(nc.semaphore("att_params"))
        moe_params = ctx.enter_context(nc.semaphore("moe_params"))
        x_loaded = ctx.enter_context(nc.semaphore("x_loaded"))
        table_dma = ctx.enter_context(nc.semaphore("table_dma"))
        setup_dma = ctx.enter_context(nc.semaphore("setup_dma"))
        bias_dma = ctx.enter_context(nc.semaphore("bias_dma"))
        setup_mem = ctx.enter_context(nc.semaphore("setup_mem"))
        pe_setup = ctx.enter_context(nc.semaphore("pe_setup"))
        vec_setup = ctx.enter_context(nc.semaphore("vec_setup"))
        angles_ready = ctx.enter_context(nc.semaphore("angles_ready"))
        act_setup = ctx.enter_context(nc.semaphore("act_setup"))
        vec_step = ctx.enter_context(nc.semaphore("vec_step"))
        act_step = ctx.enter_context(nc.semaphore("act_step"))
        pool_step = ctx.enter_context(nc.semaphore("pool_step"))
        out_dma = ctx.enter_context(nc.semaphore("out_dma"))
        x_new = Signal("x_new", 1, credit=1)
        sums1 = Signal("sums1", 1)
        sums2 = Signal("sums2", 1)
        sumsy = Signal("sumsy", 1)
        sumsc = Signal("sumsc", 1)
        head_sums = Signal("head_sums", 5)
        head_roots = Signal("head_roots", 5)
        xn_ready = Signal("xn_ready", 4)
        gains = Signal("gains", 1)
        q_normed = Signal("q_normed", 1)
        k_normed = Signal("k_normed", 1)
        cmp_zero = Signal("cmp_zero", 1)
        gate_e = Signal("gate_e", 1)
        hid_pre = Signal("hid_pre", 1)
        hid_exp = Signal("hid_exp", 1)
        hid_ready = Signal("hid_ready", 1)
        ck_ready = Signal("ck_ready", 1)
        vblk_ready = Signal("vblk_ready", 1)
        clog_pre = Signal("clog_pre", 1)
        clog_exp = Signal("clog_exp", 1)
        conv_done = Signal("conv_done", 1)
        conv_exp = Signal("conv_exp", 1)
        qk_ready = Signal("qk_ready", 1)
        f_abs = Signal("f_abs", 1)
        f_log = Signal("f_log", 1)
        um_ready = Signal("um_ready", 1)
        um_cols = Signal("um_cols", 1)
        em_ready = Signal("em_ready", 1)
        e_pre = Signal("e_pre", 4)
        e_exp = Signal("e_exp", 8)
        g_ready = Signal("g_ready", 4)
        va_ready = Signal("va_ready", 1)
        eo_ready = Signal("eo_ready", 1)
        c_normed = Signal("c_normed", 1)
        mcat_ready = Signal("mcat_ready", 1)
        p_pre = Signal("p_pre", N_GROUPS_ATT)
        p_exp = Signal("p_exp", N_GROUPS_ATT)
        y_scaled = Signal("y_scaled", 1)
        y_all = Signal("y_all", 1)
        x_mid = Signal("x_mid", 1)
        ge_pre = Signal("ge_pre", 1)
        ge_exp = Signal("ge_exp", 1)
        e2_pre = Signal("e2_pre", 1)
        e2_exp = Signal("e2_exp", 1)
        ind_ready = Signal("ind_ready", 1)
        offs_ready = Signal("offs_ready", 1)
        w_ready = Signal("w_ready", 1)
        S_ready = Signal("S_ready", 1)
        cw_ready = Signal("cw_ready", 1)
        xs_pad = Signal("xs_pad", 1)
        xw_ready = Signal("xw_ready", NEX)
        gu_done = Signal("gu_done", NEX, credit=3)
        sg_ready = Signal("sg_ready", NEX)
        h_ready = Signal("h_ready", NEX, credit=1)
        hT_full = Signal("hT_full", NEX)
        hT_ready = Signal("hT_ready", NEX, credit=1)
        y_full = Signal("y_full", NEX, credit=2)
        y_stored = Signal("y_stored", NEX, credit=3)
        jobs_made = Signal("jobs_made", 1)
        slot_left = Signal("slot_left", 1, credit=1)
        job = {n: Signal(f"job_{n}", 0, credit=c) for n, c in
               (("gu_landed", 0), ("dn_landed", 0), ("xw_ready", 0), ("gu_done", 1), ("sg_ready", 0), ("h_ready", 1),
                ("hT_full", 0), ("hT_ready", 0), ("y_full", 1), ("y_stored", 1))}
        credited = [*evacuated, x_new, gu_done, h_ready, hT_ready, y_full, y_stored, slot_left, job["gu_done"], job["h_ready"],
                    job["y_full"], job["y_stored"]]


        def is_filled(lay, use):
            b, k = USE[use]
            return filled[b].sem, filled[b].at(lay, k)

        def is_evacuated(lay, use):
            b, k = USE[use]
            return evacuated[b].sem, evacuated[b].at(lay, k)

        def is_free(lay, use):
            b, k = USE[use]
            return evacuated[b].sem, evacuated[b].at(lay, k - 1)

        def bank(use):
            return PS[:, USE[use][0], :]

        def has_landed(lay, item, extra=0):
            s, v = landed_at(item)
            return landed[s], lay * LANDED_PER_LAYER[s] + v + extra

        def job_counts(eng):
            return (eng.value_load(jobs_i[0:1, 2 * NJOB:2 * NJOB + 1], min_val=1, max_val=NJOB),
                    eng.value_load(jobs_i[0:1, 2 * NJOB + 1:2 * NJOB + 2], min_val=0, max_val=NJOB * DEPTH))

        def job_entry(eng, column, it, most):
            return eng.value_load(jobs_i[0:1, bass.ds(it + column * NJOB, 1)], min_val=0, max_val=most)

        def wait_job(eng, name, g, unit=1):
            eng.wait_ge(job[name].sem, g * unit + job[name].credit)

        def w_in_view(item):
            a, b = W_IN_ITEMS[item]
            return ring[:, item % NSLOTS, 0:KM * (b - a)].rearrange("p (m n) -> p m n", m=KM)

        w_cmp1 = ring[:, 2, KM * 512:KM * 512 + 2 * 16 * HD].rearrange("p (s j f) -> p s j f", s=2, j=16)

        def w_out_view(half):
            return ring[:, (5 + half) % NSLOTS, 0:KM * 512].rearrange("p (m n) -> p m n", m=KM)

        def w_gu(s):
            return ring[:, s, 0:KM * 2 * FE].rearrange("p (g m f) -> p g m f", g=2, m=KM)

        def w_dn(s):
            return ring[:, s, KM * 2 * FE:SLOT].rearrange("p (f d) -> p f d", f=2)

        SETUP_LOADS = 3
        PHASE_SETUP = 16 * SETUP_LOADS

        def att_load(eng, l):
            def go(dst, src):
                eng.dma_start(dst, src, allow_slow_non_contiguous=True).then_inc(att_params, 16)
            go(g1[:, :], t["norm1_g"].rearrange("l (p m) -> l p m", m=KM)[l])
            go(gq[:, :], t["nsa_q_norm"].unsqueeze(2)[l])
            go(gk[:, :], t["nsa_k_norm"].unsqueeze(2)[l])
            go(rows[0:16, :], t["mlstm_conv"].rearrange("l j (k c) -> l (j k) c", c=P)[l])
            go(rows[16:48, :], t["nsa_cmp_pe"].rearrange("l s (j b) d -> l (s j) (b d)", b=2)[l])
            go(w_cmp2[:, :, :], t["nsa_cmp_w2"].rearrange("l s f d -> l f s d")[l])
            go(if_bias[:, 0:1], t["mlstm_i_bias"].unsqueeze(2)[l])
            go(if_bias[:, 1:2], t["mlstm_f_bias"].unsqueeze(2)[l])
            go(g_qa[:, :], t["mla_q_a_norm"].rearrange("l (k p) -> l p k", k=2)[l])
            go(g_kva[:, :], t["mla_kv_a_norm"].unsqueeze(2)[l])
            qk_norm = t["mla_qk_norm"].unsqueeze(3)
            go(g_mq[0:NOPE, :], qk_norm[l][0, 0:NOPE])
            go(g_mk[0:NOPE, :], qk_norm[l][1, 0:NOPE])
            for s in range(2):
                go(g_rope[:, s, :], t["mla_qk_norm"].unsqueeze(1)[l][:, s, NOPE:QK].broadcast_to([P, ROPE]))
            go(gy[0:48, :], t["nsa_out_norm"].rearrange("l (p m) -> l p m", m=KM)[l])
            go(gy[48:80, :], t["mlstm_out_norm"].rearrange("l (p m) -> l p m", m=KM)[l])
            go(gy[80:128, :], t["mla_out_norm"].rearrange("l (p m) -> l p m", m=KM)[l])
            go(w_uq[:, :, :], t["mla_w_uq"].rearrange("l (k p) n -> l p k n", k=2)[l])
            go(w_ukv[:, :], t["mla_w_ukv"][l])

        def moe_load(eng, l):
            def go(dst, src):
                eng.dma_start(dst, src, allow_slow_non_contiguous=True).then_inc(moe_params, 16)
            go(g2[:, :], t["norm2_g"].rearrange("l (p m) -> l p m", m=KM)[l])
            go(w_rout[:, :, 0:NG], t["moe_w_group"].rearrange("l (p m) n -> l p m n", m=KM)[l])
            go(w_rout[:, :, NG:], t["moe_w_expert"].rearrange("l (p m) n -> l p m n", m=KM)[l])
            go(b_rout[:, 0:NG], t["moe_b_group"].unsqueeze(1)[l].broadcast_to([P, NG]))
            go(b_rout[:, NG:], t["moe_b_expert"].unsqueeze(1)[l].broadcast_to([P, NE]))

        block = ctx.enter_context(nc.Block())

        @block.sync
        def _(sp):
            sp.dma_start(x[:, :, :], x_in.rearrange("b (c p) d -> p (b c) d", c=CH)).then_inc(x_loaded, 16)
            sp.dma_start(table_in[0:32], rel_bias).then_inc(table_dma, 16)
            sp.dma_start(buckets, t["c33"]).then_inc(table_dma, 16)
            sp.dma_start(cst[:, :], t["c128"]).then_inc(setup_dma, 16)
            sp.dma_start(sel4[:, :], t["c4"]).then_inc(setup_dma, 16)
            sp.dma_start(pos_i[:, :], positions.rearrange("b (c p) -> p (b c)", c=CH),
                         allow_slow_non_contiguous=True).then_inc(setup_dma, 16)

            def load_gate_up(q, s, landing):
                for k, name in enumerate(("moe_w_gate", "moe_w_up")):
                    sp.dma_start(w_gu(s)[:, k], t[name].rearrange("l e (p m) f -> (l e) p m f", m=KM)[q])\
                        .then_inc(landing, 16)

            def load_down(q, s, landing):
                sp.dma_start(w_dn(s), t["moe_w_down"].rearrange("l e (m p) d -> (l e) p m d", m=2)[q])\
                    .then_inc(landing, 16)

            def load_expert(lay, e, s, first=False):
                if not first:
                    sp.wait_ge(gu_done.sem, gu_done.at(lay, e - 2))
                load_gate_up(lay * NE + e, s, landed[s])
                if not first:
                    sp.wait_ge(y_full.sem, y_full.at(lay, e - 2))
                load_down(lay * NE + e, s, down_landed[s])

            with sp.Fori(0, DEPTH) as lay:
                used = [(y_full.sem, y_full.at(lay, -1)), (y_full.sem, y_full.at(lay, 0)),
                        (slot_left.sem, slot_left.at(lay, 0)),
                        is_filled(lay, "T0c1"), is_filled(lay, "T1b")]
                for i, (a, b) in enumerate(W_IN_ITEMS):
                    sp.wait_ge(*used[i])
                    src = t["w_in"].rearrange("l (p m) n -> l p m n", m=KM)[lay][:, :, a:b]
                    sp.dma_start(w_in_view(i), src).then_inc(landed[i % NSLOTS], 16)
                    if i == 0:
                        att_load(sp, lay)
                    if i == 2:
                        src = t["nsa_cmp_w1"].rearrange("l s (j b) d f -> l s (b d) j f", b=2)[lay]
                        for k in range(2):
                            sp.dma_start(w_cmp1[:, k], src[k]).then_inc(landed[2], 16)
                moe_load(sp, lay)
                for half in range(2):
                    sp.wait_ge(*is_filled(lay, ["hid", "T3c1"][half]))
                    src = t["w_out"].rearrange("l (p m) n -> l p m n", m=KM)[lay][:, :, 512 * half:512 * half + 512]
                    sp.dma_start(w_out_view(half), src).then_inc(landed[(5 + half) % NSLOTS], 16)
                for e, use in enumerate(["T4c1", "wo10", "wo11"]):
                    sp.wait_ge(*is_filled(lay, use))
                    load_expert(lay, e, (E0 + e) % NSLOTS, first=True)
                with sp.Fori(0, 9) as it:
                    for u in range(3):
                        e = it * 3 + (3 + u)
                        load_expert(lay, e, (E0 + 3 + u) % NSLOTS)
                load_expert(lay, NEX - 1, (E0 + NEX - 1) % NSLOTS)
                sp.wait_ge(jobs_made.sem, jobs_made.at(lay, 1))
                settle(sp)
                sp.wait_ge(y_full.sem, y_full.at(lay, NEX - 2))
                settle(sp)
                n_jobs, before = job_counts(sp)
                with sp.Fori(0, n_jobs) as it:
                    q = lay * NE + job_entry(sp, 1, it, NE - 1)
                    wait_job(sp, "gu_done", before + it)
                    load_gate_up(q, JOB_SLOT, job["gu_landed"].sem)
                    wait_job(sp, "y_full", before + it)
                    load_down(q, JOB_SLOT, job["dn_landed"].sem)
            sp.wait_ge(x_new.sem, x_new.at(DEPTH - 1, 1))
            sp.dma_start(out.rearrange("b (c p) d -> p (b c) d", c=CH), x[:, :, :]).then_inc(out_dma, 16)
            sp.wait_ge(out_dma, 16)

        @block.gpsimd
        def _(pool):
            for s in credited:
                pool.sem_inc(s.sem, s.credit)
            n = [0]

            def link(ins):
                n[0] += 1
                ins.then_inc(pool_step, 1)
                pool.wait_ge(pool_step, n[0])

            for i, (dst, value) in enumerate(((ones[:, :], 1.0), (eps_col[:, :], EPS), (g_mq[NOPE:QK, :], 1.0),
                                              (g_mk[NOPE:QK, :], 1.0), (table_in[32:33], 1.0))):
                pool.memset(dst, value).then_inc(setup_mem, 1)
                pool.wait_ge(setup_mem, i + 1)
            pool.wait_ge(vec_setup, 1)
            pool.dma_start(bias_rows[:, :, 0:512], bias_out.unsqueeze(1).broadcast_to([AH, P, 512])).then_inc(bias_dma, 16)
            pool.wait_ge(bias_dma, 16)
            skew = bass.AP(tensor=bias_rows.tensor, offset=P - 1, ap=[[512, P], [P * 513, AH], [1, BIASW]])
            pool.dma_start(bias_t[:, :, :], skew).then_inc(bias_dma, 16)

            with pool.Fori(0, DEPTH) as lay:
                pool.sem_clear(pool_step)
                n[0] = 0
                pool.wait_ge(xn_ready.sem, xn_ready.at(lay, 2))
                settle(pool)
                link(pool.memset(conv_in[:, :, 0:CONV_K - 1], 0.0))
                link(pool.memset(v_aug[:, :, :, HD:HD + 1], 1.0))
                pool.memset(cmp_x[:, :, 2, :], 0.0).then_inc(cmp_zero.sem, 1)
                pool.wait_ge(xn_ready.sem, xn_ready.at(lay, 4))
                settle(pool)
                link(pool.memset(xs[:, :, NSLOT:], 0.0))
                pool.memset(ysT[:, :, NSLOT:], 0.0).then_inc(xs_pad.sem, 1)
                pool.wait_ge(w_ready.sem, w_ready.at(lay, 1))
                settle(pool)
                for c in range(CH):
                    link(pool.tensor_scalar(tmpC, const("iota"), st[:, 128 + 2 * c:129 + 2 * c],
                                            st[:, 132 + 2 * c:133 + 2 * c], ALU.is_equal, ALU.mult))
                    link(pool.tensor_scalar(Cw[:, c, :], const("iota"), st[:, 129 + 2 * c:130 + 2 * c],
                                            st[:, 133 + 2 * c:134 + 2 * c], ALU.is_equal, ALU.mult))
                    ins = pool.tensor_tensor(Cw[:, c, :], Cw[:, c, :], tmpC, ALU.add)
                    if c == 0:
                        link(ins)
                    else:
                        ins.then_inc(cw_ready.sem, 1)

        @block.tensor
        def _(pe):
            pe.wait_ge(table_dma, 32)
            pe.wait_ge(setup_mem, 5)
            pe.matmul(PS[0:AH, 0, :], table_in, buckets, start=True, stop=True).then_inc(pe_setup, 1)
            pe.wait_ge(setup_dma, PHASE_SETUP)
            pe.wait_ge(vec_setup, 1)

            with pe.Fori(0, DEPTH) as lay:
                def free(use):
                    pe.wait_ge(*is_free(lay, use))

                def fill(ins, use):
                    ins.then_inc(filled[USE[use][0]].sem, 1)

                def turn_tokens(prefix):
                    for i in range(4):
                        use = f"{prefix}{i}"
                        free(use)
                        for k in range(2):
                            for c in range(CH):
                                a = k * SEQ + c * P
                                m = pe.transpose(bank(use)[:, a:a + P], xn[:, c, 2 * i + k, :], ident)
                        fill(m, use)

                pe.wait_ge(xn_ready.sem, xn_ready.at(lay, 2))
                turn_tokens("xT")
                for i in range(4):
                    pe.wait_ge(*is_evacuated(lay, f"xT{i}"))

                def project(use, item, a, b, c, at0=0):
                    w = w_in_view(item)
                    o = W_IN_ITEMS[item][0]
                    for m in range(KM):
                        ins = pe.matmul(bank(use)[:, at0:at0 + b - a], xT[:, m, c * P:(c + 1) * P],
                                        w[:, m, a - o:b - o], start=(m == 0), stop=(m == KM - 1))
                    return ins

                pe.wait_ge(*has_landed(lay, 0))
                for c in range(CH):
                    free(f"T0c{c}")
                    fill(project(f"T0c{c}", 0, 0, 512, c), f"T0c{c}")
                pe.wait_ge(*has_landed(lay, 1))
                for c in range(CH):
                    free(f"T1ac{c}")
                    fill(project(f"T1ac{c}", 1, 512, 1024, c), f"T1ac{c}")
                free("T1b")
                for c in range(CH):
                    m = project("T1b", 1, 1024, C_BQK, c, at0=c * (C_BQK - 1024))
                fill(m, "T1b")
                pe.wait_ge(*has_landed(lay, 2))
                for i, use in enumerate(["F01", "F23"]):
                    free(use)
                    for k in range(2):
                        for m in range(KM):
                            ins = pe.matmul(bank(use)[:, k * SEQ:(k + 1) * SEQ],
                                            w_in_view(2)[:, m, (2 * i + k) * P:(2 * i + k + 1) * P], xT[:, m, :],
                                            start=(m == 0), stop=(m == KM - 1))
                    fill(ins, use)
                pe.wait_ge(*has_landed(lay, 3))
                for c in range(CH):
                    free(f"T3c{c}")
                    fill(project(f"T3c{c}", 3, C_BV, 2194, c), f"T3c{c}")
                pe.wait_ge(*has_landed(lay, 4))
                for c in range(CH):
                    free(f"T4c{c}")
                    fill(project(f"T4c{c}", 4, 2194, 2554, c), f"T4c{c}")
                free("params")
                pe.wait_ge(att_params, (lay + 1) * (16 * n_att_dmas))
                settle(pe)
                fill(pe.transpose(bank("params")[:, 0:48], rows[:, :], ident[0:48, 0:48]), "params")

                pe.wait_ge(q_normed.sem, q_normed.at(lay, 1))
                for i in range(3):
                    free(f"qT{i}")
                    settle(pe)
                    for k in range(2):
                        for c in range(CH):
                            hh = 2 * i + k
                            m = pe.transpose(bank(f"qT{i}")[0:HD, k * SEQ + c * P:k * SEQ + (c + 1) * P],
                                             proj[:, c, hh * HD:(hh + 1) * HD], ident)
                    fill(m, f"qT{i}")
                pe.wait_ge(k_normed.sem, k_normed.at(lay, 1))
                for b in range(2):
                    free(f"kT{b}")
                    settle(pe)
                    for k in range(AKV):
                        for c in range(CH):
                            a = C_KV + (b + 1) * 256 + k * HD
                            m = pe.transpose(bank(f"kT{b}")[0:HD, k * SEQ + c * P:k * SEQ + (c + 1) * P],
                                             proj[:, c, a:a + HD], ident)
                    fill(m, f"kT{b}")
                for s in range(2):
                    free(f"cmp{s}")
                    settle(pe)
                    for k in range(AKV):
                        for c in range(CH):
                            a = C_KV + s * 128 + k * HD
                            m = pe.transpose(bank(f"cmp{s}")[0:HD, k * SEQ + c * P:k * SEQ + (c + 1) * P],
                                             proj[:, c, a:a + HD], ident)
                    fill(m, f"cmp{s}")
                for s in range(2):
                    pe.wait_ge(*is_evacuated(lay, f"cmp{s}"))
                pe.wait_ge(*is_evacuated(lay, "params"))
                free("hid")
                for s in range(2):
                    for j in range(16):
                        rhs = cmp_x[:, s, :, 2 * j:2 * j + CMP_S * (NCMP - 1) + 1:CMP_S]
                        m = pe.matmul(bank("hid")[0:HD, 64 * s:64 * s + 3 * NCMP], w_cmp1[:, s, j, :], rhs,
                                      start=(j == 0), stop=(j == 15))
                fill(m, "hid")
                free("ifT")
                settle(pe)
                for g in range(2):
                    for c in range(CH):
                        m = pe.transpose(bank("ifT")[0:4, g * SEQ + c * P:g * SEQ + (c + 1) * P],
                                         proj[:, c, O_IF + 4 * g:O_IF + 4 * g + 4], ident)
                fill(m, "ifT")

                pe.wait_ge(hid_ready.sem, hid_ready.at(lay, 1))
                free("comp")
                settle(pe)
                pe.matmul(bank("comp")[0:30, 0:HD], hid_k, w_cmp2[:, 0, :], start=True, stop=True)
                fill(pe.matmul(bank("comp")[0:90, HD:2 * HD], hid_v, w_cmp2[:, 1, :], start=True, stop=True), "comp")
                pe.wait_ge(ck_ready.sem, ck_ready.at(lay, 1))
                free("kcT")
                settle(pe)
                fill(pe.transpose(bank("kcT")[0:HD, 0:30], ck, ident[0:30, 0:30]), "kcT")
                for use in ("qT0", "qT1", "qT2", "kcT"):
                    pe.wait_ge(*is_evacuated(lay, use))
                free("clog")
                for c in range(CH):
                    for hh in range(AH):
                        a = (c * AH + hh) * NCMP
                        m = pe.matmul(bank("clog")[:, a:a + NCMP], qT[:, hh, c * P:(c + 1) * P],
                                      kcT[:, (hh // AG) * NCMP:(hh // AG + 1) * NCMP], start=True, stop=True)
                fill(m, "clog")

                pe.wait_ge(clog_exp.sem, clog_exp.at(lay, 1))
                free("cPT")
                for c in range(CH):
                    m = pe.transpose(bank("cPT")[0:90, c * P:(c + 1) * P],
                                     clog[:, c].rearrange("p h n -> p (h n)"), ident)
                fill(m, "cPT")
                pe.wait_ge(*is_evacuated(lay, "cPT"))
                pe.wait_ge(vblk_ready.sem, vblk_ready.at(lay, 1))
                for c in range(CH):
                    free(f"cO{c}")
                    fill(pe.matmul(bank(f"cO{c}")[:, 0:AW], cPT[:, c * P:(c + 1) * P],
                                   vblk.rearrange("p h d -> p (h d)"), start=True, stop=True), f"cO{c}")

                pe.wait_ge(um_ready.sem, um_ready.at(lay, 1))
                free("umT")
                settle(pe)
                for c in range(CH):
                    for k, row in enumerate((rowu, rowm)):
                        m = pe.transpose(bank("umT")[:, (2 * c + k) * 4:(2 * c + k + 1) * 4],
                                         row[:, c * P:(c + 1) * P], ident[0:4, 0:4])
                fill(m, "umT")
                for i in range(2):
                    free(f"mB{i}")
                    for k in range(2):
                        hh = 2 * i + k
                        m = pe.matmul(bank(f"mB{i}")[:, k * SEQ:(k + 1) * SEQ], sel4[:, hh * P:(hh + 1) * P],
                                      rownm, start=True, stop=True)
                    fill(m, f"mB{i}")
                pe.wait_ge(qk_ready.sem, qk_ready.at(lay, 1))
                for i in range(4):
                    j, odd = i // 2, i % 2
                    o = HD * odd
                    n = SEQ - j * P
                    free(f"SS{i}")
                    for k in range(2):
                        m = pe.matmul(bank(f"SS{i}")[:, k * n:(k + 1) * n], qk[o:o + HD, 2 + k, j * P:(j + 1) * P],
                                      qk[o:o + HD, k, j * P:SEQ], start=True, stop=True)
                    fill(m, f"SS{i}")
                pe.wait_ge(g_ready.sem, g_ready.at(lay, 4))
                pe.wait_ge(va_ready.sem, va_ready.at(lay, 1))
                for c in range(CH):
                    free(f"num{c}")
                    for hh in range(BH):
                        o = bank(f"num{c}")[:, hh * (HD + 1):(hh + 1) * (HD + 1)]
                        m = pe.matmul(o, E1[:, hh, c * P:(c + 1) * P], v_aug[:, 0, hh, :], start=True, stop=(c == 0))
                        if c == 1:
                            m = pe.matmul(o, E2[:, hh, :], v_aug[:, 1, hh, :], start=False, stop=True)
                    fill(m, f"num{c}")

                pe.wait_ge(c_normed.sem, c_normed.at(lay, 1))
                free("dqT")
                for k in range(2):
                    for c in range(CH):
                        m = pe.transpose(bank("dqT")[0:QRC, k * SEQ + c * P:k * SEQ + (c + 1) * P],
                                         proj[:, c, O_DQ + k * QRC:O_DQ + (k + 1) * QRC], ident)
                fill(m, "dqT")
                free("dkvT")
                for c in range(CH):
                    m = pe.transpose(bank("dkvT")[:, c * P:(c + 1) * P], proj[:, c, O_DKV:O_DKV + KVR], ident)
                fill(m, "dkvT")
                dqT = xT[0:QRC, 6:8, :]
                dkvT = xT[:, 5, :]
                pe.wait_ge(*is_evacuated(lay, "dqT"))
                for c in range(CH):
                    for k in range(2):
                        use = f"uq{c}{k}"
                        free(use)
                        for r in range(2):
                            m = pe.matmul(bank(use)[:, 0:3 * QK], dqT[:, r, c * P:(c + 1) * P],
                                          w_uq[:, r, k * 3 * QK:(k + 1) * 3 * QK], start=(r == 0), stop=(r == 1))
                        fill(m, use)
                pe.wait_ge(*is_evacuated(lay, "dkvT"))
                for c in range(CH):
                    for k in range(2):
                        use = f"ukv{c}{k}"
                        free(use)
                        fill(pe.matmul(bank(use)[:, 0:3 * P], dkvT[:, c * P:(c + 1) * P],
                                       w_ukv[:, k * 3 * P:(k + 1) * 3 * P], start=True, stop=True), use)
                pe.wait_ge(mcat_ready.sem, mcat_ready.at(lay, 1))
                for name, src in (("mq", qc), ("mk", kc)):
                    for i in range(3):
                        free(f"{name}{i}")
                        for k in range(2):
                            for c in range(CH):
                                m = pe.transpose(bank(f"{name}{i}")[0:QK, k * SEQ + c * P:k * SEQ + (c + 1) * P],
                                                 src[:, c, 2 * i + k, :], ident)
                        fill(m, f"{name}{i}")

                def operands(g, k):
                    hh = 2 * (g % 3) + k
                    if g < 6:
                        b = g // 3
                        return qT[:, hh, :], kT[:, b, hh // AG, :]
                    return mqT[:, hh, :], mkT[:, hh, :]

                def values(g, k, c):
                    hh = 2 * (g % 3) + k
                    if g < 6:
                        a = C_KV + (g // 3 + 1) * 256 + 128 + (hh // AG) * HD
                        return proj[:, c, a:a + HD]
                    return vC[:, c, hh, :]

                def logits(g):
                    if g == 0:
                        for use in ("kT0", "kT1"):
                            pe.wait_ge(*is_evacuated(lay, use))
                    if g == 6:
                        for i in range(3):
                            pe.wait_ge(*is_evacuated(lay, f"mq{i}"))
                            pe.wait_ge(*is_evacuated(lay, f"mk{i}"))
                    for c, use in enumerate((f"LA{g}", f"LB{g}")):
                        free(use)
                        n = (c + 1) * P
                        for k in range(2):
                            q, kk = operands(g, k)
                            m = pe.matmul(bank(use)[:, k * n:(k + 1) * n], q[:, c * P:(c + 1) * P], kk[:, 0:n],
                                          start=True, stop=True)
                        fill(m, use)

                def turn_weights(g):
                    pe.wait_ge(p_exp.sem, p_exp.at(lay, g + 1))
                    free(f"PA{g}")
                    for i in range(4):
                        m = pe.transpose(bank(f"PA{g}")[:, i * P:(i + 1) * P],
                                         LP[g % 2][:, 256 + i * P:256 + (i + 1) * P], ident)
                    fill(m, f"PA{g}")
                    free(f"PB{g}")
                    for i in range(2):
                        m = pe.transpose(bank(f"PB{g}")[:, i * P:(i + 1) * P], LP[g % 2][:, i * P:(i + 1) * P], ident)
                    fill(m, f"PB{g}")

                def weighted(g):
                    pe.wait_ge(*is_evacuated(lay, f"PA{g}"))
                    pe.wait_ge(*is_evacuated(lay, f"PB{g}"))
                    free(f"O{g}")
                    for c in range(CH):
                        for k in range(2):
                            o = bank(f"O{g}")[:, (c * 2 + k) * HD:(c * 2 + k + 1) * HD]
                            for s in range(c + 1):
                                i = 4 + k if c == 0 else 2 * k + s
                                m = pe.matmul(o, PT[g % 2][:, i, :], values(g, k, s), start=(s == 0), stop=(s == c))
                    fill(m, f"O{g}")

                for s in range(N_GROUPS_ATT + 2):
                    if s < N_GROUPS_ATT:
                        logits(s)
                    if 1 <= s <= N_GROUPS_ATT:
                        turn_weights(s - 1)
                    if s >= 2:
                        weighted(s - 2)

                pe.wait_ge(y_scaled.sem, y_scaled.at(lay, 1))
                for i in range(4):
                    free(f"yT{i}")
                    for k in range(2):
                        for c in range(CH):
                            mm = 2 * i + k
                            m = pe.transpose(bank(f"yT{i}")[:, k * SEQ + c * P:k * SEQ + (c + 1) * P],
                                             y[:, c, mm:D:KM], ident)
                    fill(m, f"yT{i}")
                for i in range(4):
                    pe.wait_ge(*is_evacuated(lay, f"yT{i}"))
                for half in range(2):
                    pe.wait_ge(*has_landed(lay, 5 + half))
                    for c in range(CH):
                        use = f"wo{c}{half}"
                        free(use)
                        for m in range(KM):
                            ins = pe.matmul(bank(use), xT[:, m, c * P:(c + 1) * P], w_out_view(half)[:, m, :],
                                            start=(m == 0), stop=(m == KM - 1))
                        fill(ins, use)

                pe.wait_ge(xn_ready.sem, xn_ready.at(lay, 4))
                turn_tokens("nT")
                for i in range(4):
                    pe.wait_ge(*is_evacuated(lay, f"nT{i}"))
                pe.wait_ge(moe_params, (lay + 1) * (16 * n_moe_dmas))
                free("rout")
                for c in range(CH):
                    for m in range(KM):
                        ins = pe.matmul(bank("rout")[:, c * 36:(c + 1) * 36], xT[:, m, c * P:(c + 1) * P],
                                        w_rout[:, m, :], start=(m == 0), stop=(m == KM - 1))
                fill(ins, "rout")
                pe.wait_ge(ind_ready.sem, ind_ready.at(lay, 1))
                free("rank")
                o = bank("rank")
                pe.matmul(o[:, 0:NE], const("before"), ind[:, 0, :], start=True, stop=True)
                pe.matmul(o[:, NE:2 * NE], ones[:, :], ind[:, 0, :], start=True, stop=False)
                pe.matmul(o[:, NE:2 * NE], const("before"), ind[:, 1, :], start=False, stop=True)
                pe.matmul(o[:, 2 * NE:3 * NE], ones[:, :], ind[:, 0, :], start=True, stop=False)
                fill(pe.matmul(o[:, 2 * NE:3 * NE], ones[:, :], ind[:, 1, :], start=False, stop=True), "rank")
                pe.wait_ge(S_ready.sem, S_ready.at(lay, 1))
                for mm in range(KM):
                    free(f"xs{mm}")
                    for c in range(CH):
                        m = pe.matmul(bank(f"xs{mm}"), xn[:, c, mm, :], S[:, c, :], start=(c == 0), stop=(c == 1))
                    fill(m, f"xs{mm}")
                for mm in range(KM):
                    pe.wait_ge(*is_evacuated(lay, f"xs{mm}"))

                def gate_up(u, s, ms):
                    for m in ms:
                        for k in range(2):
                            ins = pe.matmul(PS[k * WIN:(k + 1) * WIN, u % 3, 0:FE], xw[u % 3][:, m, :],
                                            w_gu(s)[:, :, m, k * P:(k + 1) * P], start=(m == 0), stop=(m == KM - 1))
                    return ins

                def turn_h():
                    return pe.transpose(PS[:, 3, 0:P], h, ident)

                def down(u, s):
                    for mm in range(KM):
                        for f in range(2):
                            ins = pe.matmul(PS[:, 4 + u % 3, mm * WIN:(mm + 1) * WIN], w_dn(s)[:, f, mm * P:(mm + 1) * P],
                                            hT[:, f, :], start=(f == 0), stop=(f == 1))
                    return ins

                def start(e, u, extra):
                    pe.wait_ge(xw_ready.sem, xw_ready.at(lay, e + 1))
                    pe.wait_ge(*has_landed(lay, E0 + u, extra))

                def finish_turn(e):
                    pe.wait_ge(h_ready.sem, h_ready.at(lay, e + 1))
                    pe.wait_ge(hT_ready.sem, hT_ready.at(lay, e))
                    turn_h().then_inc(hT_full.sem, 1)

                def finish_down(e, u, turn):
                    s = (E0 + u) % NSLOTS
                    pe.wait_ge(down_landed[s], lay * DOWN_PER_LAYER[s] + (turn + 1) * 16)
                    pe.wait_ge(hT_ready.sem, hT_ready.at(lay, e + 1))
                    pe.wait_ge(y_stored.sem, y_stored.at(lay, e - 2))
                    down(u, s).then_inc(y_full.sem, 1)

                start(0, 0, 0)
                gate_up(0, E0 % NSLOTS, range(KM)).then_inc(gu_done.sem, 1)
                with pe.Fori(0, NEX // 3) as it:
                    for u in range(3):
                        e = it * 3 + (1 + u)
                        s = (E0 + 1 + u) % NSLOTS
                        start(e, 1 + u, it * 32)
                        gate_up(1 + u, s, range(KM // 2))
                        finish_turn(it * 3 + u)
                        gate_up(1 + u, s, range(KM // 2, KM)).then_inc(gu_done.sem, 1)
                        finish_down(it * 3 + u, u, it)
                finish_turn(NEX - 1)
                finish_down(NEX - 1, (NEX - 1) % 3, (NEX - 1) // 3)
                pe.wait_ge(jobs_made.sem, jobs_made.at(lay, 1))
                pe.wait_ge(y_stored.sem, y_stored.at(lay, NEX - 2))
                pe.wait_ge(hT_ready.sem, hT_ready.at(lay, NEX))
                settle(pe)
                n_jobs, before = job_counts(pe)
                with pe.Fori(0, n_jobs) as it:
                    g = before + it
                    wait_job(pe, "xw_ready", g + 1)
                    wait_job(pe, "gu_landed", g + 1, 32)
                    gate_up(JOB, JOB_SLOT, range(KM)).then_inc(job["gu_done"].sem, 1)
                    wait_job(pe, "h_ready", g + 1)
                    turn_h().then_inc(job["hT_full"].sem, 1)
                    wait_job(pe, "hT_ready", g + 1)
                    wait_job(pe, "dn_landed", g + 1, 16)
                    wait_job(pe, "y_stored", g)
                    down(JOB, JOB_SLOT).then_inc(job["y_full"].sem, 1)

                pe.wait_ge(cw_ready.sem, cw_ready.at(lay, 1))
                for i in range(2):
                    free(f"cw{i}")
                    for k in range(2):
                        for c in range(CH):
                            s = 2 * i + k
                            m = pe.transpose(bank(f"cw{i}")[:, k * SEQ + c * P:k * SEQ + (c + 1) * P],
                                             Cw[:, c, s * P:(s + 1) * P], ident)
                    fill(m, f"cw{i}")
                pe.wait_ge(y_stored.sem, y_stored.at(lay, NEX))
                wait_job(pe, "y_stored", before + n_jobs)
                pe.sem_inc(slot_left.sem, 1)
                for i in range(8):
                    s, k = i // 2, i % 2
                    free(f"ys{i}")
                    for j in range(4):
                        m = pe.transpose(bank(f"ys{i}")[:, j * P:(j + 1) * P],
                                         ysT[:, 4 * k + j, s * P:(s + 1) * P], ident)
                    fill(m, f"ys{i}")
                for i in range(2):
                    pe.wait_ge(*is_evacuated(lay, f"cw{i}"))
                for i in range(8):
                    pe.wait_ge(*is_evacuated(lay, f"ys{i}"))
                for c in range(CH):
                    for half in range(2):
                        use = f"fo{c}{half}"
                        free(use)
                        for s in range(4):
                            m = pe.matmul(bank(use), cwT[:, s, c * P:(c + 1) * P],
                                          ys[:, s, half * 512:(half + 1) * 512], start=(s == 0), stop=(s == 3))
                        fill(m, use)

        @block.scalar
        def _(act):
            act.wait_ge(setup_dma, PHASE_SETUP)
            act.wait_ge(angles_ready, 1)
            act.wait_ge(setup_mem, 5)
            act.activation(sinn[:, :, :], st[:, 64:96].rearrange("p (c f) -> p c f", c=CH), ACT.Sin).then_inc(act_setup, 1)
            act.activation(cosn[:, :, :], st[:, 96:128].rearrange("p (c f) -> p c f", c=CH), ACT.Sin).then_inc(act_setup, 1)

            with act.Fori(0, DEPTH) as lay:
                def evac(dst, src, use, last=True, **kw):
                    ins = act.activation(dst, src, ACT.Copy, **kw)
                    if last:
                        ins.then_inc(evacuated[USE[use][0]].sem, 1)

                def full(use):
                    act.wait_ge(*is_filled(lay, use))

                def square_sums(dst, src, to):
                    return act.activation(dst, src, ACT.Square, accum_out=to)

                steps = [0]

                def step(ins):
                    steps[0] += 1
                    ins.then_inc(act_step, 1)
                    act.wait_ge(act_step, steps[0])

                def root(v, width, sig=None):
                    step(act.activation(v, v, ACT.Ln, bias=eps_col[0:v.shape[0], :], scale=1.0 / width))
                    ins = act.activation(v, v, ACT.Exp, scale=-0.5)
                    if sig is not None:
                        ins.then_inc(sig.sem, 1)

                act.sem_clear(act_step)
                act.wait_ge(x_loaded, 16)
                act.wait_ge(x_new.sem, x_new.at(lay, 0))
                square_sums(y[:, 0, :], x[:, 0, :], st[:, 0:1])
                step(square_sums(y[:, 1, :], x[:, 1, :], st[:, 1:2]))
                root(st[:, 0:2], D, sums1)
                act.wait_ge(gains.sem, gains.at(lay, 1))
                for i in (0, 1):
                    full(f"xT{i}")
                    for k in range(2):
                        evac(xT[:, 2 * i + k, :], bank(f"xT{i}")[:, k * SEQ:(k + 1) * SEQ], f"xT{i}",
                             last=(k == 1), scale=g1[:, 2 * i + k:2 * i + k + 1])
                full("T0c0")
                evac(proj[:, 0, 0:512], bank("T0c0"), "T0c0")
                full("T1ac0")
                evac(proj[:, 0, 512:1024], bank("T1ac0"), "T1ac0")
                full("T1b")
                evac(proj[:, :, 1024:C_BQK], bank("T1b")[:, 0:292].rearrange("p (c n) -> p c n", c=CH), "T1b")
                act.wait_ge(*is_evacuated(lay, "T1b"))
                act.activation(gates[:, :, :], proj[:, :, C_GATE:C_GATE + 18], ACT.Exp, scale=-1.0).then_inc(gate_e.sem, 1)
                act.wait_ge(head_sums.sem, head_sums.at(lay, 1))
                root(st[:, 48:60], HD, head_roots)
                act.wait_ge(head_sums.sem, head_sums.at(lay, 2))
                root(st[:, 240:248], HD, head_roots)
                full("F01")
                evac(conv_in[:, 0:2, 3:], bank("F01").rearrange("p (k n) -> p k n", k=2), "F01")
                full("T3c0")
                evac(proj[:, 0, O_BV:O_BV + 512], bank("T3c0"), "T3c0")
                act.wait_ge(*is_evacuated(lay, "T3c0"))
                act.wait_ge(*is_evacuated(lay, "T3c1"))
                for c in range(CH):
                    m = act.activation(v_aug[:, c, :, 0:HD], proj[:, c, O_BV:O_BV + BW].rearrange("p (h d) -> p h d", h=BH),
                                       ACT.Copy)
                m.then_inc(va_ready.sem, 1)
                full("T4c0")
                evac(proj[:, 0, 1682:PROJ], bank("T4c0")[:, 0:360], "T4c0")
                act.wait_ge(conv_done.sem, conv_done.at(lay, 1))
                act.activation(ebuf[:, :, :], qk[:, :, :], ACT.Exp, scale=-1.0).then_inc(conv_exp.sem, 1)
                act.wait_ge(*is_evacuated(lay, "T4c0"))
                act.wait_ge(*is_evacuated(lay, "T4c1"))
                act.activation(eo[:, :, :], proj[:, :, O_O:O_O + BW], ACT.Exp, scale=-1.0).then_inc(eo_ready.sem, 1)
                for i, (a, w) in enumerate(((O_DQ, QR), (O_DKV, KVR), (O_KR, ROPE))):
                    for c in range(CH):
                        ins = square_sums(kc[:, c, 0:w // 32, 32 * i:32 * i + 32],
                                          proj[:, c, a:a + w].rearrange("p (a b) -> p a b", b=32),
                                          st[:, 8 + 2 * i + c:9 + 2 * i + c])
                step(ins)
                for i, w in enumerate((QR, KVR, ROPE)):
                    root(st[:, 8 + 2 * i:10 + 2 * i], w, sumsc if i == 2 else None)
                for i in (0, 1):
                    full(f"qT{i}")
                    evac(qT[:, 2 * i:2 * i + 2, :], bank(f"qT{i}")[0:HD, :].rearrange("p (k n) -> p k n", k=2), f"qT{i}",
                         scale=gqs[:, :])
                full("kT0")
                evac(kT[:, 0, :, :], bank("kT0")[0:HD, :].rearrange("p (k n) -> p k n", k=2), "kT0", scale=gk[:, :])
                act.wait_ge(cmp_zero.sem, cmp_zero.at(lay, 1))
                full("cmp0")
                src = bank("cmp0").rearrange("p (k n) -> p k n", k=2)
                evac(cmp_x[0:HD, 0, 0:2, :], src[0:HD], "cmp0", last=False)
                evac(cmp_x[HD:P, 0, 0:2, 0:SEQ - 1], src[0:HD, :, 1:SEQ], "cmp0")
                act.wait_ge(hid_pre.sem, hid_pre.at(lay, 1))
                act.activation(hid_e[:, :, :], hid_b[:, :, :], ACT.Exp, scale=-1.0).then_inc(hid_exp.sem, 1)
                act.wait_ge(f_abs.sem, f_abs.at(lay, 1))
                step(act.activation(rowe, rowa, ACT.Exp, scale=-1.0))
                act.activation(rowa, rowe, ACT.Ln, bias=1.0).then_inc(f_log.sem, 1)
                act.wait_ge(head_sums.sem, head_sums.at(lay, 3))
                root(st[0:30, 4:5], HD, head_roots)
                act.wait_ge(clog_pre.sem, clog_pre.at(lay, 1))
                act.activation(clog[:, :, :, :], clog[:, :, :, :], ACT.Exp).then_inc(clog_exp.sem, 1)
                full("cPT")
                evac(cPT, bank("cPT")[0:90, 0:SEQ], "cPT")
                act.wait_ge(um_cols.sem, um_cols.at(lay, 1))
                um = st[:, 16:32].rearrange("p (c k h) -> p c k h", c=CH, k=2)
                act.activation(st[:, 32:40].rearrange("p (c h) -> p c h", c=CH), um[:, :, 1, :], ACT.Exp, scale=-1.0)\
                    .then_inc(em_ready.sem, 1)
                for j, tile in enumerate((E1, E2)):
                    act.wait_ge(e_pre.sem, e_pre.at(lay, 2 + 2 * j))
                    for hh in range(BH):
                        act.activation(tile[:, hh, :], tile[:, hh, :], ACT.Exp, bias=um[:, j, 0, hh:hh + 1])\
                            .then_inc(e_exp.sem, 1)
                full("dqT")
                for k in range(2):
                    evac(xT[0:QRC, 6 + k, :], bank("dqT")[0:QRC, k * SEQ:(k + 1) * SEQ], "dqT", last=(k == 1),
                         scale=g_qa[:, k:k + 1])
                act.wait_ge(head_sums.sem, head_sums.at(lay, 4))
                root(st[:, 48:56], HD, head_roots)
                for c in range(CH):
                    full(f"uq{c}0")
                    evac(qc[:, c, 0:3, :], bank(f"uq{c}0")[:, 0:3 * QK].rearrange("p (h d) -> p h d", h=3), f"uq{c}0")
                for c in range(CH):
                    full(f"ukv{c}0")
                    src = bank(f"ukv{c}0")[:, 0:3 * P].rearrange("p (h d) -> p h d", h=3)
                    evac(kc[:, c, 0:3, 0:NOPE], src[:, :, 0:NOPE], f"ukv{c}0", last=False)
                    evac(vC[:, c, 0:3, :], src[:, :, NOPE:], f"ukv{c}0")
                act.wait_ge(head_sums.sem, head_sums.at(lay, 5))
                root(st[:, 208:232], NOPE)
                root(st[:, 232:244], ROPE, head_roots)
                for i in range(3):
                    full(f"mq{i}")
                    evac(mqT[:, 2 * i:2 * i + 2, :], bank(f"mq{i}")[0:QK, :].rearrange("p (k n) -> p k n", k=2), f"mq{i}",
                         scale=g_mqs[:, :])
                for g in range(N_GROUPS_ATT + 1):
                    if g < N_GROUPS_ATT:
                        act.wait_ge(p_pre.sem, p_pre.at(lay, g + 1))
                        for i in range(4):
                            c, k = i // 2, i % 2
                            a = k * P if c == 0 else 256 + k * SEQ
                            v = LP[g % 2][:, a:a + (c + 1) * P]
                            m = act.activation(v, v, ACT.Exp, bias=st[:, 160 + 4 * (g % 2) + i:161 + 4 * (g % 2) + i],
                                               accum_out=st[:, 176 + 4 * g + i:177 + 4 * g + i])
                        m.then_inc(p_exp.sem, 1)
                    if g >= 1:
                        full(f"PA{g - 1}")
                        evac(PT[(g - 1) % 2][:, 0:4, :], bank(f"PA{g - 1}").rearrange("p (i n) -> p i n", i=4),
                             f"PA{g - 1}")
                act.wait_ge(y_all.sem, y_all.at(lay, 1))
                for i, (a, w) in enumerate(((0, AW), (AW + BW, AW))):
                    for c in range(CH):
                        ins = square_sums(LP[i][:, w * c:w * c + w], y[:, c, a:a + w], st[:, 40 + 2 * i + c:41 + 2 * i + c])
                step(ins)
                root(st[:, 40:44], AW, sumsy)
                for i in (0, 1):
                    full(f"yT{i}")
                    for k in range(2):
                        evac(xT[:, 2 * i + k, :], bank(f"yT{i}")[:, k * SEQ:(k + 1) * SEQ], f"yT{i}",
                             last=(k == 1), scale=gy[:, 2 * i + k:2 * i + k + 1])
                act.wait_ge(x_mid.sem, x_mid.at(lay, 1))
                for c in range(CH):
                    ins = square_sums(y[:, c, :], x[:, c, :], st[:, c:c + 1])
                step(ins)
                root(st[:, 0:2], D, sums2)
                act.wait_ge(moe_params, (lay + 1) * (16 * n_moe_dmas))
                for i in (0, 1):
                    full(f"nT{i}")
                    for k in range(2):
                        evac(xT[:, 2 * i + k, :], bank(f"nT{i}")[:, k * SEQ:(k + 1) * SEQ], f"nT{i}",
                             last=(k == 1), scale=g2[:, 2 * i + k:2 * i + k + 1])
                act.wait_ge(ge_pre.sem, ge_pre.at(lay, 1))
                act.activation(pg[:, :, 0:NG], pg[:, :, 0:NG], ACT.Exp).then_inc(ge_exp.sem, 1)
                act.wait_ge(e2_pre.sem, e2_pre.at(lay, 1))
                act.activation(st[:, 140:142], st[:, 138:140], ACT.Exp).then_inc(e2_exp.sem, 1)
                for mm in range(0, KM, 2):
                    full(f"xs{mm}")
                    evac(xs[:, mm, 0:NSLOT], bank(f"xs{mm}"), f"xs{mm}", scale=g2[:, mm:mm + 1])
                for mm in range(KM):
                    act.wait_ge(*is_evacuated(lay, f"xs{mm}"))
                act.wait_ge(xs_pad.sem, xs_pad.at(lay, 1))
                act.wait_ge(offs_ready.sem, offs_ready.at(lay, 1))

                def silu(u):
                    return act.activation(sg, PS[:, u % 3, 0:P], ACT.Silu)

                def copy_hT():
                    return act.activation(hT[:, :, :], PS[:, 3, 0:P].rearrange("p (f n) -> p f n", f=2), ACT.Copy)

                def window(e, u):
                    settle(act)
                    o = act.value_load(offs_i[0:1, bass.ds(e, 1)], min_val=0, max_val=NSLOT)
                    act.wait_ge(gu_done.sem, gu_done.at(lay, e - 2))
                    act.activation(xw[u % 3], xs[:, :, bass.ds(o, WIN)], ACT.Copy).then_inc(xw_ready.sem, 1)

                def gate(e, u):
                    act.wait_ge(gu_done.sem, gu_done.at(lay, e + 1))
                    act.wait_ge(h_ready.sem, h_ready.at(lay, e))
                    silu(u).then_inc(sg_ready.sem, 1)
                    act.wait_ge(hT_full.sem, hT_full.at(lay, e + 1))
                    act.wait_ge(y_full.sem, y_full.at(lay, e))
                    copy_hT().then_inc(hT_ready.sem, 1)

                window(0, 0)
                window(1, 1)
                with act.Fori(0, NEX // 3 - 1) as it:
                    for u in range(3):
                        gate(it * 3 + u, u)
                        window(it * 3 + (u + 2), u + 2)
                for e in range(NEX - 4, NEX):
                    gate(e, e)
                    if e + 2 < NEX:
                        window(e + 2, e + 2)
                act.wait_ge(jobs_made.sem, jobs_made.at(lay, 1))
                act.wait_ge(h_ready.sem, h_ready.at(lay, NEX))
                act.wait_ge(y_full.sem, y_full.at(lay, NEX))
                settle(act)
                n_jobs, before = job_counts(act)
                with act.Fori(0, n_jobs) as it:
                    g = before + it
                    o = job_entry(act, 0, it, NSLOT)
                    wait_job(act, "gu_done", g)
                    act.activation(xw[JOB], xs[:, :, bass.ds(o, WIN)], ACT.Copy).then_inc(job["xw_ready"].sem, 1)
                    wait_job(act, "gu_done", g + 1)
                    wait_job(act, "h_ready", g)
                    silu(JOB).then_inc(job["sg_ready"].sem, 1)
                    wait_job(act, "hT_full", g + 1)
                    wait_job(act, "y_full", g)
                    copy_hT().then_inc(job["hT_ready"].sem, 1)

                full("cw0")
                evac(cwT[:, 0:2, :], bank("cw0").rearrange("p (k n) -> p k n", k=2), "cw0")
                for i in range(0, 8, 2):
                    full(f"ys{i}")
                    evac(ys[:, i // 2, 0:512], bank(f"ys{i}"), f"ys{i}")

        @block.vector
        def _(dve):
            n = [0]

            def link(ins):
                n[0] += 1
                ins.then_inc(vec_step, 1)
                dve.wait_ge(vec_step, n[0])

            dve.memset(jobs_before[:, :], 0.0)
            dve.wait_ge(pe_setup, 1)
            dve.tensor_copy(bias_out, PS[0:AH, 0, :]).then_inc(vec_setup, 1)
            TWO_PI = 6.283185307179586
            C1 = 6.28125
            C2 = 0.0019350051879882812
            C3 = TWO_PI - C1 - C2
            MAGIC = 12582912.0
            dve.wait_ge(setup_dma, PHASE_SETUP)
            posf, ang, kk = st[:, 0:2], st[:, 64:96], st[:, 96:128]
            link(dve.tensor_copy(posf, pos_i[:, :]))
            for c in range(CH):
                link(dve.tensor_scalar(ang[:, 16 * c:16 * c + 16], const("inv_freq"), posf[:, c:c + 1], None, ALU.mult))
            link(dve.tensor_scalar(kk, ang, 1.0 / TWO_PI, MAGIC, ALU.mult, ALU.add))
            link(dve.tensor_scalar(kk, kk, MAGIC, None, ALU.subtract))
            for cc in (C1, C2, C3):
                link(dve.scalar_tensor_tensor(ang, kk, -cc, ang, ALU.mult, ALU.add))
            link(dve.tensor_scalar(ang, ang, 3.1415925, -3.1415925, ALU.min, ALU.max))
            link(dve.tensor_scalar(kk, ang, 0.5, None, ALU.mult))
            dve.sem_inc(angles_ready, 1)
            dve.wait_ge(act_setup, 2)
            cosf = cosn[:, :, :].rearrange("p c f -> p (c f)")
            link(dve.tensor_tensor(cosf, cosf, cosf, ALU.mult))
            link(dve.tensor_scalar(cosf, cosf, -2.0, 1.0, ALU.mult, ALU.add))

            def bc(ap, shape):
                return ap.unsqueeze(len(ap.shape)).broadcast_to(shape)

            with dve.Fori(0, DEPTH) as lay:
                dve.sem_clear(vec_step)
                n[0] = 0

                def full(use):
                    dve.wait_ge(*is_filled(lay, use))

                def release(ins, use):
                    ins.then_inc(evacuated[USE[use][0]].sem, 1)

                def normalise_tokens(sig):
                    dve.wait_ge(sig.sem, sig.at(lay, 1))
                    for c in range(CH):
                        dve.tensor_scalar(xn[:, c], x[:, c, :].rearrange("p (q m) -> p m q", m=KM), st[:, c:c + 1], None,
                                          ALU.mult).then_inc(xn_ready.sem, 1)

                normalise_tokens(sums1)
                dve.wait_ge(att_params, (lay + 1) * (16 * n_att_dmas))
                link(dve.tensor_scalar(gqs[:, :], gq[:, :], HD ** -0.5, None, ALU.mult))
                link(dve.tensor_scalar(g_mqs[:, :], g_mq[:, :], QK ** -0.5, None, ALU.mult))
                for s in range(2):
                    for k, (tab, g) in enumerate(((cosn, 0), (sinn, 1), (cosn, 1), (sinn, 0))):
                        gg = g_rope[:, s, 16 * g:16 * g + 16].unsqueeze(1).broadcast_to([P, CH, 16])
                        ins = dve.tensor_tensor(rot[:, s, k], tab[:, :, :], gg, ALU.mult)
                ins.then_inc(gains.sem, 1)
                for i in (2, 3):
                    full(f"xT{i}")
                    for k in range(2):
                        ins = dve.tensor_scalar(xT[:, 2 * i + k, :], bank(f"xT{i}")[:, k * SEQ:(k + 1) * SEQ],
                                                g1[:, 2 * i + k:2 * i + k + 1], None, ALU.mult)
                    release(ins, f"xT{i}")
                full("T0c1")
                release(dve.tensor_copy(proj[:, 1, 0:512], bank("T0c1")), "T0c1")
                full("T1ac1")
                release(dve.tensor_copy(proj[:, 1, 512:1024], bank("T1ac1")), "T1ac1")

                for use in ("T0c0", "T0c1", "T1ac0", "T1ac1", "T1b"):
                    dve.wait_ge(*is_evacuated(lay, use))
                q4 = proj[:, :, 0:AW]
                sqq = sq[:, 0:2 * AW].rearrange("p (c n) -> p c n", c=CH)
                link(dve.tensor_tensor(sqq, q4, q4, ALU.mult))
                ssq = st[:, 48:60]
                link(dve.tensor_reduce(ssq, sq[:, 0:2 * AW].rearrange("p (a d) -> p a d", d=HD), AX.X, ALU.add))
                dve.sem_inc(head_sums.sem, 1)
                qh = q4.rearrange("p c (h d) -> p c h d", h=AH)
                ks = [proj[:, c, C_KV + 256:C_KV + 768].rearrange("p (b n) -> p b n", b=2)[:, :, 0:128] for c in range(CH)]
                for c in range(CH):
                    link(dve.tensor_tensor(sq[:, 256 * c:256 * c + 256].rearrange("p (b n) -> p b n", b=2), ks[c], ks[c],
                                           ALU.mult))
                ss = st[:, 240:248]
                link(dve.tensor_reduce(ss, sq[:, 0:512].rearrange("p (a d) -> p a d", d=HD), AX.X, ALU.add))
                dve.sem_inc(head_sums.sem, 1)
                dve.wait_ge(head_roots.sem, head_roots.at(lay, 1))
                dve.tensor_tensor(qh, qh, bc(ssq.rearrange("p (c h) -> p c h", c=CH), [P, CH, AH, HD]), ALU.mult)\
                    .then_inc(q_normed.sem, 1)
                dve.wait_ge(head_roots.sem, head_roots.at(lay, 2))
                for c in range(CH):
                    kv = ks[c].rearrange("p b (h d) -> p b h d", h=AKV)
                    ins = dve.tensor_tensor(kv, kv, bc(ss[:, 4 * c:4 * c + 4].rearrange("p (b h) -> p b h", b=2),
                                                       [P, 2, AKV, HD]), ALU.mult)
                ins.then_inc(k_normed.sem, 1)
                dve.wait_ge(gate_e.sem, gate_e.at(lay, 1))
                link(dve.tensor_scalar(gates[:, :, :], gates[:, :, :], 1.0, None, ALU.add))
                link(dve.reciprocal(gates[:, :, :], gates[:, :, :]))
                g0 = gates[:, 0, 0:3 * AH:3]
                link(dve.tensor_scalar(g0, g0, const("row_ok"), None, ALU.mult))

                full("F23")
                release(dve.tensor_copy(conv_in[:, 2:4, 3:], bank("F23").rearrange("p (k n) -> p k n", k=2)), "F23")
                full("T3c1")
                release(dve.tensor_copy(proj[:, 1, O_BV:O_BV + 512], bank("T3c1")), "T3c1")
                full("T4c1")
                release(dve.tensor_copy(proj[:, 1, 1682:PROJ], bank("T4c1")[:, 0:360]), "T4c1")
                full("params")
                link(dve.tensor_copy(cols[:, 0:16], bank("params")[:, 0:16]))
                dve.wait_ge(cmp_zero.sem, cmp_zero.at(lay, 1))
                release(dve.tensor_copy(cmp_x[:, :, 2, 0:32:2], bank("params")[:, 16:48].rearrange("p (s j) -> p s j", s=2)),
                        "params")
                dve.wait_ge(*is_evacuated(lay, "F01"))
                dve.wait_ge(*is_evacuated(lay, "F23"))
                for j in range(CONV_K):
                    for k in range(4):
                        w = cols[:, 4 * j + k:4 * j + k + 1]
                        src = conv_in[:, k, j:j + SEQ]
                        if j == 0:
                            ins = dve.tensor_scalar(qk[:, k, :], src, w, None, ALU.mult)
                        else:
                            ins = dve.scalar_tensor_tensor(qk[:, k, :], src, w, qk[:, k, :], ALU.mult, ALU.add)
                        if j == CONV_K - 1 and k == 3:
                            ins.then_inc(conv_done.sem, 1)
                        elif k == 3:
                            link(ins)

                full("qT2")
                release(dve.tensor_scalar(qT[:, 4:6, :], bank("qT2")[0:HD, :].rearrange("p (k n) -> p k n", k=2),
                                          gqs[:, :], None, ALU.mult), "qT2")
                full("kT1")
                release(dve.tensor_scalar(kT[:, 1, :, :], bank("kT1")[0:HD, :].rearrange("p (k n) -> p k n", k=2),
                                          gk[:, :], None, ALU.mult), "kT1")
                full("cmp1")
                src = bank("cmp1").rearrange("p (k n) -> p k n", k=2)
                dve.tensor_copy(cmp_x[0:HD, 1, 0:2, :], src[0:HD])
                release(dve.tensor_copy(cmp_x[HD:P, 1, 0:2, 0:SEQ - 1], src[0:HD, :, 1:SEQ]), "cmp1")
                dve.wait_ge(conv_exp.sem, conv_exp.at(lay, 1))
                link(dve.tensor_scalar(ebuf[:, :, :], ebuf[:, :, :], 1.0, None, ALU.add))
                link(dve.reciprocal(ebuf[:, :, :], ebuf[:, :, :]))
                dve.tensor_tensor(qk[:, :, :], qk[:, :, :], ebuf[:, :, :], ALU.mult).then_inc(qk_ready.sem, 1)
                full("hid")
                link(dve.tensor_copy(st[0:HD, 2:4], bank("hid")[0:HD, 30:95:64]))
                for s in range(2):
                    ins = dve.tensor_scalar(hid_b[:, s, :], bank("hid")[0:HD, 64 * s:64 * s + 30], st[0:HD, 2 + s:3 + s],
                                            None, ALU.add)
                    if s == 0:
                        link(ins)
                ins.then_inc(hid_pre.sem, 1)
                dve.wait_ge(hid_exp.sem, hid_exp.at(lay, 1))
                ins = dve.tensor_scalar(hid_e[:, :, :], hid_e[:, :, :], 1.0, None, ALU.add)
                release(ins, "hid")
                dve.wait_ge(*is_evacuated(lay, "hid"))
                link(dve.reciprocal(hid_e[:, :, :], hid_e[:, :, :]))
                link(dve.tensor_tensor(hid_k, hid_b[:, 0, :], hid_e[:, 0, :], ALU.mult))
                vv = [v[:, 1, :].rearrange("p (h n) -> p h n", h=AKV).unsqueeze(2).broadcast_to([HD, AKV, AG, NCMP])
                      for v in (hid_b, hid_e)]
                dve.tensor_tensor(hid_v.rearrange("p (h g n) -> p h g n", h=AKV, g=AG), vv[0], vv[1], ALU.mult)\
                    .then_inc(hid_ready.sem, 1)
                full("ifT")
                link(dve.tensor_scalar(rowf, bank("ifT")[0:4, SEQ:2 * SEQ], if_bias[:, 1:2], None, ALU.add))
                dve.scalar_tensor_tensor(rowa, rowf, -1.0, rowf, ALU.mult, ALU.max).then_inc(f_abs.sem, 1)
                release(dve.tensor_scalar(rowi, bank("ifT")[0:4, 0:SEQ], if_bias[:, 0:1], None, ALU.add), "ifT")
                full("comp")
                link(dve.tensor_copy(ck, bank("comp")[0:30, 0:HD]))
                vsrc = bank("comp")[0:90, HD:2 * HD].unsqueeze(1).broadcast_to([90, AH, HD])
                link(dve.tensor_tensor(vblk[:, :, :], vsrc, bc(const("head_block")[0:90, :], [90, AH, HD]), ALU.mult))
                link(dve.tensor_tensor(sq[0:30, 0:HD], ck, ck, ALU.mult))
                ss = st[0:30, 4:5]
                ins = dve.tensor_reduce(ss, sq[0:30, 0:HD], AX.X, ALU.add)
                release(ins, "comp")
                dve.wait_ge(*is_evacuated(lay, "comp"))
                dve.sem_inc(head_sums.sem, 1)
                dve.wait_ge(head_roots.sem, head_roots.at(lay, 3))
                dve.tensor_scalar(ck, ck, ss, None, ALU.mult).then_inc(ck_ready.sem, 1)
                dve.sem_inc(vblk_ready.sem, 1)
                full("kcT")
                release(dve.tensor_scalar(kcT, bank("kcT")[0:HD, 0:30], gk[:, :], None, ALU.mult), "kcT")
                full("clog")
                dve.wait_ge(bias_dma, 32)
                for c in range(CH):
                    a = P * (1 - c) + CMP_L - 1
                    link(dve.tensor_tensor(clog[:, c], bank("clog")[:, c * 90:(c + 1) * 90].rearrange("p (h n) -> p h n", h=AH),
                                           bias_t[:, :, a:a + CMP_S * (NCMP - 1) + 1:CMP_S], ALU.add))
                cl = clog[:, :, :, :].rearrange("p c h n -> p (c h) n")
                cmx = st[:, 48:60]
                ins = dve.tensor_reduce(cmx, cl, AX.X, ALU.max)
                release(ins, "clog")
                dve.wait_ge(*is_evacuated(lay, "clog"))
                dve.tensor_tensor(cl, cl, bc(cmx, [P, 2 * AH, NCMP]), ALU.subtract).then_inc(clog_pre.sem, 1)
                dve.wait_ge(f_log.sem, f_log.at(lay, 1))
                link(dve.scalar_tensor_tensor(rowf, rowf, 0.0, rowa, ALU.min, ALU.subtract))
                link(dve.tensor_tensor_scan(rowB, ones[0:4, 0:1].broadcast_to([4, SEQ]), rowf, 0.0, ALU.mult, ALU.add))
                link(dve.tensor_tensor(rowu, rowi, rowB, ALU.subtract))
                link(dve.tensor_tensor_scan(rowm, rowu, rowu, 0.0, ALU.max, ALU.max))
                link(dve.tensor_scalar(rownm, rowm, -1.0, None, ALU.mult))
                dve.tensor_tensor(rowm, rowm, rowB, ALU.add).then_inc(um_ready.sem, 1)
                dve.wait_ge(clog_exp.sem, clog_exp.at(lay, 1))
                csum = st[:, 144:156]
                link(dve.tensor_reduce(csum, cl, AX.X, ALU.add))
                link(dve.reciprocal(csum, csum))
                csum3 = csum.rearrange("p (c h) -> p c h", c=CH)
                link(dve.tensor_tensor(csum3, csum3, gates[:, :, 0:3 * AH:3], ALU.mult))
                full("umT")
                ins = dve.tensor_copy(st[:, 16:32], bank("umT")[:, 0:16])
                release(ins, "umT")
                dve.wait_ge(*is_evacuated(lay, "umT"))
                dve.sem_inc(um_cols.sem, 1)
                for i in range(2):
                    full(f"mB{i}")
                    src = bank(f"mB{i}").rearrange("p (k n) -> p k n", k=2)
                    dve.tensor_tensor(E1[:, 2 * i:2 * i + 2, :], src,
                                      const("after").unsqueeze(1).broadcast_to([P, 2, SEQ]), ALU.add).then_inc(e_pre.sem, 1)
                for i in range(2):
                    src = bank(f"mB{i}").rearrange("p (k n) -> p k n", k=2)
                    ins = dve.tensor_tensor(E2[:, 2 * i:2 * i + 2, :], src[:, :, P:SEQ],
                                            const("after")[:, 0:P].unsqueeze(1).broadcast_to([P, 2, P]), ALU.add)
                    release(ins, f"mB{i}")
                    dve.wait_ge(*is_evacuated(lay, f"mB{i}"))
                    dve.sem_inc(e_pre.sem, 1)
                for c in range(CH):
                    full(f"cO{c}")
                    release(dve.tensor_tensor(y[:, c, 0:AW].rearrange("p (h d) -> p h d", h=AH),
                                              bank(f"cO{c}")[:, 0:AW].rearrange("p (h d) -> p h d", h=AH),
                                              bc(csum3[:, c, :], [P, AH, HD]), ALU.mult), f"cO{c}")
                dve.wait_ge(sumsc.sem, sumsc.at(lay, 1))
                for i, (a, w) in enumerate(((O_DQ, QR), (O_DKV, KVR), (O_KR, ROPE))):
                    v = proj[:, :, a:a + w]
                    ins = dve.tensor_tensor(v, v, bc(st[:, 8 + 2 * i:10 + 2 * i], [P, CH, w]), ALU.mult)
                ins.then_inc(c_normed.sem, 1)
                for i in range(4):
                    j, odd = i // 2, i % 2
                    tile = (E1, E2)[j]
                    nn = SEQ - j * P
                    full(f"SS{i}")
                    dve.wait_ge(e_exp.sem, e_exp.at(lay, 4 + 4 * j))
                    ev = tile[:, odd:BH:2, :]
                    release(dve.scalar_tensor_tensor(ev, bank(f"SS{i}")[:, 0:2 * nn].rearrange("p (k n) -> p k n", k=2),
                                                     HD ** -0.5, ev, ALU.mult, ALU.mult), f"SS{i}")
                    dve.wait_ge(*is_evacuated(lay, f"SS{i}"))
                    dve.sem_inc(g_ready.sem, 1)
                full("dkvT")
                release(dve.tensor_scalar(xT[:, 5, :], bank("dkvT")[:, 0:SEQ], g_kva[:, :], None, ALU.mult), "dkvT")
                for c in range(CH):
                    full(f"num{c}")
                    ins = dve.tensor_copy(nd[:, BH * c:BH * c + BH, :],
                                          bank(f"num{c}")[:, 0:BH * (HD + 1)].rearrange("p (h d) -> p h d", h=BH))
                    release(ins, f"num{c}")
                dve.wait_ge(*is_evacuated(lay, "num1"))
                dve.wait_ge(em_ready.sem, em_ready.at(lay, 1))
                den = st[:, 48:56]
                link(dve.scalar_tensor_tensor(den, nd[:, :, HD], -1.0, nd[:, :, HD], ALU.mult, ALU.max))
                link(dve.tensor_tensor(den, den, st[:, 32:40], ALU.max))
                link(dve.reciprocal(den, den))
                hb = hB.rearrange("p c (h d) -> p (c h) d", h=BH)
                link(dve.tensor_tensor(hb, nd[:, :, 0:HD], bc(den, [P, 2 * BH, HD]), ALU.mult))
                sqb = nd[:, :, 0:HD]
                link(dve.tensor_tensor(sqb, hb, hb, ALU.mult))
                link(dve.tensor_reduce(den, sqb, AX.X, ALU.add))
                dve.sem_inc(head_sums.sem, 1)
                dve.wait_ge(eo_ready.sem, eo_ready.at(lay, 1))
                link(dve.tensor_scalar(eo[:, :, :], eo[:, :, :], 1.0, None, ALU.add))
                link(dve.reciprocal(eo[:, :, :], eo[:, :, :]))
                dve.wait_ge(head_roots.sem, head_roots.at(lay, 4))
                link(dve.tensor_tensor(hb, hb, bc(den, [P, 2 * BH, HD]), ALU.mult))
                link(dve.tensor_tensor(y[:, :, AW:AW + BW], hB, eo[:, :, :], ALU.mult))

                for c in range(CH):
                    full(f"uq{c}1")
                    release(dve.tensor_copy(qc[:, c, 3:6, :],
                                            bank(f"uq{c}1")[:, 0:3 * QK].rearrange("p (h d) -> p h d", h=3)), f"uq{c}1")
                for c in range(CH):
                    full(f"ukv{c}1")
                    src = bank(f"ukv{c}1")[:, 0:3 * P].rearrange("p (h d) -> p h d", h=3)
                    dve.tensor_copy(kc[:, c, 3:6, 0:NOPE], src[:, :, 0:NOPE])
                    release(dve.tensor_copy(vC[:, c, 3:6, :], src[:, :, NOPE:]), f"ukv{c}1")
                for c in range(CH):
                    for k in range(2):
                        dve.wait_ge(*is_evacuated(lay, f"uq{c}{k}"))
                        dve.wait_ge(*is_evacuated(lay, f"ukv{c}{k}"))
                qf = qc.rearrange("p c h d -> p (c h) d")
                kf = kc.rearrange("p c h d -> p (c h) d")
                sqm = sq[:, 0:12 * QK].rearrange("p (a d) -> p a d", d=QK)
                rq, rk, rr = st[:, 208:220], st[:, 220:232], st[:, 232:244]
                link(dve.tensor_tensor(sqm, qf, qf, ALU.mult))
                link(dve.tensor_reduce(rq, sqm[:, :, 0:NOPE], AX.X, ALU.add))
                link(dve.tensor_reduce(rr, sqm[:, :, NOPE:], AX.X, ALU.add))
                link(dve.tensor_tensor(sqm[:, :, 0:NOPE], kf[:, :, 0:NOPE], kf[:, :, 0:NOPE], ALU.mult))
                link(dve.tensor_reduce(rk, sqm[:, :, 0:NOPE], AX.X, ALU.add))
                dve.sem_inc(head_sums.sem, 1)
                dve.wait_ge(head_roots.sem, head_roots.at(lay, 5))
                link(dve.tensor_tensor(qf[:, :, 0:NOPE], qf[:, :, 0:NOPE], bc(rq, [P, 12, NOPE]), ALU.mult))
                link(dve.tensor_tensor(qf[:, :, NOPE:], qf[:, :, NOPE:], bc(rr, [P, 12, ROPE]), ALU.mult))
                link(dve.tensor_tensor(kf[:, :, 0:NOPE], kf[:, :, 0:NOPE], bc(rk, [P, 12, NOPE]), ALU.mult))
                tm = [tmpr[:, i, :].rearrange("p (c h f) -> p c h f", c=CH, h=CHD) for i in range(4)]
                q1, q2 = qc[:, :, :, NOPE:NOPE + 16], qc[:, :, :, NOPE + 16:]
                for i, (src, tab) in enumerate(((q1, 0), (q2, 1), (q2, 2), (q1, 3))):
                    link(dve.tensor_tensor(tm[i], src, rot[:, 0, tab].unsqueeze(2).broadcast_to([P, CH, CHD, 16]), ALU.mult))
                link(dve.tensor_tensor(q1, tm[0], tm[1], ALU.subtract))
                link(dve.tensor_tensor(q2, tm[2], tm[3], ALU.add))
                k1, k2 = proj[:, :, O_KR:O_KR + 16], proj[:, :, O_KR + 16:O_KR + 32]
                tk = [tmpr[:, i, 0:CH * 16].rearrange("p (c f) -> p c f", c=CH) for i in range(4)]
                for i, (src, tab) in enumerate(((k1, 0), (k2, 1), (k2, 2), (k1, 3))):
                    link(dve.tensor_tensor(tk[i], src, rot[:, 1, tab], ALU.mult))
                tkb = [v.unsqueeze(2).broadcast_to([P, CH, CHD, 16]) for v in tk]
                link(dve.tensor_tensor(kc[:, :, :, NOPE:NOPE + 16], tkb[0], tkb[1], ALU.subtract))
                dve.tensor_tensor(kc[:, :, :, NOPE + 16:], tkb[2], tkb[3], ALU.add).then_inc(mcat_ready.sem, 1)
                for i in range(3):
                    full(f"mk{i}")
                    release(dve.tensor_scalar(mkT[:, 2 * i:2 * i + 2, :], bank(f"mk{i}")[0:QK, :].rearrange("p (k n) -> p k n", k=2),
                                              g_mk[:, :], None, ALU.mult), f"mk{i}")

                def scores(g):
                    full(f"LA{g}")
                    full(f"LB{g}")
                    if g >= 2:
                        dve.wait_ge(*is_filled(lay, f"PB{g - 2}"))
                    settle(dve)
                    for i in range(4):
                        c, k = i // 2, i % 2
                        hh = 2 * (g % 3) + k
                        nn = (c + 1) * P
                        a = k * P if c == 0 else 256 + k * SEQ
                        b0 = P if c == 0 else 0
                        bias = bias_t[:, hh, b0:SEQ] if g < 6 else const("causal")[:, b0:SEQ]
                        ins = dve.tensor_tensor_reduce(LP[g % 2][:, a:a + nn],
                                                       bank(f"LA{g}" if c == 0 else f"LB{g}")[:, k * nn:(k + 1) * nn], bias,
                                                       1.0, LOWEST, ALU.add, ALU.max,
                                                       st[:, 160 + 4 * (g % 2) + i:161 + 4 * (g % 2) + i])
                        if i == 1:
                            release(ins, f"LA{g}")
                        if i == 3:
                            release(ins, f"LB{g}")
                    dve.wait_ge(*is_evacuated(lay, f"LA{g}"))
                    dve.wait_ge(*is_evacuated(lay, f"LB{g}"))
                    v = st[:, 160 + 4 * (g % 2):164 + 4 * (g % 2)]
                    dve.tensor_scalar(v, v, -1.0, None, ALU.mult).then_inc(p_pre.sem, 1)

                def weighted(g):
                    kind, pair = g // 3, g % 3
                    s = st[:, 176 + 4 * g:180 + 4 * g]
                    link(dve.reciprocal(s, s))
                    s3 = s.rearrange("p (c k) -> p c k", c=CH)
                    if kind < 2:
                        gg = gates[:, :, 6 * pair + kind + 1:6 * pair + 6:3]
                        link(dve.tensor_tensor(s3, s3, gg, ALU.mult))
                    full(f"O{g}")
                    src = bank(f"O{g}")[:, 0:4 * HD].rearrange("p (c k d) -> p c k d", c=CH, k=2)
                    a = (AW + BW if kind == 2 else 0) + pair * 2 * HD
                    dst = y[:, :, a:a + 2 * HD].rearrange("p c (k d) -> p c k d", k=2)
                    sb3 = bc(s3, [P, CH, 2, HD])
                    if kind == 2:
                        release(dve.tensor_tensor(dst, src, sb3, ALU.mult), f"O{g}")
                    else:
                        tmp = sq[:, 0:4 * HD].rearrange("p (c k d) -> p c k d", c=CH, k=2)
                        ins = dve.tensor_tensor(tmp, src, sb3, ALU.mult)
                        release(ins, f"O{g}")
                        dve.wait_ge(*is_evacuated(lay, f"O{g}"))
                        link(dve.tensor_tensor(dst, dst, tmp, ALU.add))

                for s in range(N_GROUPS_ATT + 2):
                    if s < N_GROUPS_ATT:
                        scores(s)
                    if 1 <= s <= N_GROUPS_ATT:
                        full(f"PB{s - 1}")
                        release(dve.tensor_copy(PT[(s - 1) % 2][:, 4:6, :],
                                                bank(f"PB{s - 1}")[:, 0:256].rearrange("p (i n) -> p i n", i=2)), f"PB{s - 1}")
                    if s >= 2:
                        dve.wait_ge(p_exp.sem, p_exp.at(lay, s - 1))
                        weighted(s - 2)
                dve.wait_ge(*is_evacuated(lay, f"O{N_GROUPS_ATT - 1}"))
                dve.wait_ge(*is_evacuated(lay, f"O{N_GROUPS_ATT - 2}"))
                dve.sem_inc(y_all.sem, 1)
                dve.wait_ge(sumsy.sem, sumsy.at(lay, 1))
                for i, a in enumerate((0, AW + BW)):
                    v = y[:, :, a:a + AW]
                    ins = dve.tensor_tensor(v, v, bc(st[:, 40 + 2 * i:42 + 2 * i], [P, CH, AW]), ALU.mult)
                ins.then_inc(y_scaled.sem, 1)
                for i in (2, 3):
                    full(f"yT{i}")
                    for k in range(2):
                        ins = dve.tensor_scalar(xT[:, 2 * i + k, :], bank(f"yT{i}")[:, k * SEQ:(k + 1) * SEQ],
                                                gy[:, 2 * i + k:2 * i + k + 1], None, ALU.mult)
                    release(ins, f"yT{i}")
                for half in range(2):
                    for c in range(CH):
                        use = f"wo{c}{half}"
                        full(use)
                        v = x[:, c, half * 512:(half + 1) * 512]
                        release(dve.tensor_tensor(v, v, bank(use), ALU.add), use)
                dve.wait_ge(*is_evacuated(lay, "wo11"))
                dve.sem_inc(x_mid.sem, 1)

                normalise_tokens(sums2)
                dve.wait_ge(moe_params, (lay + 1) * (16 * n_moe_dmas))
                for i in (2, 3):
                    full(f"nT{i}")
                    for k in range(2):
                        ins = dve.tensor_scalar(xT[:, 2 * i + k, :], bank(f"nT{i}")[:, k * SEQ:(k + 1) * SEQ],
                                                g2[:, 2 * i + k:2 * i + k + 1], None, ALU.mult)
                    release(ins, f"nT{i}")
                full("rout")
                ins = dve.tensor_tensor(rl, bank("rout")[:, 0:2 * (NG + NE)].rearrange("p (c n) -> p c n", c=CH),
                                        b_rout[:, :].unsqueeze(1).broadcast_to([P, CH, NG + NE]), ALU.add)
                release(ins, "rout")
                dve.wait_ge(*is_evacuated(lay, "rout"))
                link(dve.memset(pg, LOWEST))
                link(dve.tensor_copy(pg[:, :, 0:NG], rl[:, :, 0:NG]))
                for c in range(CH):
                    link(dve.max(m8[:, c, :], pg[:, c, :]))
                for c in range(CH):
                    link(dve.max_index(i8g[:, c, :], m8[:, c, :], pg[:, c, :]))
                v = pg[:, :, 0:NG]
                link(dve.tensor_tensor(v, v, m8[:, :, 0:1].broadcast_to([P, CH, NG]), ALU.subtract))
                dve.sem_inc(ge_pre.sem, 1)
                gi = st[:, 128:130]
                link(dve.tensor_copy(gi, i8g[:, :, 0]))
                iota = const("iota")
                ohg = oh[:, 0, :, 0:NG]
                link(dve.tensor_tensor(ohg, iota[:, 0:NG].unsqueeze(1).broadcast_to([P, CH, NG]), bc(gi, [P, CH, NG]),
                                       ALU.is_equal))
                for c in range(CH):
                    link(dve.tensor_tensor(elp[:, c, :].rearrange("p (g j) -> p g j", g=NG),
                                           rl[:, c, NG:].rearrange("p (g j) -> p g j", g=NG),
                                           bc(ohg[:, c, :], [P, NG, EPG]), ALU.mult))
                link(dve.tensor_reduce(els, elp.rearrange("p c (g j) -> p c j g", g=NG), AX.X, ALU.add))
                for c in range(CH):
                    link(dve.max(m8e[:, c, :], els[:, c, :]))
                link(dve.tensor_tensor(st[:, 138:140], m8e[:, :, 1], m8e[:, :, 0], ALU.subtract))
                dve.sem_inc(e2_pre.sem, 1)
                for c in range(CH):
                    link(dve.max_index(i8e[:, c, :], m8e[:, c, :], els[:, c, :]))
                eid = st[:, 130:134].rearrange("p (k c) -> p k c", k=2)
                for k in range(2):
                    link(dve.tensor_copy(eid[:, k, :], i8e[:, :, k]))
                    link(dve.scalar_tensor_tensor(eid[:, k, :], gi, float(EPG), eid[:, k, :], ALU.mult, ALU.add))
                for k in range(2):
                    link(dve.tensor_tensor(oh[:, k], iota[:, 0:NE].unsqueeze(1).broadcast_to([P, CH, NE]),
                                           bc(eid[:, k, :], [P, CH, NE]), ALU.is_equal))
                link(dve.tensor_tensor(ind, oh[:, 0], oh[:, 1], ALU.add))
                dve.sem_inc(ind_ready.sem, 1)
                dve.wait_ge(ge_exp.sem, ge_exp.at(lay, 1))
                gs = st[:, 142:144]
                link(dve.tensor_reduce(gs, pg[:, :, 0:NG], AX.X, ALU.add))
                dve.wait_ge(e2_exp.sem, e2_exp.at(lay, 1))
                e2 = st[:, 140:142]
                w12 = st[:, 132:136].rearrange("p (c k) -> p c k", c=CH)
                tmpw = st[:, 156:158]
                link(dve.tensor_scalar(tmpw, e2, 1.0, None, ALU.add))
                link(dve.tensor_tensor(tmpw, tmpw, gs, ALU.mult))
                link(dve.reciprocal(w12[:, :, 0], tmpw))
                link(dve.tensor_tensor(w12[:, :, 1], w12[:, :, 0], e2, ALU.mult))
                full("rank")
                link(dve.tensor_copy(cnt, bank("rank")[:, 2 * NE:3 * NE]))
                link(dve.tensor_tensor_scan(offs, ones[:, 0:NE], cnt, 0.0, ALU.mult, ALU.add))
                link(dve.tensor_tensor(offs, offs, cnt, ALU.subtract))
                link(dve.tensor_copy(offs_i[0:1, :], offs[0:1, :]))
                dve.sem_inc(offs_ready.sem, 1)
                ins = dve.tensor_tensor(base, bank("rank")[:, 0:2 * NE].rearrange("p (c e) -> p c e", c=CH),
                                        offs.unsqueeze(1).broadcast_to([P, CH, NE]), ALU.add)
                release(ins, "rank")
                dve.wait_ge(*is_evacuated(lay, "rank"))
                for c in range(CH):
                    for k in range(2):
                        link(dve.tensor_tensor_reduce(junk, oh[:, k, c], base[:, c], 1.0, 0.0, ALU.mult, ALU.add,
                                                      st[:, 128 + 2 * c + k:129 + 2 * c + k]))
                dve.sem_inc(w_ready.sem, 1)
                for c in range(CH):
                    link(dve.tensor_scalar(tmpS, iota, st[:, 128 + 2 * c:129 + 2 * c], None, ALU.is_equal))
                    link(dve.scalar_tensor_tensor(S[:, c, :], iota, st[:, 129 + 2 * c:130 + 2 * c], tmpS, ALU.is_equal,
                                                  ALU.add))
                dve.sem_inc(S_ready.sem, 1)
                for mm in range(1, KM, 2):
                    full(f"xs{mm}")
                    release(dve.tensor_scalar(xs[:, mm, 0:NSLOT], bank(f"xs{mm}"), g2[:, mm:mm + 1], None, ALU.mult),
                            f"xs{mm}")

                link(dve.tensor_scalar(jx, cnt, float(WIN), None, ALU.is_gt))
                for k in range(2, SEQ // WIN):
                    link(dve.scalar_tensor_tensor(jx, cnt, float(k * WIN), jx, ALU.is_gt, ALU.add))
                link(dve.tensor_tensor_scan(jlast, ones[:, 0:NE], jx, 1.0, ALU.mult, ALU.add))
                link(dve.tensor_tensor(jfirst, jlast, jx, ALU.subtract))
                place = bc(iota[:, 0:NJOB], [P, NJOB, NE])

                def by_expert(v):
                    return v.unsqueeze(1).broadcast_to([P, NJOB, NE])

                link(dve.tensor_tensor(jM, place, by_expert(jfirst), ALU.is_ge))
                link(dve.tensor_tensor(jt, place, by_expert(jlast), ALU.is_lt))
                link(dve.tensor_tensor(jM, jM, jt, ALU.mult))
                link(dve.tensor_tensor(jt, place, by_expert(jfirst), ALU.subtract))
                link(dve.tensor_scalar(jt, jt, 1.0, float(WIN), ALU.add, ALU.mult))
                link(dve.tensor_scalar(jx, cnt, float(WIN), None, ALU.subtract))
                link(dve.tensor_tensor(jt, jt, by_expert(jx), ALU.min))
                link(dve.tensor_tensor(jt, jt, by_expert(offs), ALU.add))
                link(dve.tensor_tensor(jt, jt, jM, ALU.mult))
                link(dve.tensor_reduce(jobs[:, 0:NJOB], jt, AX.X, ALU.add))
                link(dve.tensor_tensor(jt, jM, by_expert(iota[:, 0:NE]), ALU.mult))
                link(dve.tensor_reduce(jobs[:, NJOB:2 * NJOB], jt, AX.X, ALU.add))
                link(dve.tensor_copy(jobs[:, 0:1], offs[:, NE - 1:NE]))
                link(dve.memset(jobs[:, NJOB:NJOB + 1], float(NE - 1)))
                link(dve.tensor_copy(jobs[:, 2 * NJOB:2 * NJOB + 1], jlast[:, NE - 1:NE]))
                link(dve.tensor_copy(jobs[0:1, 2 * NJOB + 1:], jobs_before[:, :]))
                link(dve.tensor_tensor(jobs_before[:, :], jobs_before[:, :], jobs[0:1, 2 * NJOB:2 * NJOB + 1], ALU.add))
                link(dve.tensor_copy(jobs_i[0:1, :], jobs[0:1, :]))
                dve.sem_inc(jobs_made.sem, 1)

                def gate_times_up(u):
                    return dve.tensor_tensor(h, sg, PS[:, u % 3, P:2 * P], ALU.mult)

                def store(o, u):
                    return dve.tensor_copy(ysT[:, :, bass.ds(o, WIN)],
                                           PS[:, 4 + u % 3, :].rearrange("p (m n) -> p m n", m=KM))

                def gated(e, u):
                    dve.wait_ge(sg_ready.sem, sg_ready.at(lay, e + 1))
                    gate_times_up(u).then_inc(h_ready.sem, 1)

                def stored(e, u):
                    o = dve.value_load(offs_i[0:1, bass.ds(e, 1)], min_val=0, max_val=NSLOT)
                    dve.wait_ge(y_full.sem, y_full.at(lay, e + 1))
                    dve.wait_ge(y_stored.sem, y_stored.at(lay, e))
                    store(o, u).then_inc(y_stored.sem, 1)

                dve.wait_ge(xs_pad.sem, xs_pad.at(lay, 1))
                gated(0, 0)
                with dve.Fori(0, NEX // 3) as it:
                    for u in range(3):
                        gated(it * 3 + (1 + u), 1 + u)
                        stored(it * 3 + u, u)
                stored(NEX - 1, NEX - 1)
                dve.wait_ge(y_stored.sem, y_stored.at(lay, NEX))
                settle(dve)
                n_jobs, before = job_counts(dve)
                with dve.Fori(0, n_jobs) as it:
                    g = before + it
                    o = job_entry(dve, 0, it, NSLOT)
                    wait_job(dve, "sg_ready", g + 1)
                    gate_times_up(JOB).then_inc(job["h_ready"].sem, 1)
                    wait_job(dve, "y_full", g + 1)
                    wait_job(dve, "y_stored", g)
                    store(o, JOB).then_inc(job["y_stored"].sem, 1)

                full("cw1")
                release(dve.tensor_copy(cwT[:, 2:4, :], bank("cw1").rearrange("p (k n) -> p k n", k=2)), "cw1")
                for i in range(1, 8, 2):
                    full(f"ys{i}")
                    release(dve.tensor_copy(ys[:, i // 2, 512:1024], bank(f"ys{i}")), f"ys{i}")
                for c in range(CH):
                    for half in range(2):
                        use = f"fo{c}{half}"
                        full(use)
                        v = x[:, c, half * 512:(half + 1) * 512]
                        release(dve.tensor_tensor(v, v, bank(use), ALU.add), use)
                dve.wait_ge(*is_evacuated(lay, "fo11"))
                dve.sem_inc(x_new.sem, 1)


_INS = ['x', 'positions', 'rel_bias', 'norm1_g', 'w_in', 'nsa_cmp_pe', 'nsa_cmp_w1', 'nsa_cmp_w2', 'nsa_q_norm',
        'nsa_k_norm', 'nsa_out_norm', 'mlstm_conv', 'mlstm_i_bias', 'mlstm_f_bias', 'mlstm_out_norm', 'mla_q_a_norm',
        'mla_w_uq', 'mla_kv_a_norm', 'mla_w_ukv', 'mla_qk_norm', 'mla_out_norm', 'w_out', 'norm2_g', 'moe_w_group',
        'moe_b_group', 'moe_w_expert', 'moe_b_expert', 'moe_w_gate', 'moe_w_up', 'moe_w_down']


def shape_constants():
    import numpy as np
    f = np.float32
    p = np.arange(P)[:, None]
    u = np.arange(SEQ)[None, :]
    tab = {
        "ident": np.eye(P, dtype=f),
        "before": (p < np.arange(P)[None, :]).astype(f),
        "causal": np.where(P + p - u < 0, f(NEG), f(0)),
        "after": np.where(u < p, f(NEG), f(0)),
        "iota": np.broadcast_to(np.arange(NSLOT, dtype=f), (P, NSLOT)),
        "inv_freq": np.broadcast_to(f(1.0) / (f(10000.0) ** (np.arange(16, dtype=f) * f(2.0) / f(ROPE))), (P, 16)),
        "row_ok": (p >= CMP_L - 1).astype(f),
        "head_block": (p // NCMP == np.arange(AH)[None, :]).astype(f),
    }
    c128 = np.ascontiguousarray(np.concatenate([tab[n] for n, _ in C128], axis=1).astype(f))
    dist = 255 - np.arange(512)
    nn = np.maximum(dist, 0)
    large = 16 + (np.log(np.maximum(nn, 1).astype(f) / f(16)) / f(np.log(8.0)) * f(16)).astype(np.int32)
    bucket = np.where(nn < 16, nn, np.minimum(large, 31))
    c33 = np.zeros((33, 512), f)
    c33[bucket, np.arange(512)] = 1.0
    c33[:32, dist < 0] = 0.0
    c33[32, dist < 0] = NEG
    c4 = np.kron(np.eye(4, dtype=f), np.ones((1, P), f))
    return {"c128": c128, "c33": c33, "c4": c4}


def kernel(**inputs):
    import numpy as _np
    import concourse.bacc as _bacc
    from concourse import mybir as _mybir
    from concourse.bass_utils import run_bass_kernel_spmd as _run

    nc = _bacc.Bacc("TRN2", target_bir_lowering=False, num_devices=1)
    arrays, aps = {}, {}
    given = {n: _np.ascontiguousarray(inputs[n]) for n in _INS}
    given.update(shape_constants())
    for name, a in given.items():
        arrays[f"in_{name}"] = a
        aps[name] = nc.dram_tensor(f"in_{name}", a.shape, _mybir.dt.from_np(a.dtype), kind="ExternalInput").ap()
    out = nc.dram_tensor("out_0", (1, SEQ, D), F32, kind="ExternalOutput").ap()
    trunk(nc, aps, out)
    r = _run(nc, [arrays], core_ids=[0])
    return r.results[0]["out_0"]
```

```python
from contextlib import ExitStack

import concourse.bass as bass
from concourse import mybir

ALU = mybir.AluOpType
ACT = mybir.ActivationFunctionType
AX = mybir.AxisListType
F32 = mybir.dt.float32
I32 = mybir.dt.int32
U32 = mybir.dt.uint32

P = 128
D = 1024
KM = D // P
SEQ = 256
CH = SEQ // P
DEPTH = 2
HD = 64
AH, AKV = 6, 2
AG = AH // AKV
AW = AH * HD
BH = 4
BW = BH * HD
CHD = 6
NOPE, ROPE = 64, 32
QK = NOPE + ROPE
QR, KVR = 192, 128
QRC = QR // 2
CMP_L, CMP_S = 32, 16
NCMP = (SEQ - CMP_L) // CMP_S + 1
CONV_K = 4
NG, EPG = 4, 8
NE = NG * EPG
FE = 256
NSLOT = 2 * SEQ
WIN = 64
NEX = NE - 1
NJOB = 8
EPS = 1e-6
NEG = -1e30
LOWEST = -3.0e38
BIASW = 384

C_KV, C_GATE, C_BQK, C_BV = AW, 1152, 1170, 1682
O_BV = C_BV - 512
O_IF, O_O, O_DQ = O_BV + BW, O_BV + BW + 8, O_BV + 2 * BW + 8
O_DKV, O_KR, PROJ = O_DQ + QR, O_DQ + QR + KVR, O_DQ + QR + KVR + ROPE
W_IN_ITEMS = [(1682, 2194), (2194, 2554), (0, 512), (512, 1170), (1170, 1682)]
SLOT = KM * 768
NSLOTS = 3
E0 = len(W_IN_ITEMS) + 2
EXTRA = 3
N_RING = NEX - 1
ITEM_DMAS = [1, 1, 3, 1, 1, 1, 1] + [2] * N_RING
JOB_SLOT = (E0 + N_RING) % NSLOTS
JOB = NEX % 3

C128 = [("ident", 128), ("before", 128), ("causal", 256), ("after", 256), ("iota", 512),
        ("inv_freq", 16), ("row_ok", 1), ("head_block", 6)]
C128_AT = {}
_at = 0
for _n, _w in C128:
    C128_AT[_n] = (_at, _w)
    _at += _w
C128_W = _at

N_GROUPS_ATT = 9
FILLERS = [[["kcT"], [], ["clog"]],
           [[], ["cPT"], []],
           [["cO0"], ["cO1"], ["SS0"]],
           [["SS1"], ["SS2"], ["SS3"]],
           [["num0"], ["num1"], ["mq0"]],
           [["mq1"], ["mq2"], ["mk0"]],
           [["mk1", "mk2"], [], []]]
FILLERS += [[[], [], []]] * (N_GROUPS_ATT + 2 - len(FILLERS))


def group_uses():
    uses = []
    for s in range(N_GROUPS_ATT + 2):
        if s == 6:
            uses += [(f, 7) for f in FILLERS[s][0]]
        if s < N_GROUPS_ATT:
            uses += [(f"LA{s}", 2 * (s % 2)), (f"LB{s}", 2 * (s % 2) + 1)]
        if s != 6:
            uses += [(f, 7) for f in FILLERS[s][0]]
        if 1 <= s <= N_GROUPS_ATT:
            uses += [(f"PA{s - 1}", 4), (f"PB{s - 1}", 5)]
        uses += [(f, 7) for f in FILLERS[s][1]]
        if s >= 2:
            uses += [(f"O{s - 2}", 6)]
        uses += [(f, 7) for f in FILLERS[s][2]]
    return uses


BANK_USES = [(f"xT{i}", i) for i in range(4)]
for _i, _n in enumerate(
        ["T3c0", "T3c1", "T4c0", "T4c1", "T0c0", "dqT", "dkvT", "ifT", "params", "T0c1", "uq00", "uq01", "uq10", "uq11",
         "ukv00", "ukv01", "ukv10", "ukv11", "umT", "mB0", "mB1", "T1ac0", "T1ac1", "T1b", "cmp0", "cmp1", "F01", "hid",
         "qT0", "qT1", "qT2", "kT0", "kT1", "F23", "comp"]):
    BANK_USES.append((_n, (4 + _i) % 8))
BANK_USES += group_uses()
BANK_USES += [(f"yT{i}", i) for i in range(4)] + [("wo00", 4), ("wo01", 5), ("wo10", 6), ("wo11", 7)]
BANK_USES += [(f"nT{i}", i) for i in range(4)] + [("rout", 4), ("rank", 5)]
BANK_USES += [(f"xs{m}", (6 + m) % 8) for m in range(8)] + [("cw0", 7), ("cw1", 2)]
BANK_USES += [(f"ys{i}", i) for i in range(8)] + [("fo00", 0), ("fo01", 1), ("fo10", 2), ("fo11", 3)]
PER_BANK = [sum(b == k for _, b in BANK_USES) for k in range(8)]
USE = {}
for _n, _b in BANK_USES:
    assert _n not in USE
    USE[_n] = (_b, 1 + sum(1 for x, b in BANK_USES[:[u[0] for u in BANK_USES].index(_n)] if b == _b))


def landed_at(item):
    s = item % NSLOTS
    return s, 16 * sum(ITEM_DMAS[j] for j in range(s, item + 1, NSLOTS))


DOWN_PER_LAYER = [16 * len(range((s - E0) % NSLOTS, N_RING, NSLOTS)) for s in range(NSLOTS)]
LANDED_PER_LAYER = [16 * sum(ITEM_DMAS[s::NSLOTS]) for s in range(NSLOTS)]


def trunk(nc, t, out):
    x_in, positions, rel_bias = t["x"], t["positions"], t["rel_bias"]
    ctx = ExitStack()
    with ctx:
        def sb(name, shape, dt=F32):
            return ctx.enter_context(nc.sbuf_tensor(name, shape, dt))

        waits_passed = ctx.enter_context(nc.semaphore("waits_passed"))

        def settle(eng):
            eng.sem_inc(waits_passed, 1)

        class Signal:
            def __init__(self, name, per, credit=0):
                self.sem = ctx.enter_context(nc.semaphore(name))
                self.per, self.credit = per, credit

            def at(self, lay, k):
                return lay * self.per + (k + self.credit)

        x = sb("x", [P, CH, D])
        ring = sb("ring", [P, NSLOTS, SLOT])
        cst = sb("cst", [P, C128_W])
        ident = cst[:, 0:128]

        def const(name):
            a, w = C128_AT[name]
            return cst[:, a:a + w]

        ones = sb("ones", [P, P])
        bias_t = sb("bias_t", [P, AH, BIASW])
        sel4 = sb("sel4", [4, 4 * P])
        cosn = sb("cosn", [P, CH, 16])
        sinn = sb("sinn", [P, CH, 16])
        rot = sb("rot", [P, 2, 4, CH, 16])
        w_uq = sb("w_uq", [QRC, 2, CHD * QK])
        w_ukv = sb("w_ukv", [P, CHD * P])
        w_cmp2 = sb("w_cmp2", [HD, 2, HD])
        rows = sb("rows", [48, P])
        cols = sb("cols", [P, 48])
        g1 = sb("g1", [P, KM])
        g2 = sb("g2", [P, KM])
        gy = sb("gy", [P, KM])
        gq = sb("gq", [HD, 1])
        gqs = sb("gqs", [HD, 1])
        gk = sb("gk", [HD, 1])
        if_bias = sb("if_bias", [4, 2])
        g_qa = sb("g_qa", [QRC, 2])
        g_kva = sb("g_kva", [P, 1])
        g_mq = sb("g_mq", [QK, 1])
        g_mqs = sb("g_mqs", [QK, 1])
        g_mk = sb("g_mk", [QK, 1])
        g_rope = sb("g_rope", [P, 2, ROPE])
        w_rout = sb("w_rout", [P, KM, NG + NE])
        b_rout = sb("b_rout", [P, NG + NE])
        eps_col = sb("eps_col", [P, 1])
        st = sb("st", [P, 256])

        ARENA = 23480
        arena = sb("arena", [P, ARENA + 1032])
        at = [0]

        def carve(*shape, parts=P, start=None):
            n = 1
            for s in shape:
                n *= s
            a = at[0] if start is None else start
            if start is None:
                at[0] = a + n
            v = arena[0:parts, a:a + n]
            if len(shape) == 1:
                return v
            names = "abcde"[:len(shape)]
            kw = {names[i]: shape[i] for i in range(len(shape))}
            return v.rearrange(f"p ({' '.join(names)}) -> p {' '.join(names)}", **kw)

        xn = carve(CH, KM, P)
        y = carve(CH, D, start=0)
        xT_at = at[0]
        xT = carve(KM, SEQ)
        moe_at = at[0]
        LP = [carve(768, start=xT_at), carve(768, start=xT_at + 768)]
        proj = carve(CH, PROJ)
        qT = carve(AH, SEQ, parts=HD)
        kT = carve(2, AKV, SEQ, parts=HD)
        sq_at = at[0]
        sq = carve(1536)
        nd = carve(2 * BH, HD + 1, start=sq_at)
        hB = carve(CH, BW, start=sq_at + 2 * BH * (HD + 1) + 8)
        kc = carve(CH, CHD, QK)
        qc = carve(CH, CHD, QK)
        vC = carve(CH, CHD, HD)
        conv_at = at[0]
        y_junk = carve(2, CH, AW, start=conv_at - 2 * CH * AW)
        conv_in = carve(4, CONV_K - 1 + SEQ)
        mq_at = at[0]
        qk = carve(4, SEQ)
        E2 = carve(BH, P)
        mk_at = at[0]
        E1 = carve(BH, SEQ)
        ebuf = arena[:, ARENA:ARENA + 4 * SEQ].rearrange("p (k n) -> p k n", k=4)
        v_aug = carve(CH, BH, HD + 1)
        mqT = carve(CHD, SEQ, parts=QK, start=mq_at)
        mkT = carve(CHD, SEQ, parts=QK, start=mk_at)
        assert at[0] - mk_at >= CHD * SEQ
        dqT = [carve(SEQ, parts=QRC, start=AW), carve(SEQ, parts=QRC, start=D + AW)]
        dkvT = carve(SEQ, start=AW + BW)
        pt_at = at[0]
        cmp_x = carve(2, 3, SEQ)
        PT = [carve(6, P, start=pt_at), carve(6, P, start=pt_at + 768)]
        eo = carve(CH, BW)
        gates = carve(CH, 3 * AH)
        hid_e = carve(2, 30, parts=HD)
        hid_b = carve(2, 30, parts=HD)
        hid_k = carve(30, parts=HD)
        hid_v = carve(90, parts=HD)
        ck = carve(HD, parts=30)
        kcT = carve(30, parts=HD)
        vblk = carve(AH, HD, parts=90)
        clog = carve(CH, AH, NCMP)
        cPT = carve(SEQ, parts=90)
        rowi, rowf, rowa, rowB, rowu, rowm, rownm = [carve(SEQ, parts=4, start=conv_at + SEQ * i) for i in range(7)]
        rowe = rownm
        tmpr = carve(4, CH * CHD * 16)
        arena_att = at[0]
        at[0] = moe_at
        xs = carve(KM, NSLOT + WIN)
        ysT = carve(KM, NSLOT + WIN)
        ys = carve(4, D, start=moe_at)
        S_at = at[0]
        S = carve(CH, NSLOT)
        tmpS = carve(CH, NSLOT)
        Cw = carve(CH, NSLOT)
        tmpC = carve(NSLOT)
        cwT = carve(4, SEQ, start=S_at)
        xw = [carve(KM, WIN) for _ in range(3)]
        sg = carve(FE // 2)
        h = carve(FE // 2)
        hT = carve(2, WIN)
        rl = carve(CH, NG + NE)
        pg = carve(CH, 8)
        m8 = carve(CH, 8)
        m8e = carve(CH, 8)
        elp = carve(CH, NE)
        els = carve(CH, 8)
        oh = carve(2, CH, NE)
        ind = carve(CH, NE)
        base = carve(CH, NE)
        cnt = carve(NE)
        offs = carve(NE)
        junk = carve(2 * CH, NE)
        jx = carve(NE)
        jlast = carve(NE)
        jfirst = carve(NE)
        jM = carve(NJOB, NE)
        jt = carve(NJOB, NE)
        jobs = carve(2 * NJOB + 2)
        extra_gu = carve(2, KM, FE)
        extra_dn = carve(2, D, start=0)
        assert at[0] <= ARENA + 1032 and arena_att <= ARENA, (at[0], arena_att)
        table_in = arena[0:33, ARENA:ARENA + AH]
        buckets = arena[0:33, ARENA + 8:ARENA + 520]
        bias_out = arena[0:AH, ARENA + 520:ARENA + 1032]
        i8g = sb("i8g", [P, CH, 8], U32)
        i8e = sb("i8e", [P, CH, 8], U32)
        offs_i = sb("offs_i", [1, NE], I32)
        jobs_i = sb("jobs_i", [1, 2 * NJOB + 2], I32)
        jobs_before = sb("jobs_before", [1, 1])
        pos_i = sb("pos_i", [P, CH], I32)

        PS = ctx.enter_context(nc.psum_tensor("PS", [P, 8, 512], F32))
        bias_rows = nc.dram_tensor("bias_rows", [AH, P, 513], F32, kind="Internal").ap()

        filled = [Signal(f"bank{b}_filled", PER_BANK[b]) for b in range(8)]
        evacuated = [Signal(f"bank{b}_evacuated", PER_BANK[b], credit=1) for b in range(8)]
        landed = [ctx.enter_context(nc.semaphore(f"slot{s}_landed")) for s in range(NSLOTS)]
        down_landed = [ctx.enter_context(nc.semaphore(f"slot{s}_down_landed")) for s in range(NSLOTS)]
        g1_loaded = ctx.enter_context(nc.semaphore("g1_loaded"))
        extra_landed = ctx.enter_context(nc.semaphore("extra_landed"))
        extra_down_landed = ctx.enter_context(nc.semaphore("extra_down_landed"))
        n_att_dmas, n_moe_dmas = 18, 5
        att_params = ctx.enter_context(nc.semaphore("att_params"))
        moe_params = ctx.enter_context(nc.semaphore("moe_params"))
        x_loaded = ctx.enter_context(nc.semaphore("x_loaded"))
        table_dma = ctx.enter_context(nc.semaphore("table_dma"))
        setup_dma = ctx.enter_context(nc.semaphore("setup_dma"))
        bias_dma = ctx.enter_context(nc.semaphore("bias_dma"))
        setup_mem = ctx.enter_context(nc.semaphore("setup_mem"))
        pe_setup = ctx.enter_context(nc.semaphore("pe_setup"))
        vec_setup = ctx.enter_context(nc.semaphore("vec_setup"))
        angles_ready = ctx.enter_context(nc.semaphore("angles_ready"))
        act_setup = ctx.enter_context(nc.semaphore("act_setup"))
        vec_step = ctx.enter_context(nc.semaphore("vec_step"))
        act_step = ctx.enter_context(nc.semaphore("act_step"))
        pool_step = ctx.enter_context(nc.semaphore("pool_step"))
        out_dma = ctx.enter_context(nc.semaphore("out_dma"))
        x_new = Signal("x_new", 2, credit=2)
        sums1 = Signal("sums1", 2)
        sums2 = Signal("sums2", 2)
        sumsy = Signal("sumsy", 2)
        sumsc = Signal("sumsc", 1)
        head_sums = {n: Signal(f"{n}_sums", 1) for n in ("mla", "nsa_q", "nsa_k", "cmp_k", "mlstm")}
        head_roots = {n: Signal(f"{n}_roots", 1) for n in ("mla", "nsa_q", "nsa_k", "cmp_k", "mlstm")}
        xn_ready = Signal("xn_ready", 4)
        gains = Signal("gains", 1)
        q_normed = Signal("q_normed", 1)
        k_normed = Signal("k_normed", 1)
        cmp_zero = Signal("cmp_zero", 1)
        gate_e = Signal("gate_e", 1)
        hid_pre = Signal("hid_pre", 1)
        hid_exp = Signal("hid_exp", 1)
        hid_ready = Signal("hid_ready", 1)
        ck_ready = Signal("ck_ready", 1)
        vblk_ready = Signal("vblk_ready", 1)
        clog_pre = Signal("clog_pre", 1)
        clog_exp = Signal("clog_exp", 1)
        conv_done = Signal("conv_done", 2)
        conv_exp = Signal("conv_exp", 2)
        qk_ready = Signal("qk_ready", 1)
        f_abs = Signal("f_abs", 1)
        f_log = Signal("f_log", 1)
        um_ready = Signal("um_ready", 1)
        um_cols = Signal("um_cols", 1)
        em_ready = Signal("em_ready", 1)
        e_pre = Signal("e_pre", 4)
        e_exp = Signal("e_exp", 8)
        g_ready = Signal("g_ready", 4)
        va_ready = Signal("va_ready", 1)
        eo_ready = Signal("eo_ready", 1)
        c_normed = Signal("c_normed", 1)
        mcat_ready = Signal("mcat_ready", 1)
        p_pre = Signal("p_pre", N_GROUPS_ATT)
        p_exp = Signal("p_exp", N_GROUPS_ATT)
        y_scaled = Signal("y_scaled", 2)
        y_all = Signal("y_all", 2)
        x_mid = Signal("x_mid", 2)
        ge_pre = Signal("ge_pre", 1)
        ge_exp = Signal("ge_exp", 1)
        e2_pre = Signal("e2_pre", 1)
        e2_exp = Signal("e2_exp", 1)
        ind_ready = Signal("ind_ready", 1)
        offs_ready = Signal("offs_ready", 1)
        w_ready = Signal("w_ready", 1)
        S_ready = Signal("S_ready", 2)
        cw_ready = Signal("cw_ready", 1)
        xs_pad = Signal("xs_pad", 1)
        xw_ready = Signal("xw_ready", NEX)
        gu_done = Signal("gu_done", NEX, credit=3)
        sg_ready = Signal("sg_ready", NEX)
        h_ready = Signal("h_ready", NEX, credit=1)
        hT_full = Signal("hT_full", NEX)
        hT_ready = Signal("hT_ready", NEX, credit=1)
        y_full = Signal("y_full", NEX, credit=2)
        y_stored = Signal("y_stored", NEX, credit=3)
        jobs_made = Signal("jobs_made", 1)
        slot_left = Signal("slot_left", 1, credit=1)
        job = {n: Signal(f"job_{n}", 0, credit=c) for n, c in
               (("gu_landed", 0), ("dn_landed", 0), ("xw_ready", 0), ("gu_done", 1), ("sg_ready", 0), ("h_ready", 1),
                ("hT_full", 0), ("hT_ready", 0), ("y_full", 1), ("y_stored", 1))}
        credited = [*evacuated, x_new, gu_done, h_ready, hT_ready, y_full, y_stored, slot_left, job["gu_done"], job["h_ready"],
                    job["y_full"], job["y_stored"]]


        def is_filled(lay, use):
            b, k = USE[use]
            return filled[b].sem, filled[b].at(lay, k)

        def is_evacuated(lay, use):
            b, k = USE[use]
            return evacuated[b].sem, evacuated[b].at(lay, k)

        def is_free(lay, use):
            b, k = USE[use]
            return evacuated[b].sem, evacuated[b].at(lay, k - 1)

        def bank(use):
            return PS[:, USE[use][0], :]

        def has_landed(lay, item, extra=0):
            s, v = landed_at(item)
            return landed[s], lay * LANDED_PER_LAYER[s] + v + extra

        def job_counts(eng):
            return (eng.value_load(jobs_i[0:1, 2 * NJOB:2 * NJOB + 1], min_val=1, max_val=NJOB),
                    eng.value_load(jobs_i[0:1, 2 * NJOB + 1:2 * NJOB + 2], min_val=0, max_val=NJOB * DEPTH))

        def job_entry(eng, column, it, most):
            return eng.value_load(jobs_i[0:1, bass.ds(it + column * NJOB, 1)], min_val=0, max_val=most)

        def wait_job(eng, name, g, unit=1):
            eng.wait_ge(job[name].sem, g * unit + job[name].credit)

        def w_in_view(item):
            a, b = W_IN_ITEMS[item]
            return ring[:, item % NSLOTS, 0:KM * (b - a)].rearrange("p (m n) -> p m n", m=KM)

        w_cmp1 = ring[:, 2, KM * 512:KM * 512 + 2 * 16 * HD].rearrange("p (s j f) -> p s j f", s=2, j=16)

        def w_out_view(half):
            return ring[:, (5 + half) % NSLOTS, 0:KM * 512].rearrange("p (m n) -> p m n", m=KM)

        def w_gu(s):
            return ring[:, s, 0:KM * 2 * FE].rearrange("p (g m f) -> p g m f", g=2, m=KM)

        def w_dn(s):
            return ring[:, s, KM * 2 * FE:SLOT].rearrange("p (f d) -> p f d", f=2)

        SETUP_LOADS = 3
        PHASE_SETUP = 16 * SETUP_LOADS

        def att_load(eng, l):
            def go(dst, src):
                eng.dma_start(dst, src, allow_slow_non_contiguous=True).then_inc(att_params, 16)
            go(gq[:, :], t["nsa_q_norm"].unsqueeze(2)[l])
            go(gk[:, :], t["nsa_k_norm"].unsqueeze(2)[l])
            go(rows[0:16, :], t["mlstm_conv"].rearrange("l j (k c) -> l (j k) c", c=P)[l])
            go(rows[16:48, :], t["nsa_cmp_pe"].rearrange("l s (j b) d -> l (s j) (b d)", b=2)[l])
            go(w_cmp2[:, :, :], t["nsa_cmp_w2"].rearrange("l s f d -> l f s d")[l])
            go(if_bias[:, 0:1], t["mlstm_i_bias"].unsqueeze(2)[l])
            go(if_bias[:, 1:2], t["mlstm_f_bias"].unsqueeze(2)[l])
            go(g_qa[:, :], t["mla_q_a_norm"].rearrange("l (k p) -> l p k", k=2)[l])
            go(g_kva[:, :], t["mla_kv_a_norm"].unsqueeze(2)[l])
            qk_norm = t["mla_qk_norm"].unsqueeze(3)
            go(g_mq[0:NOPE, :], qk_norm[l][0, 0:NOPE])
            go(g_mk[0:NOPE, :], qk_norm[l][1, 0:NOPE])
            for s in range(2):
                go(g_rope[:, s, :], t["mla_qk_norm"].unsqueeze(1)[l][:, s, NOPE:QK].broadcast_to([P, ROPE]))
            go(gy[0:48, :], t["nsa_out_norm"].rearrange("l (p m) -> l p m", m=KM)[l])
            go(gy[48:80, :], t["mlstm_out_norm"].rearrange("l (p m) -> l p m", m=KM)[l])
            go(gy[80:128, :], t["mla_out_norm"].rearrange("l (p m) -> l p m", m=KM)[l])
            go(w_uq[:, :, :], t["mla_w_uq"].rearrange("l (k p) n -> l p k n", k=2)[l])
            go(w_ukv[:, :], t["mla_w_ukv"][l])

        def moe_load(eng, l):
            def go(dst, src):
                eng.dma_start(dst, src, allow_slow_non_contiguous=True).then_inc(moe_params, 16)
            go(g2[:, :], t["norm2_g"].rearrange("l (p m) -> l p m", m=KM)[l])
            go(w_rout[:, :, 0:NG], t["moe_w_group"].rearrange("l (p m) n -> l p m n", m=KM)[l])
            go(w_rout[:, :, NG:], t["moe_w_expert"].rearrange("l (p m) n -> l p m n", m=KM)[l])
            go(b_rout[:, 0:NG], t["moe_b_group"].unsqueeze(1)[l].broadcast_to([P, NG]))
            go(b_rout[:, NG:], t["moe_b_expert"].unsqueeze(1)[l].broadcast_to([P, NE]))

        block = ctx.enter_context(nc.Block())

        @block.sync
        def _(sp):
            sp.dma_start(pos_i[:, :], positions.rearrange("b (c p) -> p (b c)", c=CH),
                         allow_slow_non_contiguous=True).then_inc(setup_dma, 16)
            sp.dma_start(cst[:, :], t["c128"]).then_inc(setup_dma, 16)
            sp.dma_start(sel4[:, :], t["c4"]).then_inc(setup_dma, 16)
            sp.dma_start(x[:, :, :], x_in.rearrange("b (c p) d -> p (b c) d", c=CH)).then_inc(x_loaded, 16)
            sp.dma_start(table_in[0:32], rel_bias).then_inc(table_dma, 16)
            sp.dma_start(buckets, t["c33"]).then_inc(table_dma, 16)

            def load_gate_up(q, to, landing):
                for k, name in enumerate(("moe_w_gate", "moe_w_up")):
                    sp.dma_start(to[:, k], t[name].rearrange("l e (p m) f -> (l e) p m f", m=KM)[q]).then_inc(landing, 16)

            def load_down(q, to, landing):
                sp.dma_start(to, t["moe_w_down"].rearrange("l e (m p) d -> (l e) p m d", m=2)[q]).then_inc(landing, 16)

            def load_expert(lay, e, s, before):
                sp.wait_ge(gu_done.sem, gu_done.at(lay, before + 1))
                load_gate_up(lay * NE + e, w_gu(s), landed[s])
                sp.wait_ge(y_full.sem, y_full.at(lay, before + 1))
                load_down(lay * NE + e, w_dn(s), down_landed[s])

            with sp.Fori(0, DEPTH) as lay:
                used = [(y_full.sem, y_full.at(lay, 0)), (slot_left.sem, slot_left.at(lay, 0)),
                        (y_full.sem, y_full.at(lay, -1)),
                        is_filled(lay, "T3c1"), is_filled(lay, "T4c1")]
                sp.wait_ge(y_full.sem, y_full.at(lay, -1))
                settle(sp)
                sp.dma_start(g1[:, :], t["norm1_g"].rearrange("l (p m) -> l p m", m=KM)[lay]).then_inc(g1_loaded, 16)
                for i, (a, b) in enumerate(W_IN_ITEMS):
                    sp.wait_ge(*used[i])
                    settle(sp)
                    src = t["w_in"].rearrange("l (p m) n -> l p m n", m=KM)[lay][:, :, a:b]
                    sp.dma_start(w_in_view(i), src).then_inc(landed[i % NSLOTS], 16)
                    if i == 0:
                        att_load(sp, lay)
                    if i == 2:
                        src = t["nsa_cmp_w1"].rearrange("l s (j b) d f -> l s (b d) j f", b=2)[lay]
                        for k in range(2):
                            sp.dma_start(w_cmp1[:, k], src[k]).then_inc(landed[2], 16)
                moe_load(sp, lay)
                for half in range(2):
                    sp.wait_ge(*is_filled(lay, ["hid", "T1b"][half]))
                    src = t["w_out"].rearrange("l (p m) n -> l p m n", m=KM)[lay][:, :, 512 * half:512 * half + 512]
                    sp.dma_start(w_out_view(half), src).then_inc(landed[(5 + half) % NSLOTS], 16)
                for e, use in enumerate(["F23", "wo10", "wo11"]):
                    sp.wait_ge(*is_filled(lay, use))
                    load_gate_up(lay * NE + e, w_gu((E0 + e) % NSLOTS), landed[(E0 + e) % NSLOTS])
                    load_down(lay * NE + e, w_dn((E0 + e) % NSLOTS), down_landed[(E0 + e) % NSLOTS])
                load_gate_up(lay * NE + EXTRA, extra_gu, extra_landed)
                sp.wait_ge(*is_filled(lay, "xs7"))
                settle(sp)
                load_down(lay * NE + EXTRA, extra_dn, extra_down_landed)
                for e in (4, 5, 6):
                    load_expert(lay, e, (E0 + e - 1) % NSLOTS, e - 4)
                with sp.Fori(0, (NEX - 7) // 3) as it:
                    for u in range(3):
                        e = it * 3 + (7 + u)
                        load_expert(lay, e, (E0 + 6 + u) % NSLOTS, e - 3)
                sp.wait_ge(jobs_made.sem, jobs_made.at(lay, 1))
                settle(sp)
                sp.wait_ge(y_full.sem, y_full.at(lay, NEX - 2))
                settle(sp)
                n_jobs, before = job_counts(sp)
                with sp.Fori(0, n_jobs) as it:
                    q = lay * NE + job_entry(sp, 1, it, NE - 1)
                    wait_job(sp, "gu_done", before + it)
                    load_gate_up(q, w_gu(JOB_SLOT), job["gu_landed"].sem)
                    wait_job(sp, "y_full", before + it)
                    load_down(q, w_dn(JOB_SLOT), job["dn_landed"].sem)
            sp.wait_ge(x_new.sem, x_new.at(DEPTH - 1, 2))
            sp.dma_start(out.rearrange("b (c p) d -> p (b c) d", c=CH), x[:, :, :]).then_inc(out_dma, 16)
            sp.wait_ge(out_dma, 16)

        @block.gpsimd
        def _(pool):
            for s in credited:
                pool.sem_inc(s.sem, s.credit)
            n = [0]

            def link(ins):
                n[0] += 1
                ins.then_inc(pool_step, 1)
                pool.wait_ge(pool_step, n[0])

            for i, (dst, value) in enumerate(((ones[:, :], 1.0), (eps_col[:, :], EPS), (g_mq[NOPE:QK, :], 1.0),
                                              (g_mk[NOPE:QK, :], 1.0), (table_in[32:33], 1.0))):
                pool.memset(dst, value).then_inc(setup_mem, 1)
                pool.wait_ge(setup_mem, i + 1)
            pool.wait_ge(vec_setup, 1)
            pool.wait_ge(landed[1], 16)
            pool.dma_start(bias_rows[:, :, 0:512], bias_out.unsqueeze(1).broadcast_to([AH, P, 512])).then_inc(bias_dma, 16)
            pool.wait_ge(bias_dma, 16)
            skew = bass.AP(tensor=bias_rows.tensor, offset=P - 1, ap=[[512, P], [P * 513, AH], [1, BIASW]])
            pool.dma_start(bias_t[:, :, :], skew).then_inc(bias_dma, 16)

            with pool.Fori(0, DEPTH) as lay:
                pool.sem_clear(pool_step)
                n[0] = 0
                pool.wait_ge(xn_ready.sem, xn_ready.at(lay, 2))
                settle(pool)
                link(pool.memset(v_aug[:, :, :, HD:HD + 1], 1.0))
                link(pool.memset(cmp_x[:, :, 2, :], 0.0))
                pool.sem_inc(cmp_zero.sem, 1)
                pool.wait_ge(*is_filled(lay, "mB1"))
                settle(pool)
                link(pool.memset(conv_in[:, :, 0:CONV_K - 1], 0.0))
                pool.wait_ge(*is_evacuated(lay, "params"))
                for i in range(2):
                    pool.wait_ge(*is_evacuated(lay, ["F01", "F23"][i]))
                    settle(pool)
                    tap = ebuf[:, 2 * i:2 * i + 2]
                    both = qk[:, 2 * i:2 * i + 2, :]
                    for j in range(CONV_K):
                        for k in range(2):
                            w = cols[:, 4 * j + 2 * i + k:4 * j + 2 * i + k + 1]
                            link(pool.tensor_scalar((both if j == 0 else tap)[:, k, :], conv_in[:, 2 * i + k, j:j + SEQ], w,
                                                    None, ALU.mult))
                        if j > 0:
                            link(pool.tensor_tensor(both, both, tap, ALU.add))
                    pool.sem_inc(conv_done.sem, 1)
                pool.wait_ge(xn_ready.sem, xn_ready.at(lay, 4))
                settle(pool)
                link(pool.memset(xs[:, :, NSLOT:], 0.0))
                pool.memset(ysT[:, :, NSLOT:], 0.0).then_inc(xs_pad.sem, 1)
                pool.wait_ge(w_ready.sem, w_ready.at(lay, 1))
                settle(pool)
                for c in range(CH):
                    link(pool.tensor_scalar(tmpC, const("iota"), st[:, 128 + 2 * c:129 + 2 * c],
                                            st[:, 132 + 2 * c:133 + 2 * c], ALU.is_equal, ALU.mult))
                    link(pool.tensor_scalar(Cw[:, c, :], const("iota"), st[:, 129 + 2 * c:130 + 2 * c],
                                            st[:, 133 + 2 * c:134 + 2 * c], ALU.is_equal, ALU.mult))
                    ins = pool.tensor_tensor(Cw[:, c, :], Cw[:, c, :], tmpC, ALU.add)
                    if c == 0:
                        link(ins)
                    else:
                        ins.then_inc(cw_ready.sem, 1)

        @block.tensor
        def _(pe):
            pe.wait_ge(table_dma, 32)
            pe.wait_ge(setup_mem, 5)
            pe.matmul(PS[0:AH, 0, :], table_in, buckets, start=True, stop=True).then_inc(pe_setup, 1)
            pe.wait_ge(setup_dma, PHASE_SETUP)
            pe.wait_ge(vec_setup, 1)

            with pe.Fori(0, DEPTH) as lay:
                def free(use):
                    pe.wait_ge(*is_free(lay, use))

                def fill(ins, use):
                    ins.then_inc(filled[USE[use][0]].sem, 1)

                def turn_tokens(prefix):
                    for i in range(4):
                        use = f"{prefix}{i}"
                        free(use)
                        for k in range(2):
                            for c in range(CH):
                                a = k * SEQ + c * P
                                m = pe.transpose(bank(use)[:, a:a + P], xn[:, c, 2 * i + k, :], ident)
                        fill(m, use)

                pe.wait_ge(xn_ready.sem, xn_ready.at(lay, 2))
                turn_tokens("xT")
                for i in range(4):
                    pe.wait_ge(*is_evacuated(lay, f"xT{i}"))

                def project(use, item, a, b, c, at0=0):
                    w = w_in_view(item)
                    o = W_IN_ITEMS[item][0]
                    for m in range(KM):
                        ins = pe.matmul(bank(use)[:, at0:at0 + b - a], xT[:, m, c * P:(c + 1) * P],
                                        w[:, m, a - o:b - o], start=(m == 0), stop=(m == KM - 1))
                    return ins

                def project_chunk(use, item, a, b, c):
                    free(use)
                    fill(project(use, item, a, b, c), use)

                def project_features(use, i):
                    free(use)
                    for k in range(2):
                        for m in range(KM):
                            ins = pe.matmul(bank(use)[:, k * SEQ:(k + 1) * SEQ],
                                            w_in_view(4)[:, m, (2 * i + k) * P:(2 * i + k + 1) * P], xT[:, m, :],
                                            start=(m == 0), stop=(m == KM - 1))
                    fill(ins, use)

                pe.wait_ge(*has_landed(lay, 0))
                for c in range(CH):
                    project_chunk(f"T3c{c}", 0, C_BV, 2194, c)
                pe.wait_ge(*has_landed(lay, 1))
                for c in range(CH):
                    project_chunk(f"T4c{c}", 1, 2194, 2554, c)
                pe.wait_ge(*has_landed(lay, 2))
                project_chunk("T0c0", 2, 0, 512, 0)
                pe.wait_ge(c_normed.sem, c_normed.at(lay, 1))
                free("dqT")
                for k in range(2):
                    for c in range(CH):
                        m = pe.transpose(bank("dqT")[0:QRC, k * SEQ + c * P:k * SEQ + (c + 1) * P],
                                         proj[:, c, O_DQ + k * QRC:O_DQ + (k + 1) * QRC], ident)
                fill(m, "dqT")
                free("dkvT")
                for c in range(CH):
                    m = pe.transpose(bank("dkvT")[:, c * P:(c + 1) * P], proj[:, c, O_DKV:O_DKV + KVR], ident)
                fill(m, "dkvT")
                free("ifT")
                settle(pe)
                for g in range(2):
                    for c in range(CH):
                        m = pe.transpose(bank("ifT")[0:4, g * SEQ + c * P:g * SEQ + (c + 1) * P],
                                         proj[:, c, O_IF + 4 * g:O_IF + 4 * g + 4], ident)
                fill(m, "ifT")

                free("params")
                pe.wait_ge(att_params, (lay + 1) * (16 * n_att_dmas))
                settle(pe)
                fill(pe.transpose(bank("params")[:, 0:48], rows[:, :], ident[0:48, 0:48]), "params")
                project_chunk("T0c1", 2, 0, 512, 1)
                pe.wait_ge(*is_evacuated(lay, "dqT"))
                for c in range(CH):
                    for k in range(2):
                        use = f"uq{c}{k}"
                        free(use)
                        for r in range(2):
                            m = pe.matmul(bank(use)[:, 0:3 * QK], dqT[r][:, c * P:(c + 1) * P],
                                          w_uq[:, r, k * 3 * QK:(k + 1) * 3 * QK], start=(r == 0), stop=(r == 1))
                        fill(m, use)
                pe.wait_ge(*is_evacuated(lay, "dkvT"))
                for c in range(CH):
                    for k in range(2):
                        use = f"ukv{c}{k}"
                        free(use)
                        fill(pe.matmul(bank(use)[:, 0:3 * P], dkvT[:, c * P:(c + 1) * P],
                                       w_ukv[:, k * 3 * P:(k + 1) * 3 * P], start=True, stop=True), use)
                pe.wait_ge(um_ready.sem, um_ready.at(lay, 1))
                free("umT")
                settle(pe)
                for c in range(CH):
                    for k, row in enumerate((rowu, rowm)):
                        m = pe.transpose(bank("umT")[:, (2 * c + k) * 4:(2 * c + k + 1) * 4],
                                         row[:, c * P:(c + 1) * P], ident[0:4, 0:4])
                fill(m, "umT")
                for i in range(2):
                    free(f"mB{i}")
                    for k in range(2):
                        hh = 2 * i + k
                        m = pe.matmul(bank(f"mB{i}")[:, k * SEQ:(k + 1) * SEQ], sel4[:, hh * P:(hh + 1) * P],
                                      rownm, start=True, stop=True)
                    fill(m, f"mB{i}")
                pe.wait_ge(*has_landed(lay, 3))
                for c in range(CH):
                    project_chunk(f"T1ac{c}", 3, 512, 1024, c)
                free("T1b")
                for c in range(CH):
                    m = project("T1b", 3, 1024, C_BQK, c, at0=c * (C_BQK - 1024))
                fill(m, "T1b")
                for use in ("T0c0", "T0c1", "T1ac0", "T1ac1"):
                    pe.wait_ge(*is_evacuated(lay, use))
                for s in range(2):
                    free(f"cmp{s}")
                    settle(pe)
                    for k in range(AKV):
                        for c in range(CH):
                            a = C_KV + s * 128 + k * HD
                            m = pe.transpose(bank(f"cmp{s}")[0:HD, k * SEQ + c * P:k * SEQ + (c + 1) * P],
                                             proj[:, c, a:a + HD], ident)
                    fill(m, f"cmp{s}")
                pe.wait_ge(*has_landed(lay, 4))
                project_features("F01", 0)
                for s in range(2):
                    pe.wait_ge(*is_evacuated(lay, f"cmp{s}"))
                pe.wait_ge(*is_evacuated(lay, "params"))
                free("hid")
                for s in range(2):
                    for j in range(16):
                        rhs = cmp_x[:, s, :, 2 * j:2 * j + CMP_S * (NCMP - 1) + 1:CMP_S]
                        m = pe.matmul(bank("hid")[0:HD, 64 * s:64 * s + 3 * NCMP], w_cmp1[:, s, j, :], rhs,
                                      start=(j == 0), stop=(j == 15))
                fill(m, "hid")
                pe.wait_ge(q_normed.sem, q_normed.at(lay, 1))
                for i in range(3):
                    free(f"qT{i}")
                    settle(pe)
                    for k in range(2):
                        for c in range(CH):
                            hh = 2 * i + k
                            m = pe.transpose(bank(f"qT{i}")[0:HD, k * SEQ + c * P:k * SEQ + (c + 1) * P],
                                             proj[:, c, hh * HD:(hh + 1) * HD], ident)
                    fill(m, f"qT{i}")
                pe.wait_ge(k_normed.sem, k_normed.at(lay, 1))
                for b in range(2):
                    free(f"kT{b}")
                    settle(pe)
                    for k in range(AKV):
                        for c in range(CH):
                            a = C_KV + (b + 1) * 256 + k * HD
                            m = pe.transpose(bank(f"kT{b}")[0:HD, k * SEQ + c * P:k * SEQ + (c + 1) * P],
                                             proj[:, c, a:a + HD], ident)
                    fill(m, f"kT{b}")
                project_features("F23", 1)
                pe.wait_ge(hid_ready.sem, hid_ready.at(lay, 1))
                free("comp")
                settle(pe)
                pe.matmul(bank("comp")[0:30, 0:HD], hid_k, w_cmp2[:, 0, :], start=True, stop=True)
                fill(pe.matmul(bank("comp")[0:90, HD:2 * HD], hid_v, w_cmp2[:, 1, :], start=True, stop=True), "comp")

                def filler(use):
                    if use == "kcT":
                        pe.wait_ge(ck_ready.sem, ck_ready.at(lay, 1))
                        free(use)
                        settle(pe)
                        m = pe.transpose(bank(use)[0:HD, 0:30], ck, ident[0:30, 0:30])
                    elif use == "clog":
                        for u in ("qT0", "qT1", "qT2", "kcT"):
                            pe.wait_ge(*is_evacuated(lay, u))
                        free(use)
                        for c in range(CH):
                            for hh in range(AH):
                                a = (c * AH + hh) * NCMP
                                m = pe.matmul(bank(use)[:, a:a + NCMP], qT[:, hh, c * P:(c + 1) * P],
                                              kcT[:, (hh // AG) * NCMP:(hh // AG + 1) * NCMP], start=True, stop=True)
                    elif use == "cPT":
                        pe.wait_ge(clog_exp.sem, clog_exp.at(lay, 1))
                        free(use)
                        for c in range(CH):
                            m = pe.transpose(bank(use)[0:90, c * P:(c + 1) * P],
                                             clog[:, c].rearrange("p h n -> p (h n)"), ident)
                    elif use in ("cO0", "cO1"):
                        c = int(use[2])
                        pe.wait_ge(*is_evacuated(lay, "cPT"))
                        pe.wait_ge(vblk_ready.sem, vblk_ready.at(lay, 1))
                        free(use)
                        m = pe.matmul(bank(use)[:, 0:AW], cPT[:, c * P:(c + 1) * P],
                                      vblk.rearrange("p h d -> p (h d)"), start=True, stop=True)
                    elif use[:2] == "SS":
                        j, o = int(use[2]) // 2, HD * (int(use[2]) % 2)
                        n = SEQ - j * P
                        pe.wait_ge(qk_ready.sem, qk_ready.at(lay, 1))
                        free(use)
                        for k in range(2):
                            m = pe.matmul(bank(use)[:, k * n:(k + 1) * n], qk[o:o + HD, 2 + k, j * P:(j + 1) * P],
                                          qk[o:o + HD, k, j * P:SEQ], start=True, stop=True)
                    elif use[:3] == "num":
                        c = int(use[3])
                        pe.wait_ge(g_ready.sem, g_ready.at(lay, 4))
                        pe.wait_ge(va_ready.sem, va_ready.at(lay, 1))
                        free(use)
                        for hh in range(BH):
                            o = bank(use)[:, hh * (HD + 1):(hh + 1) * (HD + 1)]
                            m = pe.matmul(o, E1[:, hh, c * P:(c + 1) * P], v_aug[:, 0, hh, :], start=True, stop=(c == 0))
                            if c == 1:
                                m = pe.matmul(o, E2[:, hh, :], v_aug[:, 1, hh, :], start=False, stop=True)
                    else:
                        src, i = {"mq": qc, "mk": kc}[use[:2]], int(use[2])
                        pe.wait_ge(mcat_ready.sem, mcat_ready.at(lay, 1))
                        free(use)
                        for k in range(2):
                            for c in range(CH):
                                m = pe.transpose(bank(use)[0:QK, k * SEQ + c * P:k * SEQ + (c + 1) * P],
                                                 src[:, c, 2 * i + k, :], ident)
                    fill(m, use)

                def operands(g, k):
                    hh = 2 * (g % 3) + k
                    if g < 6:
                        b = g // 3
                        return qT[:, hh, :], kT[:, b, hh // AG, :]
                    return mqT[:, hh, :], mkT[:, hh, :]

                def values(g, k, c):
                    hh = 2 * (g % 3) + k
                    if g < 6:
                        a = C_KV + (g // 3 + 1) * 256 + 128 + (hh // AG) * HD
                        return proj[:, c, a:a + HD]
                    return vC[:, c, hh, :]

                def logits(g):
                    if g == 0:
                        for use in ("kT0", "kT1"):
                            pe.wait_ge(*is_evacuated(lay, use))
                    if g == 6:
                        pe.wait_ge(*is_evacuated(lay, "mk2"))
                    for c, use in enumerate((f"LA{g}", f"LB{g}")):
                        free(use)
                        n = (c + 1) * P
                        for k in range(2):
                            q, kk = operands(g, k)
                            m = pe.matmul(bank(use)[:, k * n:(k + 1) * n], q[:, c * P:(c + 1) * P], kk[:, 0:n],
                                          start=True, stop=True)
                        fill(m, use)

                def turn_weights(g):
                    pe.wait_ge(p_exp.sem, p_exp.at(lay, g + 1))
                    free(f"PA{g}")
                    for i in range(4):
                        m = pe.transpose(bank(f"PA{g}")[:, i * P:(i + 1) * P],
                                         LP[g % 2][:, 256 + i * P:256 + (i + 1) * P], ident)
                    fill(m, f"PA{g}")
                    free(f"PB{g}")
                    for i in range(2):
                        m = pe.transpose(bank(f"PB{g}")[:, i * P:(i + 1) * P], LP[g % 2][:, i * P:(i + 1) * P], ident)
                    fill(m, f"PB{g}")

                def weighted(g):
                    pe.wait_ge(*is_evacuated(lay, f"PA{g}"))
                    pe.wait_ge(*is_evacuated(lay, f"PB{g}"))
                    free(f"O{g}")
                    for c in range(CH):
                        for k in range(2):
                            o = bank(f"O{g}")[:, (c * 2 + k) * HD:(c * 2 + k + 1) * HD]
                            for s in range(c + 1):
                                i = 4 + k if c == 0 else 2 * k + s
                                m = pe.matmul(o, PT[g % 2][:, i, :], values(g, k, s), start=(s == 0), stop=(s == c))
                    fill(m, f"O{g}")

                for s in range(N_GROUPS_ATT + 2):
                    if s == 6:
                        for use in FILLERS[s][0]:
                            filler(use)
                    if s < N_GROUPS_ATT:
                        logits(s)
                    if s != 6:
                        for use in FILLERS[s][0]:
                            filler(use)
                    if 1 <= s <= N_GROUPS_ATT:
                        turn_weights(s - 1)
                    for use in FILLERS[s][1]:
                        filler(use)
                    if s >= 2:
                        weighted(s - 2)
                    for use in FILLERS[s][2]:
                        filler(use)

                pe.wait_ge(y_scaled.sem, y_scaled.at(lay, 2))
                for i in range(4):
                    free(f"yT{i}")
                    for k in range(2):
                        for c in range(CH):
                            mm = 2 * i + k
                            m = pe.transpose(bank(f"yT{i}")[:, k * SEQ + c * P:k * SEQ + (c + 1) * P],
                                             y[:, c, mm:D:KM], ident)
                    fill(m, f"yT{i}")
                for i in range(4):
                    pe.wait_ge(*is_evacuated(lay, f"yT{i}"))
                for half in range(2):
                    pe.wait_ge(*has_landed(lay, 5 + half))
                for c in range(CH):
                    for half in range(2):
                        use = f"wo{c}{half}"
                        free(use)
                        for m in range(KM):
                            ins = pe.matmul(bank(use), xT[:, m, c * P:(c + 1) * P], w_out_view(half)[:, m, :],
                                            start=(m == 0), stop=(m == KM - 1))
                        fill(ins, use)

                pe.wait_ge(xn_ready.sem, xn_ready.at(lay, 4))
                turn_tokens("nT")
                for i in range(4):
                    pe.wait_ge(*is_evacuated(lay, f"nT{i}"))
                pe.wait_ge(moe_params, (lay + 1) * (16 * n_moe_dmas))
                free("rout")
                for c in range(CH):
                    for m in range(KM):
                        ins = pe.matmul(bank("rout")[:, c * 36:(c + 1) * 36], xT[:, m, c * P:(c + 1) * P],
                                        w_rout[:, m, :], start=(m == 0), stop=(m == KM - 1))
                fill(ins, "rout")
                pe.wait_ge(ind_ready.sem, ind_ready.at(lay, 1))
                free("rank")
                o = bank("rank")
                pe.matmul(o[:, 0:NE], const("before"), ind[:, 0, :], start=True, stop=True)
                pe.matmul(o[:, NE:2 * NE], ones[:, :], ind[:, 0, :], start=True, stop=False)
                pe.matmul(o[:, NE:2 * NE], const("before"), ind[:, 1, :], start=False, stop=True)
                pe.matmul(o[:, 2 * NE:3 * NE], ones[:, :], ind[:, 0, :], start=True, stop=False)
                fill(pe.matmul(o[:, 2 * NE:3 * NE], ones[:, :], ind[:, 1, :], start=False, stop=True), "rank")
                pe.wait_ge(S_ready.sem, S_ready.at(lay, 2))
                for mm in range(KM):
                    free(f"xs{mm}")
                    for c in range(CH):
                        m = pe.matmul(bank(f"xs{mm}"), xn[:, c, mm, :], S[:, c, :], start=(c == 0), stop=(c == 1))
                    fill(m, f"xs{mm}")
                for mm in range(KM):
                    pe.wait_ge(*is_evacuated(lay, f"xs{mm}"))

                def gate_up(u, w, ms):
                    for m in ms:
                        for k in range(2):
                            ins = pe.matmul(PS[k * WIN:(k + 1) * WIN, u % 3, 0:FE], xw[u % 3][:, m, :],
                                            w[:, :, m, k * P:(k + 1) * P], start=(m == 0), stop=(m == KM - 1))
                    return ins

                def turn_h():
                    return pe.transpose(PS[:, 3, 0:P], h, ident)

                def down(u, w):
                    for mm in range(KM):
                        for f in range(2):
                            ins = pe.matmul(PS[:, 4 + u % 3, mm * WIN:(mm + 1) * WIN], w[:, f, mm * P:(mm + 1) * P],
                                            hT[:, f, :], start=(f == 0), stop=(f == 1))
                    return ins

                def gu_weights(e, turn=0):
                    if e == EXTRA:
                        pe.wait_ge(extra_landed, (lay + 1) * 32)
                        return extra_gu
                    item = E0 + e - (e > EXTRA)
                    pe.wait_ge(*has_landed(lay, item, turn * 32))
                    return w_gu(item % NSLOTS)

                def dn_weights(e, turn=0):
                    if e == EXTRA:
                        pe.wait_ge(extra_down_landed, (lay + 1) * 16)
                        return extra_dn
                    r = e - (e > EXTRA)
                    s = (E0 + r) % NSLOTS
                    pe.wait_ge(down_landed[s], lay * DOWN_PER_LAYER[s] + (turn + (r // NSLOTS + 1)) * 16)
                    return w_dn(s)

                def finish_turn(e):
                    pe.wait_ge(h_ready.sem, h_ready.at(lay, e + 1))
                    pe.wait_ge(hT_ready.sem, hT_ready.at(lay, e))
                    turn_h().then_inc(hT_full.sem, 1)

                def finish_down(e, e0, turn=0):
                    w = dn_weights(e0, turn)
                    pe.wait_ge(hT_ready.sem, hT_ready.at(lay, e + 1))
                    pe.wait_ge(y_stored.sem, y_stored.at(lay, e - 2))
                    down(e0, w).then_inc(y_full.sem, 1)

                def step(e, e0, turn=0):
                    pe.wait_ge(xw_ready.sem, xw_ready.at(lay, e + 1))
                    w = gu_weights(e0, turn)
                    gate_up(e0, w, range(KM // 2))
                    finish_turn(e - 1)
                    gate_up(e0, w, range(KM // 2, KM)).then_inc(gu_done.sem, 1)
                    finish_down(e - 1, e0 - 1, turn)

                pe.wait_ge(xw_ready.sem, xw_ready.at(lay, 1))
                gate_up(0, gu_weights(0), range(KM)).then_inc(gu_done.sem, 1)
                for e in range(1, 7):
                    step(e, e)
                with pe.Fori(0, (NEX - 7) // 3) as it:
                    for u in range(3):
                        step(it * 3 + (7 + u), 7 + u, it)
                finish_turn(NEX - 1)
                finish_down(NEX - 1, NEX - 1)
                pe.wait_ge(cw_ready.sem, cw_ready.at(lay, 1))
                for i in range(2):
                    free(f"cw{i}")
                    for k in range(2):
                        for c in range(CH):
                            s = 2 * i + k
                            m = pe.transpose(bank(f"cw{i}")[:, k * SEQ + c * P:k * SEQ + (c + 1) * P],
                                             Cw[:, c, s * P:(s + 1) * P], ident)
                    fill(m, f"cw{i}")
                pe.wait_ge(jobs_made.sem, jobs_made.at(lay, 1))
                pe.wait_ge(y_stored.sem, y_stored.at(lay, NEX - 2))
                pe.wait_ge(hT_ready.sem, hT_ready.at(lay, NEX))
                settle(pe)
                n_jobs, before = job_counts(pe)
                with pe.Fori(0, n_jobs) as it:
                    g = before + it
                    wait_job(pe, "xw_ready", g + 1)
                    wait_job(pe, "gu_landed", g + 1, 32)
                    gate_up(JOB, w_gu(JOB_SLOT), range(KM)).then_inc(job["gu_done"].sem, 1)
                    wait_job(pe, "h_ready", g + 1)
                    turn_h().then_inc(job["hT_full"].sem, 1)
                    wait_job(pe, "hT_ready", g + 1)
                    wait_job(pe, "dn_landed", g + 1, 16)
                    wait_job(pe, "y_stored", g)
                    down(JOB, w_dn(JOB_SLOT)).then_inc(job["y_full"].sem, 1)

                pe.wait_ge(y_stored.sem, y_stored.at(lay, NEX))
                wait_job(pe, "y_stored", before + n_jobs)
                pe.sem_inc(slot_left.sem, 1)
                for i in range(8):
                    s, k = i // 2, i % 2
                    free(f"ys{i}")
                    for j in range(4):
                        m = pe.transpose(bank(f"ys{i}")[:, j * P:(j + 1) * P],
                                         ysT[:, 4 * k + j, s * P:(s + 1) * P], ident)
                    fill(m, f"ys{i}")
                for i in range(2):
                    pe.wait_ge(*is_evacuated(lay, f"cw{i}"))
                for i in range(8):
                    pe.wait_ge(*is_evacuated(lay, f"ys{i}"))
                for c in range(CH):
                    for half in range(2):
                        use = f"fo{c}{half}"
                        free(use)
                        for s in range(4):
                            m = pe.matmul(bank(use), cwT[:, s, c * P:(c + 1) * P],
                                          ys[:, s, half * 512:(half + 1) * 512], start=(s == 0), stop=(s == 3))
                        fill(m, use)

        @block.scalar
        def _(act):
            act.preload_act_table_set("trig_and_small")
            act.wait_ge(setup_dma, PHASE_SETUP)
            act.wait_ge(angles_ready, 1)
            act.wait_ge(setup_mem, 5)
            act.activation(sinn[:, :, :], st[:, 64:96].rearrange("p (c f) -> p c f", c=CH), ACT.Sin).then_inc(act_setup, 1)
            act.activation(cosn[:, :, :], st[:, 96:128].rearrange("p (c f) -> p c f", c=CH), ACT.Sin).then_inc(act_setup, 1)

            with act.Fori(0, DEPTH) as lay:
                def evac(dst, src, use, last=True, **kw):
                    ins = act.activation(dst, src, ACT.Copy, **kw)
                    if last:
                        ins.then_inc(evacuated[USE[use][0]].sem, 1)

                def full(use):
                    act.wait_ge(*is_filled(lay, use))

                def square_sums(dst, src, to):
                    return act.activation(dst, src, ACT.Square, accum_out=to)

                steps = [0]

                def step(ins):
                    steps[0] += 1
                    ins.then_inc(act_step, 1)
                    act.wait_ge(act_step, steps[0])

                def sigmoid(dst, src, sig):
                    step(act.activation(dst, src, ACT.Exp, scale=-1.0))
                    step(act.activation(dst, dst, ACT.Ln, bias=1.0))
                    act.activation(dst, dst, ACT.Exp, scale=-1.0).then_inc(sig.sem, 1)

                def convolved(i):
                    act.wait_ge(conv_done.sem, conv_done.at(lay, i + 1))
                    sigmoid(ebuf[:, 2 * i:2 * i + 2], qk[:, 2 * i:2 * i + 2, :], conv_exp)

                def root(v, width, sig=None):
                    step(act.activation(v, v, ACT.Ln, bias=eps_col[0:v.shape[0], :], scale=1.0 / width))
                    ins = act.activation(v, v, ACT.Exp, scale=-0.5)
                    if sig is not None:
                        ins.then_inc(sig.sem, 1)

                act.sem_clear(act_step)
                act.preload_act_table_set("natural_log_exp_and_others")
                act.wait_ge(x_loaded, 16)
                for c in range(CH):
                    act.wait_ge(x_new.sem, x_new.at(lay, c - 1))
                    step(square_sums(y[:, c, :], x[:, c, :], st[:, c:c + 1]))
                    root(st[:, c:c + 1], D, sums1)
                act.wait_ge(g1_loaded, (lay + 1) * 16)
                for i in (0, 1):
                    full(f"xT{i}")
                    for k in range(2):
                        evac(xT[:, 2 * i + k, :], bank(f"xT{i}")[:, k * SEQ:(k + 1) * SEQ], f"xT{i}",
                             last=(k == 1), scale=g1[:, 2 * i + k:2 * i + k + 1])
                full("T3c0")
                evac(proj[:, 0, O_BV:O_BV + 512], bank("T3c0"), "T3c0")
                full("T4c0")
                evac(proj[:, 0, 1682:PROJ], bank("T4c0")[:, 0:360], "T4c0")
                for use in ("T3c0", "T3c1", "T4c0", "T4c1"):
                    act.wait_ge(*is_evacuated(lay, use))
                for i, (a, w) in enumerate(((O_DQ, QR), (O_DKV, KVR), (O_KR, ROPE))):
                    for c in range(CH):
                        ins = square_sums(kc[:, c, 0:w // 32, 32 * i:32 * i + 32],
                                          proj[:, c, a:a + w].rearrange("p (a b) -> p a b", b=32),
                                          st[:, 8 + 2 * i + c:9 + 2 * i + c])
                step(ins)
                for i, w in enumerate((QR, KVR, ROPE)):
                    root(st[:, 8 + 2 * i:10 + 2 * i], w, sumsc if i == 2 else None)
                for c in range(CH):
                    m = act.activation(v_aug[:, c, :, 0:HD], proj[:, c, O_BV:O_BV + BW].rearrange("p (h d) -> p h d", h=BH),
                                       ACT.Copy)
                m.then_inc(va_ready.sem, 1)
                sigmoid(eo[:, :, :], proj[:, :, O_O:O_O + BW], eo_ready)
                full("T0c0")
                evac(proj[:, 0, 0:512], bank("T0c0"), "T0c0")
                act.wait_ge(gains.sem, gains.at(lay, 1))
                full("dqT")
                for k in range(2):
                    evac(dqT[k], bank("dqT")[0:QRC, k * SEQ:(k + 1) * SEQ], "dqT", last=(k == 1), scale=g_qa[:, k:k + 1])
                act.wait_ge(f_abs.sem, f_abs.at(lay, 1))
                step(act.activation(rowe, rowa, ACT.Exp, scale=-1.0))
                act.activation(rowa, rowe, ACT.Ln, bias=1.0).then_inc(f_log.sem, 1)
                for c in range(CH):
                    full(f"uq{c}0")
                    evac(qc[:, c, 0:3, :], bank(f"uq{c}0")[:, 0:3 * QK].rearrange("p (h d) -> p h d", h=3), f"uq{c}0")
                for c in range(CH):
                    full(f"ukv{c}0")
                    src = bank(f"ukv{c}0")[:, 0:3 * P].rearrange("p (h d) -> p h d", h=3)
                    evac(kc[:, c, 0:3, 0:NOPE], src[:, :, 0:NOPE], f"ukv{c}0", last=False)
                    evac(vC[:, c, 0:3, :], src[:, :, NOPE:], f"ukv{c}0")
                act.wait_ge(um_cols.sem, um_cols.at(lay, 1))
                um = st[:, 16:32].rearrange("p (c k h) -> p c k h", c=CH, k=2)
                act.activation(st[:, 32:40].rearrange("p (c h) -> p c h", c=CH), um[:, :, 1, :], ACT.Exp, scale=-1.0)\
                    .then_inc(em_ready.sem, 1)
                for j, tile in enumerate((E1, E2)):
                    act.wait_ge(e_pre.sem, e_pre.at(lay, 2 + 2 * j))
                    for hh in range(BH):
                        act.activation(tile[:, hh, :], tile[:, hh, :], ACT.Exp, bias=um[:, j, 0, hh:hh + 1])\
                            .then_inc(e_exp.sem, 1)
                act.wait_ge(head_sums["mla"].sem, head_sums["mla"].at(lay, 1))
                root(st[:, 208:232], NOPE)
                root(st[:, 232:244], ROPE, head_roots["mla"])
                full("T1ac0")
                evac(proj[:, 0, 512:1024], bank("T1ac0"), "T1ac0")
                full("T1b")
                evac(proj[:, :, 1024:C_BQK], bank("T1b")[:, 0:292].rearrange("p (c n) -> p c n", c=CH), "T1b")
                act.wait_ge(*is_evacuated(lay, "T1b"))
                act.activation(gates[:, :, :], proj[:, :, C_GATE:C_GATE + 18], ACT.Exp, scale=-1.0).then_inc(gate_e.sem, 1)
                act.wait_ge(cmp_zero.sem, cmp_zero.at(lay, 1))
                full("cmp0")
                src = bank("cmp0").rearrange("p (k n) -> p k n", k=2)
                evac(cmp_x[0:HD, 0, 0:2, :], src[0:HD], "cmp0", last=False)
                evac(cmp_x[HD:P, 0, 0:2, 0:SEQ - 1], src[0:HD, :, 1:SEQ], "cmp0")
                act.wait_ge(head_sums["nsa_q"].sem, head_sums["nsa_q"].at(lay, 1))
                root(st[:, 72:84], HD, head_roots["nsa_q"])
                act.wait_ge(head_sums["nsa_k"].sem, head_sums["nsa_k"].at(lay, 1))
                root(st[:, 64:72], HD, head_roots["nsa_k"])
                full("F01")
                evac(conv_in[:, 0:2, 3:], bank("F01").rearrange("p (k n) -> p k n", k=2), "F01")
                act.wait_ge(hid_pre.sem, hid_pre.at(lay, 1))
                act.activation(hid_e[:, :, :], hid_b[:, :, :], ACT.Exp, scale=-1.0).then_inc(hid_exp.sem, 1)
                for i in (0, 1):
                    full(f"qT{i}")
                    evac(qT[:, 2 * i:2 * i + 2, :], bank(f"qT{i}")[0:HD, :].rearrange("p (k n) -> p k n", k=2), f"qT{i}",
                         scale=gqs[:, :])
                convolved(0)
                full("kT0")
                evac(kT[:, 0, :, :], bank("kT0")[0:HD, :].rearrange("p (k n) -> p k n", k=2), "kT0", scale=gk[:, :])
                act.wait_ge(head_sums["cmp_k"].sem, head_sums["cmp_k"].at(lay, 1))
                root(st[0:30, 4:5], HD, head_roots["cmp_k"])

                def between(s):
                    if s == 0:
                        act.wait_ge(clog_pre.sem, clog_pre.at(lay, 1))
                        act.activation(clog[:, :, :, :], clog[:, :, :, :], ACT.Exp).then_inc(clog_exp.sem, 1)
                        convolved(1)
                    if s == 1:
                        full("cPT")
                        evac(cPT, bank("cPT")[0:90, 0:SEQ], "cPT")
                    if s == 4:
                        full("mq0")
                        turned_q(0)
                        act.wait_ge(head_sums["mlstm"].sem, head_sums["mlstm"].at(lay, 1))
                        root(st[:, 84:92], HD, head_roots["mlstm"])
                        full("mq1")
                        turned_q(1)
                    if s == 5:
                        full("mq2")
                        turned_q(2)
                    if s == 8:
                        y_norm(0)

                def y_norm(i):
                    act.wait_ge(y_all.sem, y_all.at(lay, i + 1))
                    for c in range(CH):
                        ins = square_sums(y_junk[:, i, c, :], y[:, c, i * (AW + BW):i * (AW + BW) + AW],
                                          st[:, 40 + 2 * i + c:41 + 2 * i + c])
                    step(ins)
                    root(st[:, 40 + 2 * i:42 + 2 * i], AW, sumsy)

                def turned_q(i):
                    evac(mqT[:, 2 * i:2 * i + 2, :], bank(f"mq{i}")[0:QK, :].rearrange("p (k n) -> p k n", k=2), f"mq{i}",
                         scale=g_mqs[:, :])

                for g in range(N_GROUPS_ATT + 1):
                    if g < N_GROUPS_ATT:
                        act.wait_ge(p_pre.sem, p_pre.at(lay, g + 1))
                        for i in range(4):
                            c, k = i // 2, i % 2
                            a = k * P if c == 0 else 256 + k * SEQ
                            v = LP[g % 2][:, a:a + (c + 1) * P]
                            m = act.activation(v, v, ACT.Exp, bias=st[:, 160 + 4 * (g % 2) + i:161 + 4 * (g % 2) + i],
                                               accum_out=st[:, 176 + 4 * g + i:177 + 4 * g + i])
                        m.then_inc(p_exp.sem, 1)
                    if g >= 1:
                        full(f"PA{g - 1}")
                        evac(PT[(g - 1) % 2][:, 0:4, :], bank(f"PA{g - 1}").rearrange("p (i n) -> p i n", i=4),
                             f"PA{g - 1}")
                    between(g)
                y_norm(1)
                for i in (0, 1):
                    full(f"yT{i}")
                    for k in range(2):
                        evac(xT[:, 2 * i + k, :], bank(f"yT{i}")[:, k * SEQ:(k + 1) * SEQ], f"yT{i}",
                             last=(k == 1), scale=gy[:, 2 * i + k:2 * i + k + 1])
                for c in range(CH):
                    act.wait_ge(x_mid.sem, x_mid.at(lay, c + 1))
                    step(square_sums(y[:, c, :], x[:, c, :], st[:, c:c + 1]))
                    root(st[:, c:c + 1], D, sums2)
                act.wait_ge(moe_params, (lay + 1) * (16 * n_moe_dmas))
                for i in (0, 1):
                    full(f"nT{i}")
                    for k in range(2):
                        evac(xT[:, 2 * i + k, :], bank(f"nT{i}")[:, k * SEQ:(k + 1) * SEQ], f"nT{i}",
                             last=(k == 1), scale=g2[:, 2 * i + k:2 * i + k + 1])
                act.wait_ge(ge_pre.sem, ge_pre.at(lay, 1))
                act.activation(pg[:, :, 0:NG], pg[:, :, 0:NG], ACT.Exp).then_inc(ge_exp.sem, 1)
                act.wait_ge(e2_pre.sem, e2_pre.at(lay, 1))
                act.activation(st[:, 140:142], st[:, 138:140], ACT.Exp).then_inc(e2_exp.sem, 1)
                act.preload_act_table_set("silu_and_others")
                for mm in range(0, KM, 2):
                    full(f"xs{mm}")
                    evac(xs[:, mm, 0:NSLOT], bank(f"xs{mm}"), f"xs{mm}", scale=g2[:, mm:mm + 1])
                for mm in range(KM):
                    act.wait_ge(*is_evacuated(lay, f"xs{mm}"))
                act.wait_ge(xs_pad.sem, xs_pad.at(lay, 1))
                act.wait_ge(offs_ready.sem, offs_ready.at(lay, 1))

                def silu(u):
                    return act.activation(sg, PS[:, u % 3, 0:P], ACT.Silu)

                def copy_hT():
                    return act.activation(hT[:, :, :], PS[:, 3, 0:P].rearrange("p (f n) -> p f n", f=2), ACT.Copy)

                def window(e, u):
                    settle(act)
                    o = act.value_load(offs_i[0:1, bass.ds(e, 1)], min_val=0, max_val=NSLOT)
                    act.wait_ge(gu_done.sem, gu_done.at(lay, e - 2))
                    act.activation(xw[u % 3], xs[:, :, bass.ds(o, WIN)], ACT.Copy).then_inc(xw_ready.sem, 1)

                def gate(e, u):
                    act.wait_ge(gu_done.sem, gu_done.at(lay, e + 1))
                    act.wait_ge(h_ready.sem, h_ready.at(lay, e))
                    silu(u).then_inc(sg_ready.sem, 1)
                    act.wait_ge(hT_full.sem, hT_full.at(lay, e + 1))
                    act.wait_ge(y_full.sem, y_full.at(lay, e))
                    copy_hT().then_inc(hT_ready.sem, 1)

                window(0, 0)
                window(1, 1)
                with act.Fori(0, NEX // 3 - 1) as it:
                    for u in range(3):
                        gate(it * 3 + u, u)
                        window(it * 3 + (u + 2), u + 2)
                for e in range(NEX - 4, NEX):
                    gate(e, e)
                    if e + 2 < NEX:
                        window(e + 2, e + 2)
                full("cw0")
                evac(cwT[:, 0:2, :], bank("cw0").rearrange("p (k n) -> p k n", k=2), "cw0")
                act.wait_ge(jobs_made.sem, jobs_made.at(lay, 1))
                act.wait_ge(h_ready.sem, h_ready.at(lay, NEX))
                act.wait_ge(y_full.sem, y_full.at(lay, NEX))
                settle(act)
                n_jobs, before = job_counts(act)
                with act.Fori(0, n_jobs) as it:
                    g = before + it
                    o = job_entry(act, 0, it, NSLOT)
                    wait_job(act, "gu_done", g)
                    act.activation(xw[JOB], xs[:, :, bass.ds(o, WIN)], ACT.Copy).then_inc(job["xw_ready"].sem, 1)
                    wait_job(act, "gu_done", g + 1)
                    wait_job(act, "h_ready", g)
                    silu(JOB).then_inc(job["sg_ready"].sem, 1)
                    wait_job(act, "hT_full", g + 1)
                    wait_job(act, "y_full", g)
                    copy_hT().then_inc(job["hT_ready"].sem, 1)

                for i in range(0, 8, 2):
                    full(f"ys{i}")
                    evac(ys[:, i // 2, 0:512], bank(f"ys{i}"), f"ys{i}")

        @block.vector
        def _(dve):
            n = [0]

            def link(ins):
                n[0] += 1
                ins.then_inc(vec_step, 1)
                dve.wait_ge(vec_step, n[0])

            dve.memset(jobs_before[:, :], 0.0)
            TWO_PI = 6.283185307179586
            C1 = 6.28125
            C2 = 0.0019350051879882812
            C3 = TWO_PI - C1 - C2
            MAGIC = 12582912.0
            dve.wait_ge(setup_dma, PHASE_SETUP)
            posf, ang, kk = st[:, 0:2], st[:, 64:96], st[:, 96:128]
            link(dve.tensor_copy(posf, pos_i[:, :]))
            for c in range(CH):
                link(dve.tensor_scalar(ang[:, 16 * c:16 * c + 16], const("inv_freq"), posf[:, c:c + 1], None, ALU.mult))
            link(dve.tensor_scalar(kk, ang, 1.0 / TWO_PI, MAGIC, ALU.mult, ALU.add))
            link(dve.tensor_scalar(kk, kk, MAGIC, None, ALU.subtract))
            for cc in (C1, C2, C3):
                link(dve.scalar_tensor_tensor(ang, kk, -cc, ang, ALU.mult, ALU.add))
            link(dve.tensor_scalar(ang, ang, 3.1415925, -3.1415925, ALU.min, ALU.max))
            link(dve.tensor_scalar(kk, ang, 0.5, None, ALU.mult))
            dve.sem_inc(angles_ready, 1)
            dve.wait_ge(pe_setup, 1)
            dve.tensor_copy(bias_out, PS[0:AH, 0, :]).then_inc(vec_setup, 1)
            dve.wait_ge(act_setup, 2)
            cosf = cosn[:, :, :].rearrange("p c f -> p (c f)")
            link(dve.tensor_tensor(cosf, cosf, cosf, ALU.mult))
            link(dve.tensor_scalar(cosf, cosf, -2.0, 1.0, ALU.mult, ALU.add))

            def bc(ap, shape):
                return ap.unsqueeze(len(ap.shape)).broadcast_to(shape)

            with dve.Fori(0, DEPTH) as lay:
                dve.sem_clear(vec_step)
                n[0] = 0

                def full(use):
                    dve.wait_ge(*is_filled(lay, use))

                def release(ins, use):
                    ins.then_inc(evacuated[USE[use][0]].sem, 1)

                def normalise_tokens(sig):
                    for c in range(CH):
                        dve.wait_ge(sig.sem, sig.at(lay, c + 1))
                        dve.tensor_scalar(xn[:, c], x[:, c, :].rearrange("p (q m) -> p m q", m=KM), st[:, c:c + 1], None,
                                          ALU.mult).then_inc(xn_ready.sem, 1)

                normalise_tokens(sums1)
                dve.wait_ge(g1_loaded, (lay + 1) * 16)
                for i in (2, 3):
                    full(f"xT{i}")
                    for k in range(2):
                        ins = dve.tensor_scalar(xT[:, 2 * i + k, :], bank(f"xT{i}")[:, k * SEQ:(k + 1) * SEQ],
                                                g1[:, 2 * i + k:2 * i + k + 1], None, ALU.mult)
                    release(ins, f"xT{i}")
                dve.wait_ge(att_params, (lay + 1) * (16 * n_att_dmas))
                link(dve.tensor_scalar(gqs[:, :], gq[:, :], HD ** -0.5, None, ALU.mult))
                link(dve.tensor_scalar(g_mqs[:, :], g_mq[:, :], QK ** -0.5, None, ALU.mult))
                for s in range(2):
                    for k, (tab, g) in enumerate(((cosn, 0), (sinn, 1), (cosn, 1), (sinn, 0))):
                        gg = g_rope[:, s, 16 * g:16 * g + 16].unsqueeze(1).broadcast_to([P, CH, 16])
                        ins = dve.tensor_tensor(rot[:, s, k], tab[:, :, :], gg, ALU.mult)
                ins.then_inc(gains.sem, 1)
                full("T3c1")
                release(dve.tensor_copy(proj[:, 1, O_BV:O_BV + 512], bank("T3c1")), "T3c1")
                full("T4c1")
                release(dve.tensor_copy(proj[:, 1, 1682:PROJ], bank("T4c1")[:, 0:360]), "T4c1")
                dve.wait_ge(sumsc.sem, sumsc.at(lay, 1))
                for i, (a, w) in enumerate(((O_DQ, QR), (O_DKV, KVR), (O_KR, ROPE))):
                    v = proj[:, :, a:a + w]
                    ins = dve.tensor_tensor(v, v, bc(st[:, 8 + 2 * i:10 + 2 * i], [P, CH, w]), ALU.mult)
                ins.then_inc(c_normed.sem, 1)
                full("dkvT")
                release(dve.tensor_scalar(dkvT, bank("dkvT")[:, 0:SEQ], g_kva[:, :], None, ALU.mult), "dkvT")
                full("ifT")
                link(dve.tensor_scalar(rowf, bank("ifT")[0:4, SEQ:2 * SEQ], if_bias[:, 1:2], None, ALU.add))
                dve.scalar_tensor_tensor(rowa, rowf, -1.0, rowf, ALU.mult, ALU.max).then_inc(f_abs.sem, 1)
                release(dve.tensor_scalar(rowi, bank("ifT")[0:4, 0:SEQ], if_bias[:, 0:1], None, ALU.add), "ifT")
                full("params")
                link(dve.tensor_copy(cols[:, 0:16], bank("params")[:, 0:16]))
                dve.wait_ge(cmp_zero.sem, cmp_zero.at(lay, 1))
                release(dve.tensor_copy(cmp_x[:, :, 2, 0:32:2], bank("params")[:, 16:48].rearrange("p (s j) -> p s j", s=2)),
                        "params")
                full("T0c1")
                release(dve.tensor_copy(proj[:, 1, 0:512], bank("T0c1")), "T0c1")
                dve.wait_ge(f_log.sem, f_log.at(lay, 1))
                link(dve.scalar_tensor_tensor(rowf, rowf, 0.0, rowa, ALU.min, ALU.subtract))
                link(dve.tensor_tensor_scan(rowB, ones[0:4, 0:1].broadcast_to([4, SEQ]), rowf, 0.0, ALU.mult, ALU.add))
                link(dve.tensor_tensor(rowu, rowi, rowB, ALU.subtract))
                link(dve.tensor_tensor_scan(rowm, rowu, rowu, 0.0, ALU.max, ALU.max))
                link(dve.tensor_scalar(rownm, rowm, -1.0, None, ALU.mult))
                dve.tensor_tensor(rowm, rowm, rowB, ALU.add).then_inc(um_ready.sem, 1)
                for c in range(CH):
                    full(f"uq{c}1")
                    release(dve.tensor_copy(qc[:, c, 3:6, :],
                                            bank(f"uq{c}1")[:, 0:3 * QK].rearrange("p (h d) -> p h d", h=3)), f"uq{c}1")
                for c in range(CH):
                    full(f"ukv{c}1")
                    src = bank(f"ukv{c}1")[:, 0:3 * P].rearrange("p (h d) -> p h d", h=3)
                    dve.tensor_copy(kc[:, c, 3:6, 0:NOPE], src[:, :, 0:NOPE])
                    release(dve.tensor_copy(vC[:, c, 3:6, :], src[:, :, NOPE:]), f"ukv{c}1")
                for c in range(CH):
                    for k in range(2):
                        dve.wait_ge(*is_evacuated(lay, f"uq{c}{k}"))
                        dve.wait_ge(*is_evacuated(lay, f"ukv{c}{k}"))
                full("umT")
                ins = dve.tensor_copy(st[:, 16:32], bank("umT")[:, 0:16])
                release(ins, "umT")
                dve.wait_ge(*is_evacuated(lay, "umT"))
                dve.sem_inc(um_cols.sem, 1)
                for i in range(2):
                    full(f"mB{i}")
                    src = bank(f"mB{i}").rearrange("p (k n) -> p k n", k=2)
                    dve.tensor_tensor(E1[:, 2 * i:2 * i + 2, :], src,
                                      const("after").unsqueeze(1).broadcast_to([P, 2, SEQ]), ALU.add).then_inc(e_pre.sem, 1)
                for i in range(2):
                    src = bank(f"mB{i}").rearrange("p (k n) -> p k n", k=2)
                    ins = dve.tensor_tensor(E2[:, 2 * i:2 * i + 2, :], src[:, :, P:SEQ],
                                            const("after")[:, 0:P].unsqueeze(1).broadcast_to([P, 2, P]), ALU.add)
                    release(ins, f"mB{i}")
                    dve.wait_ge(*is_evacuated(lay, f"mB{i}"))
                    dve.sem_inc(e_pre.sem, 1)
                qf = qc.rearrange("p c h d -> p (c h) d")
                kf = kc.rearrange("p c h d -> p (c h) d")
                sqm = sq[:, 0:12 * QK].rearrange("p (a d) -> p a d", d=QK)
                rq, rk, rr = st[:, 208:220], st[:, 220:232], st[:, 232:244]
                link(dve.tensor_tensor(sqm, qf, qf, ALU.mult))
                link(dve.tensor_reduce(rq, sqm[:, :, 0:NOPE], AX.X, ALU.add))
                link(dve.tensor_reduce(rr, sqm[:, :, NOPE:], AX.X, ALU.add))
                link(dve.tensor_tensor(sqm[:, :, 0:NOPE], kf[:, :, 0:NOPE], kf[:, :, 0:NOPE], ALU.mult))
                link(dve.tensor_reduce(rk, sqm[:, :, 0:NOPE], AX.X, ALU.add))
                dve.sem_inc(head_sums["mla"].sem, 1)
                dve.wait_ge(head_roots["mla"].sem, head_roots["mla"].at(lay, 1))
                link(dve.tensor_tensor(qf[:, :, 0:NOPE], qf[:, :, 0:NOPE], bc(rq, [P, 12, NOPE]), ALU.mult))
                link(dve.tensor_tensor(qf[:, :, NOPE:], qf[:, :, NOPE:], bc(rr, [P, 12, ROPE]), ALU.mult))
                link(dve.tensor_tensor(kf[:, :, 0:NOPE], kf[:, :, 0:NOPE], bc(rk, [P, 12, NOPE]), ALU.mult))
                tm = [tmpr[:, i, :].rearrange("p (c h f) -> p c h f", c=CH, h=CHD) for i in range(4)]
                q1, q2 = qc[:, :, :, NOPE:NOPE + 16], qc[:, :, :, NOPE + 16:]
                for i, (src, tab) in enumerate(((q1, 0), (q2, 1), (q2, 2), (q1, 3))):
                    link(dve.tensor_tensor(tm[i], src, rot[:, 0, tab].unsqueeze(2).broadcast_to([P, CH, CHD, 16]), ALU.mult))
                link(dve.tensor_tensor(q1, tm[0], tm[1], ALU.subtract))
                link(dve.tensor_tensor(q2, tm[2], tm[3], ALU.add))
                k1, k2 = proj[:, :, O_KR:O_KR + 16], proj[:, :, O_KR + 16:O_KR + 32]
                tk = [tmpr[:, i, 0:CH * 16].rearrange("p (c f) -> p c f", c=CH) for i in range(4)]
                for i, (src, tab) in enumerate(((k1, 0), (k2, 1), (k2, 2), (k1, 3))):
                    link(dve.tensor_tensor(tk[i], src, rot[:, 1, tab], ALU.mult))
                tkb = [v.unsqueeze(2).broadcast_to([P, CH, CHD, 16]) for v in tk]
                link(dve.tensor_tensor(kc[:, :, :, NOPE:NOPE + 16], tkb[0], tkb[1], ALU.subtract))
                dve.tensor_tensor(kc[:, :, :, NOPE + 16:], tkb[2], tkb[3], ALU.add).then_inc(mcat_ready.sem, 1)
                full("T1ac1")
                release(dve.tensor_copy(proj[:, 1, 512:1024], bank("T1ac1")), "T1ac1")
                full("cmp1")
                src = bank("cmp1").rearrange("p (k n) -> p k n", k=2)
                dve.tensor_copy(cmp_x[0:HD, 1, 0:2, :], src[0:HD])
                release(dve.tensor_copy(cmp_x[HD:P, 1, 0:2, 0:SEQ - 1], src[0:HD, :, 1:SEQ]), "cmp1")
                for use in ("T0c0", "T0c1", "T1ac0", "T1ac1", "T1b"):
                    dve.wait_ge(*is_evacuated(lay, use))
                q4 = proj[:, :, 0:AW]
                sqq = sq[:, 0:2 * AW].rearrange("p (c n) -> p c n", c=CH)
                link(dve.tensor_tensor(sqq, q4, q4, ALU.mult))
                ssq = st[:, 72:84]
                link(dve.tensor_reduce(ssq, sq[:, 0:2 * AW].rearrange("p (a d) -> p a d", d=HD), AX.X, ALU.add))
                dve.sem_inc(head_sums["nsa_q"].sem, 1)
                qh = q4.rearrange("p c (h d) -> p c h d", h=AH)
                ks = [proj[:, c, C_KV + 256:C_KV + 768].rearrange("p (b n) -> p b n", b=2)[:, :, 0:128] for c in range(CH)]
                for c in range(CH):
                    link(dve.tensor_tensor(sq[:, 256 * c:256 * c + 256].rearrange("p (b n) -> p b n", b=2), ks[c], ks[c],
                                           ALU.mult))
                ss = st[:, 64:72]
                link(dve.tensor_reduce(ss, sq[:, 0:512].rearrange("p (a d) -> p a d", d=HD), AX.X, ALU.add))
                dve.sem_inc(head_sums["nsa_k"].sem, 1)
                dve.wait_ge(head_roots["nsa_q"].sem, head_roots["nsa_q"].at(lay, 1))
                dve.tensor_tensor(qh, qh, bc(ssq.rearrange("p (c h) -> p c h", c=CH), [P, CH, AH, HD]), ALU.mult)\
                    .then_inc(q_normed.sem, 1)
                dve.wait_ge(head_roots["nsa_k"].sem, head_roots["nsa_k"].at(lay, 1))
                for c in range(CH):
                    kv = ks[c].rearrange("p b (h d) -> p b h d", h=AKV)
                    ins = dve.tensor_tensor(kv, kv, bc(ss[:, 4 * c:4 * c + 4].rearrange("p (b h) -> p b h", b=2),
                                                       [P, 2, AKV, HD]), ALU.mult)
                ins.then_inc(k_normed.sem, 1)
                dve.wait_ge(gate_e.sem, gate_e.at(lay, 1))
                link(dve.tensor_scalar(gates[:, :, :], gates[:, :, :], 1.0, None, ALU.add))
                link(dve.reciprocal(gates[:, :, :], gates[:, :, :]))
                g0 = gates[:, 0, 0:3 * AH:3]
                link(dve.tensor_scalar(g0, g0, const("row_ok"), None, ALU.mult))

                full("hid")
                link(dve.tensor_copy(st[0:HD, 2:4], bank("hid")[0:HD, 30:95:64]))
                for s in range(2):
                    ins = dve.tensor_scalar(hid_b[:, s, :], bank("hid")[0:HD, 64 * s:64 * s + 30], st[0:HD, 2 + s:3 + s],
                                            None, ALU.add)
                    if s == 0:
                        link(ins)
                ins.then_inc(hid_pre.sem, 1)
                dve.wait_ge(hid_exp.sem, hid_exp.at(lay, 1))
                ins = dve.tensor_scalar(hid_e[:, :, :], hid_e[:, :, :], 1.0, None, ALU.add)
                release(ins, "hid")
                dve.wait_ge(*is_evacuated(lay, "hid"))
                link(dve.reciprocal(hid_e[:, :, :], hid_e[:, :, :]))
                link(dve.tensor_tensor(hid_k, hid_b[:, 0, :], hid_e[:, 0, :], ALU.mult))
                vv = [v[:, 1, :].rearrange("p (h n) -> p h n", h=AKV).unsqueeze(2).broadcast_to([HD, AKV, AG, NCMP])
                      for v in (hid_b, hid_e)]
                dve.tensor_tensor(hid_v.rearrange("p (h g n) -> p h g n", h=AKV, g=AG), vv[0], vv[1], ALU.mult)\
                    .then_inc(hid_ready.sem, 1)
                full("qT2")
                release(dve.tensor_scalar(qT[:, 4:6, :], bank("qT2")[0:HD, :].rearrange("p (k n) -> p k n", k=2),
                                          gqs[:, :], None, ALU.mult), "qT2")
                full("kT1")
                release(dve.tensor_scalar(kT[:, 1, :, :], bank("kT1")[0:HD, :].rearrange("p (k n) -> p k n", k=2),
                                          gk[:, :], None, ALU.mult), "kT1")
                full("F23")
                release(dve.tensor_copy(conv_in[:, 2:4, 3:], bank("F23").rearrange("p (k n) -> p k n", k=2)), "F23")
                full("comp")
                link(dve.tensor_copy(ck, bank("comp")[0:30, 0:HD]))
                vsrc = bank("comp")[0:90, HD:2 * HD].unsqueeze(1).broadcast_to([90, AH, HD])
                link(dve.tensor_tensor(vblk[:, :, :], vsrc, bc(const("head_block")[0:90, :], [90, AH, HD]), ALU.mult))
                link(dve.tensor_tensor(sq[0:30, 0:HD], ck, ck, ALU.mult))
                ss = st[0:30, 4:5]
                ins = dve.tensor_reduce(ss, sq[0:30, 0:HD], AX.X, ALU.add)
                release(ins, "comp")
                dve.wait_ge(*is_evacuated(lay, "comp"))
                dve.sem_inc(head_sums["cmp_k"].sem, 1)
                dve.wait_ge(head_roots["cmp_k"].sem, head_roots["cmp_k"].at(lay, 1))
                dve.tensor_scalar(ck, ck, ss, None, ALU.mult).then_inc(ck_ready.sem, 1)
                dve.sem_inc(vblk_ready.sem, 1)
                cl = clog[:, :, :, :].rearrange("p c h n -> p (c h) n")
                csum3 = st[:, 144:156].rearrange("p (c h) -> p c h", c=CH)
                den = st[:, 84:92]
                hb = hB.rearrange("p c (h d) -> p (c h) d", h=BH)

                dve.wait_ge(bias_dma, 32)
                def between(s, at):
                    if (s, at) == (0, 0):
                        full("kcT")
                        release(dve.tensor_scalar(kcT, bank("kcT")[0:HD, 0:30], gk[:, :], None, ALU.mult), "kcT")
                    if (s, at) == (0, 2):
                        full("clog")
                        for c in range(CH):
                            a = P * (1 - c) + CMP_L - 1
                            link(dve.tensor_tensor(clog[:, c], bank("clog")[:, c * 90:(c + 1) * 90].rearrange("p (h n) -> p h n", h=AH),
                                                   bias_t[:, :, a:a + CMP_S * (NCMP - 1) + 1:CMP_S], ALU.add))
                        cmx = st[:, 48:60]
                        ins = dve.tensor_reduce(cmx, cl, AX.X, ALU.max)
                        release(ins, "clog")
                        dve.wait_ge(*is_evacuated(lay, "clog"))
                        dve.tensor_tensor(cl, cl, bc(cmx, [P, 2 * AH, NCMP]), ALU.subtract).then_inc(clog_pre.sem, 1)
                    if (s, at) == (1, 1):
                        dve.wait_ge(clog_exp.sem, clog_exp.at(lay, 1))
                        csum = st[:, 144:156]
                        link(dve.tensor_reduce(csum, cl, AX.X, ALU.add))
                        link(dve.reciprocal(csum, csum))
                        link(dve.tensor_tensor(csum3, csum3, gates[:, :, 0:3 * AH:3], ALU.mult))
                    if (s, at) == (1, 2):
                        dve.wait_ge(conv_exp.sem, conv_exp.at(lay, 2))
                        dve.tensor_tensor(qk[:, :, :], qk[:, :, :], ebuf, ALU.mult).then_inc(qk_ready.sem, 1)
                    if s == 2 and at < 2:
                        full(f"cO{at}")
                        link(dve.tensor_tensor(y[:, at, 0:AW].rearrange("p (h d) -> p h d", h=AH),
                                               bank(f"cO{at}")[:, 0:AW].rearrange("p (h d) -> p h d", h=AH),
                                               bc(csum3[:, at, :], [P, AH, HD]), ALU.mult))
                        dve.sem_inc(evacuated[7].sem, 1)
                    if (s, at) == (2, 2):
                        weigh_scores(0)
                    if s == 3:
                        weigh_scores(1 + at)
                    if s == 4 and at < 2:
                        full(f"num{at}")
                        release(dve.tensor_copy(nd[:, BH * at:BH * at + BH, :],
                                                bank(f"num{at}")[:, 0:BH * (HD + 1)]
                                                .rearrange("p (h d) -> p h d", h=BH)), f"num{at}")
                    if (s, at) == (4, 2):
                        dve.wait_ge(*is_evacuated(lay, "num1"))
                        dve.wait_ge(em_ready.sem, em_ready.at(lay, 1))
                        link(dve.scalar_tensor_tensor(den, nd[:, :, HD], -1.0, nd[:, :, HD], ALU.mult, ALU.max))
                        link(dve.tensor_tensor(den, den, st[:, 32:40], ALU.max))
                        link(dve.reciprocal(den, den))
                        link(dve.tensor_tensor(hb, nd[:, :, 0:HD], bc(den, [P, 2 * BH, HD]), ALU.mult))
                        sqb = nd[:, :, 0:HD]
                        link(dve.tensor_tensor(sqb, hb, hb, ALU.mult))
                        link(dve.tensor_reduce(den, sqb, AX.X, ALU.add))
                        dve.sem_inc(head_sums["mlstm"].sem, 1)
                    if (s, at) == (6, 2):
                        dve.wait_ge(eo_ready.sem, eo_ready.at(lay, 1))
                        dve.wait_ge(head_roots["mlstm"].sem, head_roots["mlstm"].at(lay, 1))
                        link(dve.tensor_tensor(hb, hb, bc(den, [P, 2 * BH, HD]), ALU.mult))
                        link(dve.tensor_tensor(y[:, :, AW:AW + BW], hB, eo[:, :, :], ALU.mult))
                    if (s, at) == (7, 2):
                        dve.sem_inc(y_all.sem, 1)
                    if (s, at) == (9, 2):
                        scale_y(0)
                    if (s, at) in ((5, 2), (6, 0)):
                        for i in ([0], [1, 2])[s - 5]:
                            full(f"mk{i}")
                            release(dve.tensor_scalar(mkT[:, 2 * i:2 * i + 2, :],
                                                      bank(f"mk{i}")[0:QK, :].rearrange("p (k n) -> p k n", k=2),
                                                      g_mk[:, :], None, ALU.mult), f"mk{i}")

                def scale_y(i):
                    dve.wait_ge(sumsy.sem, sumsy.at(lay, i + 1))
                    v = y[:, :, i * (AW + BW):i * (AW + BW) + AW]
                    dve.tensor_tensor(v, v, bc(st[:, 40 + 2 * i:42 + 2 * i], [P, CH, AW]), ALU.mult)\
                        .then_inc(y_scaled.sem, 1)

                def weigh_scores(i):
                    j, odd = i // 2, i % 2
                    nn = SEQ - j * P
                    full(f"SS{i}")
                    dve.wait_ge(e_exp.sem, e_exp.at(lay, 4 + 4 * j))
                    ev = (E1, E2)[j][:, odd:BH:2, :]
                    release(dve.scalar_tensor_tensor(ev, bank(f"SS{i}")[:, 0:2 * nn].rearrange("p (k n) -> p k n", k=2),
                                                     HD ** -0.5, ev, ALU.mult, ALU.mult), f"SS{i}")
                    dve.wait_ge(*is_evacuated(lay, f"SS{i}"))
                    dve.sem_inc(g_ready.sem, 1)

                def scores(g):
                    full(f"LA{g}")
                    full(f"LB{g}")
                    if g >= 2:
                        dve.wait_ge(*is_filled(lay, f"PB{g - 2}"))
                    settle(dve)
                    for i in range(4):
                        c, k = i // 2, i % 2
                        hh = 2 * (g % 3) + k
                        nn = (c + 1) * P
                        a = k * P if c == 0 else 256 + k * SEQ
                        b0 = P if c == 0 else 0
                        bias = bias_t[:, hh, b0:SEQ] if g < 6 else const("causal")[:, b0:SEQ]
                        ins = dve.tensor_tensor_reduce(LP[g % 2][:, a:a + nn],
                                                       bank(f"LA{g}" if c == 0 else f"LB{g}")[:, k * nn:(k + 1) * nn], bias,
                                                       1.0, LOWEST, ALU.add, ALU.max,
                                                       st[:, 160 + 4 * (g % 2) + i:161 + 4 * (g % 2) + i])
                        if i == 1:
                            release(ins, f"LA{g}")
                        if i == 3:
                            release(ins, f"LB{g}")
                    dve.wait_ge(*is_evacuated(lay, f"LA{g}"))
                    dve.wait_ge(*is_evacuated(lay, f"LB{g}"))
                    v = st[:, 160 + 4 * (g % 2):164 + 4 * (g % 2)]
                    dve.tensor_scalar(v, v, -1.0, None, ALU.mult).then_inc(p_pre.sem, 1)

                def weighted(g):
                    kind, pair = g // 3, g % 3
                    s = st[:, 176 + 4 * g:180 + 4 * g]
                    link(dve.reciprocal(s, s))
                    s3 = s.rearrange("p (c k) -> p c k", c=CH)
                    if kind < 2:
                        gg = gates[:, :, 6 * pair + kind + 1:6 * pair + 6:3]
                        link(dve.tensor_tensor(s3, s3, gg, ALU.mult))
                    full(f"O{g}")
                    src = bank(f"O{g}")[:, 0:4 * HD].rearrange("p (c k d) -> p c k d", c=CH, k=2)
                    a = (AW + BW if kind == 2 else 0) + pair * 2 * HD
                    dst = y[:, :, a:a + 2 * HD].rearrange("p c (k d) -> p c k d", k=2)
                    sb3 = bc(s3, [P, CH, 2, HD])
                    if kind == 2:
                        release(dve.tensor_tensor(dst, src, sb3, ALU.mult), f"O{g}")
                    else:
                        tmp = sq[:, 1536 - 4 * HD:1536].rearrange("p (c k d) -> p c k d", c=CH, k=2)
                        ins = dve.tensor_tensor(tmp, src, sb3, ALU.mult)
                        release(ins, f"O{g}")
                        dve.wait_ge(*is_evacuated(lay, f"O{g}"))
                        link(dve.tensor_tensor(dst, dst, tmp, ALU.add))

                for s in range(N_GROUPS_ATT + 2):
                    if s == 6:
                        between(s, 0)
                    if s < N_GROUPS_ATT:
                        scores(s)
                    if s < 6:
                        between(s, 0)
                    if 1 <= s <= N_GROUPS_ATT:
                        full(f"PB{s - 1}")
                        release(dve.tensor_copy(PT[(s - 1) % 2][:, 4:6, :],
                                                bank(f"PB{s - 1}")[:, 0:256].rearrange("p (i n) -> p i n", i=2)), f"PB{s - 1}")
                    between(s, 1)
                    if s >= 2:
                        dve.wait_ge(p_exp.sem, p_exp.at(lay, s - 1))
                        weighted(s - 2)
                    between(s, 2)
                dve.wait_ge(*is_evacuated(lay, f"O{N_GROUPS_ATT - 1}"))
                dve.sem_inc(y_all.sem, 1)
                scale_y(1)
                for i in (2, 3):
                    full(f"yT{i}")
                    for k in range(2):
                        ins = dve.tensor_scalar(xT[:, 2 * i + k, :], bank(f"yT{i}")[:, k * SEQ:(k + 1) * SEQ],
                                                gy[:, 2 * i + k:2 * i + k + 1], None, ALU.mult)
                    release(ins, f"yT{i}")
                for c in range(CH):
                    for half in range(2):
                        use = f"wo{c}{half}"
                        full(use)
                        v = x[:, c, half * 512:(half + 1) * 512]
                        release(dve.tensor_tensor(v, v, bank(use), ALU.add), use)
                    dve.wait_ge(*is_evacuated(lay, f"wo{c}0"))
                    dve.wait_ge(*is_evacuated(lay, f"wo{c}1"))
                    dve.sem_inc(x_mid.sem, 1)

                normalise_tokens(sums2)
                dve.wait_ge(moe_params, (lay + 1) * (16 * n_moe_dmas))
                for i in (2, 3):
                    full(f"nT{i}")
                    for k in range(2):
                        ins = dve.tensor_scalar(xT[:, 2 * i + k, :], bank(f"nT{i}")[:, k * SEQ:(k + 1) * SEQ],
                                                g2[:, 2 * i + k:2 * i + k + 1], None, ALU.mult)
                    release(ins, f"nT{i}")
                link(dve.memset(pg, LOWEST))
                full("rout")
                ins = dve.tensor_tensor(rl, bank("rout")[:, 0:2 * (NG + NE)].rearrange("p (c n) -> p c n", c=CH),
                                        b_rout[:, :].unsqueeze(1).broadcast_to([P, CH, NG + NE]), ALU.add)
                release(ins, "rout")
                dve.wait_ge(*is_evacuated(lay, "rout"))
                link(dve.tensor_copy(pg[:, :, 0:NG], rl[:, :, 0:NG]))
                for c in range(CH):
                    ins = dve.max(m8[:, c, :], pg[:, c, :])
                link(ins)
                for c in range(CH):
                    ins = dve.max_index(i8g[:, c, :], m8[:, c, :], pg[:, c, :])
                link(ins)
                v = pg[:, :, 0:NG]
                link(dve.tensor_tensor(v, v, m8[:, :, 0:1].broadcast_to([P, CH, NG]), ALU.subtract))
                dve.sem_inc(ge_pre.sem, 1)
                gi = st[:, 128:130]
                link(dve.tensor_copy(gi, i8g[:, :, 0]))
                iota = const("iota")
                ohg = oh[:, 0, :, 0:NG]
                link(dve.tensor_tensor(ohg, iota[:, 0:NG].unsqueeze(1).broadcast_to([P, CH, NG]), bc(gi, [P, CH, NG]),
                                       ALU.is_equal))
                for c in range(CH):
                    ins = (dve.tensor_tensor(elp[:, c, :].rearrange("p (g j) -> p g j", g=NG),
                                           rl[:, c, NG:].rearrange("p (g j) -> p g j", g=NG),
                                           bc(ohg[:, c, :], [P, NG, EPG]), ALU.mult))
                link(ins)
                link(dve.tensor_reduce(els, elp.rearrange("p c (g j) -> p c j g", g=NG), AX.X, ALU.add))
                for c in range(CH):
                    ins = dve.max(m8e[:, c, :], els[:, c, :])
                link(ins)
                link(dve.tensor_tensor(st[:, 138:140], m8e[:, :, 1], m8e[:, :, 0], ALU.subtract))
                dve.sem_inc(e2_pre.sem, 1)
                for c in range(CH):
                    ins = dve.max_index(i8e[:, c, :], m8e[:, c, :], els[:, c, :])
                link(ins)
                eid = st[:, 130:134].rearrange("p (k c) -> p k c", k=2)
                link(dve.tensor_copy(eid, i8e[:, :, 0:2].rearrange("p c k -> p k c")))
                link(dve.scalar_tensor_tensor(eid, gi.unsqueeze(1).broadcast_to([P, 2, CH]), float(EPG), eid, ALU.mult,
                                              ALU.add))
                for k in range(2):
                    ins = dve.tensor_tensor(oh[:, k], iota[:, 0:NE].unsqueeze(1).broadcast_to([P, CH, NE]),
                                            bc(eid[:, k, :], [P, CH, NE]), ALU.is_equal)
                link(ins)
                link(dve.tensor_tensor(ind, oh[:, 0], oh[:, 1], ALU.add))
                dve.sem_inc(ind_ready.sem, 1)
                dve.wait_ge(ge_exp.sem, ge_exp.at(lay, 1))
                gs = st[:, 142:144]
                link(dve.tensor_reduce(gs, pg[:, :, 0:NG], AX.X, ALU.add))
                dve.wait_ge(e2_exp.sem, e2_exp.at(lay, 1))
                e2 = st[:, 140:142]
                w12 = st[:, 132:136].rearrange("p (c k) -> p c k", c=CH)
                tmpw = st[:, 156:158]
                link(dve.tensor_scalar(tmpw, e2, 1.0, None, ALU.add))
                link(dve.tensor_tensor(tmpw, tmpw, gs, ALU.mult))
                link(dve.reciprocal(w12[:, :, 0], tmpw))
                link(dve.tensor_tensor(w12[:, :, 1], w12[:, :, 0], e2, ALU.mult))
                full("rank")
                link(dve.tensor_copy(cnt, bank("rank")[:, 2 * NE:3 * NE]))
                link(dve.tensor_tensor_scan(offs, ones[:, 0:NE], cnt, 0.0, ALU.mult, ALU.add))
                link(dve.tensor_tensor(offs, offs, cnt, ALU.subtract))
                link(dve.tensor_copy(offs_i[0:1, :], offs[0:1, :]))
                dve.sem_inc(offs_ready.sem, 1)
                ins = dve.tensor_tensor(base, bank("rank")[:, 0:2 * NE].rearrange("p (c e) -> p c e", c=CH),
                                        offs.unsqueeze(1).broadcast_to([P, CH, NE]), ALU.add)
                release(ins, "rank")
                dve.wait_ge(*is_evacuated(lay, "rank"))
                for c in range(CH):
                    for k in range(2):
                        ins = dve.tensor_tensor_reduce(junk[:, 2 * c + k], oh[:, k, c], base[:, c], 1.0, 0.0, ALU.mult,
                                                       ALU.add, st[:, 128 + 2 * c + k:129 + 2 * c + k])
                link(ins)
                dve.sem_inc(w_ready.sem, 1)
                for c in range(CH):
                    ins = dve.tensor_scalar(tmpS[:, c], iota, st[:, 128 + 2 * c:129 + 2 * c], None, ALU.is_equal)
                link(ins)
                for c in range(CH):
                    dve.scalar_tensor_tensor(S[:, c, :], iota, st[:, 129 + 2 * c:130 + 2 * c], tmpS[:, c], ALU.is_equal,
                                             ALU.add).then_inc(S_ready.sem, 1)
                for mm in range(1, KM, 2):
                    full(f"xs{mm}")
                    release(dve.tensor_scalar(xs[:, mm, 0:NSLOT], bank(f"xs{mm}"), g2[:, mm:mm + 1], None, ALU.mult),
                            f"xs{mm}")

                link(dve.tensor_scalar(jx, cnt, float(WIN), None, ALU.is_gt))
                for k in range(2, SEQ // WIN):
                    link(dve.scalar_tensor_tensor(jx, cnt, float(k * WIN), jx, ALU.is_gt, ALU.add))
                link(dve.tensor_tensor_scan(jlast, ones[:, 0:NE], jx, 1.0, ALU.mult, ALU.add))
                link(dve.tensor_tensor(jfirst, jlast, jx, ALU.subtract))
                place = bc(iota[:, 0:NJOB], [P, NJOB, NE])

                def by_expert(v):
                    return v.unsqueeze(1).broadcast_to([P, NJOB, NE])

                link(dve.tensor_tensor(jM, place, by_expert(jfirst), ALU.is_ge))
                link(dve.tensor_tensor(jt, place, by_expert(jlast), ALU.is_lt))
                link(dve.tensor_tensor(jM, jM, jt, ALU.mult))
                link(dve.tensor_tensor(jt, place, by_expert(jfirst), ALU.subtract))
                link(dve.tensor_scalar(jt, jt, 1.0, float(WIN), ALU.add, ALU.mult))
                link(dve.tensor_scalar(jx, cnt, float(WIN), None, ALU.subtract))
                link(dve.tensor_tensor(jt, jt, by_expert(jx), ALU.min))
                link(dve.tensor_tensor(jt, jt, by_expert(offs), ALU.add))
                link(dve.tensor_tensor(jt, jt, jM, ALU.mult))
                link(dve.tensor_reduce(jobs[:, 0:NJOB], jt, AX.X, ALU.add))
                link(dve.tensor_tensor(jt, jM, by_expert(iota[:, 0:NE]), ALU.mult))
                link(dve.tensor_reduce(jobs[:, NJOB:2 * NJOB], jt, AX.X, ALU.add))
                link(dve.tensor_copy(jobs[:, 0:1], offs[:, NE - 1:NE]))
                link(dve.memset(jobs[:, NJOB:NJOB + 1], float(NE - 1)))
                link(dve.tensor_copy(jobs[:, 2 * NJOB:2 * NJOB + 1], jlast[:, NE - 1:NE]))
                link(dve.tensor_copy(jobs[0:1, 2 * NJOB + 1:], jobs_before[:, :]))
                link(dve.tensor_tensor(jobs_before[:, :], jobs_before[:, :], jobs[0:1, 2 * NJOB:2 * NJOB + 1], ALU.add))
                link(dve.tensor_copy(jobs_i[0:1, :], jobs[0:1, :]))
                dve.sem_inc(jobs_made.sem, 1)

                def gate_times_up(u):
                    return dve.tensor_tensor(h, sg, PS[:, u % 3, P:2 * P], ALU.mult)

                def store(o, u):
                    return dve.tensor_copy(ysT[:, :, bass.ds(o, WIN)],
                                           PS[:, 4 + u % 3, :].rearrange("p (m n) -> p m n", m=KM))

                def gated(e, u):
                    dve.wait_ge(sg_ready.sem, sg_ready.at(lay, e + 1))
                    gate_times_up(u).then_inc(h_ready.sem, 1)

                def stored(e, u):
                    o = dve.value_load(offs_i[0:1, bass.ds(e, 1)], min_val=0, max_val=NSLOT)
                    dve.wait_ge(y_full.sem, y_full.at(lay, e + 1))
                    dve.wait_ge(y_stored.sem, y_stored.at(lay, e))
                    store(o, u).then_inc(y_stored.sem, 1)

                dve.wait_ge(xs_pad.sem, xs_pad.at(lay, 1))
                gated(0, 0)
                with dve.Fori(0, NEX // 3) as it:
                    for u in range(3):
                        gated(it * 3 + (1 + u), 1 + u)
                        stored(it * 3 + u, u)
                stored(NEX - 1, NEX - 1)
                full("cw1")
                release(dve.tensor_copy(cwT[:, 2:4, :], bank("cw1").rearrange("p (k n) -> p k n", k=2)), "cw1")
                dve.wait_ge(y_stored.sem, y_stored.at(lay, NEX))
                settle(dve)
                n_jobs, before = job_counts(dve)
                with dve.Fori(0, n_jobs) as it:
                    g = before + it
                    o = job_entry(dve, 0, it, NSLOT)
                    wait_job(dve, "sg_ready", g + 1)
                    gate_times_up(JOB).then_inc(job["h_ready"].sem, 1)
                    wait_job(dve, "y_full", g + 1)
                    wait_job(dve, "y_stored", g)
                    store(o, JOB).then_inc(job["y_stored"].sem, 1)

                for i in range(1, 8, 2):
                    full(f"ys{i}")
                    release(dve.tensor_copy(ys[:, i // 2, 512:1024], bank(f"ys{i}")), f"ys{i}")
                for c in range(CH):
                    for half in range(2):
                        use = f"fo{c}{half}"
                        full(use)
                        v = x[:, c, half * 512:(half + 1) * 512]
                        release(dve.tensor_tensor(v, v, bank(use), ALU.add), use)
                    dve.wait_ge(*is_evacuated(lay, f"fo{c}0"))
                    dve.wait_ge(*is_evacuated(lay, f"fo{c}1"))
                    dve.sem_inc(x_new.sem, 1)


_INS = ['x', 'positions', 'rel_bias', 'norm1_g', 'w_in', 'nsa_cmp_pe', 'nsa_cmp_w1', 'nsa_cmp_w2', 'nsa_q_norm',
        'nsa_k_norm', 'nsa_out_norm', 'mlstm_conv', 'mlstm_i_bias', 'mlstm_f_bias', 'mlstm_out_norm', 'mla_q_a_norm',
        'mla_w_uq', 'mla_kv_a_norm', 'mla_w_ukv', 'mla_qk_norm', 'mla_out_norm', 'w_out', 'norm2_g', 'moe_w_group',
        'moe_b_group', 'moe_w_expert', 'moe_b_expert', 'moe_w_gate', 'moe_w_up', 'moe_w_down']


def shape_constants():
    import numpy as np
    f = np.float32
    p = np.arange(P)[:, None]
    u = np.arange(SEQ)[None, :]
    tab = {
        "ident": np.eye(P, dtype=f),
        "before": (p < np.arange(P)[None, :]).astype(f),
        "causal": np.where(P + p - u < 0, f(NEG), f(0)),
        "after": np.where(u < p, f(NEG), f(0)),
        "iota": np.broadcast_to(np.arange(NSLOT, dtype=f), (P, NSLOT)),
        "inv_freq": np.broadcast_to(f(1.0) / (f(10000.0) ** (np.arange(16, dtype=f) * f(2.0) / f(ROPE))), (P, 16)),
        "row_ok": (p >= CMP_L - 1).astype(f),
        "head_block": (p // NCMP == np.arange(AH)[None, :]).astype(f),
    }
    c128 = np.ascontiguousarray(np.concatenate([tab[n] for n, _ in C128], axis=1).astype(f))
    dist = 255 - np.arange(512)
    nn = np.maximum(dist, 0)
    large = 16 + (np.log(np.maximum(nn, 1).astype(f) / f(16)) / f(np.log(8.0)) * f(16)).astype(np.int32)
    bucket = np.where(nn < 16, nn, np.minimum(large, 31))
    c33 = np.zeros((33, 512), f)
    c33[bucket, np.arange(512)] = 1.0
    c33[:32, dist < 0] = 0.0
    c33[32, dist < 0] = NEG
    c4 = np.kron(np.eye(4, dtype=f), np.ones((1, P), f))
    return {"c128": c128, "c33": c33, "c4": c4}


def kernel(**inputs):
    import numpy as _np
    import concourse.bacc as _bacc
    from concourse import mybir as _mybir
    from concourse.bass_utils import run_bass_kernel_spmd as _run

    nc = _bacc.Bacc("TRN2", target_bir_lowering=False, num_devices=1)
    arrays, aps = {}, {}
    given = {n: _np.ascontiguousarray(inputs[n]) for n in _INS}
    given.update(shape_constants())
    for name, a in given.items():
        arrays[f"in_{name}"] = a
        aps[name] = nc.dram_tensor(f"in_{name}", a.shape, _mybir.dt.from_np(a.dtype), kind="ExternalInput").ap()
    out = nc.dram_tensor("out_0", (1, SEQ, D), F32, kind="ExternalOutput").ap()
    trunk(nc, aps, out)
    r = _run(nc, [arrays], core_ids=[0])
    return r.results[0]["out_0"]
```
